# Optimizing a Trainium2 kernel written in Bass

```python
import math
import jax, jax.numpy as jnp
from jax import lax
import numpy as np

D_MODEL = 2048
BATCH = 1
SEQ = 128
DEPTH = 2
DEC_BATCH = 1
DEC_SEQ = 128
PAST_LEN = 128

GRID_W = 64
HEAD_DIM = 64
BLK = 128
A_HEADS = 8
A_KV_HEADS = 2
A_GROUP = A_HEADS // A_KV_HEADS
WIN = 128
DIFF_HEADS = 4
DIFF_V_DIM = 2 * HEAD_DIM
NA_HEADS = 8
NA_ROWS = 8
NA_COLS = 16
F_GROUPS = 4
F_GROUP_W = 128
N_BRANCH = 4
BR_W = A_HEADS * HEAD_DIM
IN_W = A_HEADS * HEAD_DIM + 2 * A_KV_HEADS * HEAD_DIM + 2 * DIFF_HEADS * 2 * HEAD_DIM + DIFF_HEADS * DIFF_V_DIM + 3 * NA_HEADS * HEAD_DIM + F_GROUPS * F_GROUP_W
N_GROUPS = 4
EXP_PER_GROUP = 4
N_EXPERTS = N_GROUPS * EXP_PER_GROUP
TOP_K = 2
D_EXPERT = 256
ROPE_BASE = 10000.0
EPS = 1e-6
NEG = -1e30

kernel_name = 'hybrid_diffusion_prefix_trunk_step'

F32 = jnp.float32

def rmsnorm(x, g):
    xf = x.astype(F32)
    y = xf * lax.rsqrt(jnp.mean(xf * xf, -1, keepdims=True) + EPS)
    return (y * g.astype(F32)).astype(x.dtype)

def modulation(cond, w_mod, b_mod):
    m = jax.nn.silu(cond) @ w_mod + b_mod
    return jnp.split(m[:, None, :], 6, axis=-1)

def project_in(h, w_in):
    b, L = h.shape[:2]
    sizes = (A_HEADS * HEAD_DIM, A_KV_HEADS * HEAD_DIM, A_KV_HEADS * HEAD_DIM,
             DIFF_HEADS * 2 * HEAD_DIM, DIFF_HEADS * 2 * HEAD_DIM, DIFF_HEADS * DIFF_V_DIM,
             NA_HEADS * HEAD_DIM, NA_HEADS * HEAD_DIM, NA_HEADS * HEAD_DIM, F_GROUPS * F_GROUP_W)
    splits = np.cumsum(sizes)[:-1].tolist()
    a_q, a_k, a_v, b_q, b_k, b_v, c_q, c_k, c_v, f = jnp.split(h @ w_in, splits, axis=-1)
    return (a_q.reshape(b, L, A_KV_HEADS, A_GROUP, HEAD_DIM),
            a_k.reshape(b, L, A_KV_HEADS, HEAD_DIM), a_v.reshape(b, L, A_KV_HEADS, HEAD_DIM),
            b_q.reshape(b, L, DIFF_HEADS, 2, HEAD_DIM), b_k.reshape(b, L, DIFF_HEADS, 2, HEAD_DIM),
            b_v.reshape(b, L, DIFF_HEADS, DIFF_V_DIM),
            c_q.reshape(b, L, NA_HEADS, HEAD_DIM), c_k.reshape(b, L, NA_HEADS, HEAD_DIM),
            c_v.reshape(b, L, NA_HEADS, HEAD_DIM), f.reshape(b, L, F_GROUPS, F_GROUP_W))

def rope_2d_tables(L):
    nf = HEAD_DIM // 4
    t = jnp.arange(L)
    inv = ROPE_BASE ** (-jnp.arange(nf, dtype=F32) / nf)
    pos = jnp.stack([t // GRID_W, t % GRID_W], -1).astype(F32)
    ang = pos[:, :, None] * inv
    return jnp.cos(ang), jnp.sin(ang)

def rope_2d(x, cos, sin):
    shp = x.shape
    nf = HEAD_DIM // 4
    xr = x.reshape(*shp[:-1], 2, 2, nf)
    ex = (1,) * (len(shp) - 3)
    c = cos.reshape(1, shp[1], *ex, 2, nf).astype(x.dtype)
    s = sin.reshape(1, shp[1], *ex, 2, nf).astype(x.dtype)
    x1 = xr[..., 0, :]
    x2 = xr[..., 1, :]
    return jnp.stack([x1 * c - x2 * s, x2 * c + x1 * s], axis=-2).reshape(shp)

def map_blocks(fn, q, blk):
    b, L = q.shape[:2]
    nb = L // blk
    qb = jnp.moveaxis(q.reshape(b, nb, blk, *q.shape[2:]), 1, 0)
    out = lax.map(lambda a: fn(a[0], a[1]), (qb, jnp.arange(nb)))
    return jnp.moveaxis(out, 0, 1).reshape(b, L, *out.shape[3:])

def sink_softmax(s, sink):
    sk = jnp.broadcast_to(sink.astype(F32).reshape(1, A_KV_HEADS, A_GROUP, 1, 1), s.shape[:-1] + (1,))
    return jax.nn.softmax(jnp.concatenate([s, sk], -1), -1)[..., :-1]

def sink_gqa_context(q, k, v, sink):
    scale = HEAD_DIM ** -0.5

    def blk(qb, i):
        s = jnp.einsum('bqkgd,bskd->bkgqs', qb, k, preferred_element_type=F32) * scale
        p = sink_softmax(s, sink).astype(v.dtype)
        return jnp.einsum('bkgqs,bskd->bqkgd', p, v)

    return map_blocks(blk, q, BLK)

def sink_gqa_latent(q, k, v, kc, vc, sink):
    b, L = k.shape[:2]
    lc = kc.shape[1]
    scale = HEAD_DIM ** -0.5
    pad = ((0, 0), (WIN, WIN), (0, 0), (0, 0))
    kp = jnp.pad(k, pad)
    vp = jnp.pad(v, pad)
    band = BLK + 2 * WIN
    qi = jnp.arange(BLK)[:, None]
    kj = jnp.arange(band)[None, :]

    def blk(qb, i):
        start = i * BLK
        kb = lax.dynamic_slice_in_dim(kp, start, band, axis=1)
        vb = lax.dynamic_slice_in_dim(vp, start, band, axis=1)
        qpos = start + qi
        kpos = start - WIN + kj
        valid = (kpos >= 0) & (kpos < L) & (jnp.abs(qpos - kpos) <= WIN)
        s_c = jnp.einsum('bqkgd,bskd->bkgqs', qb, kc, preferred_element_type=F32) * scale
        s_l = jnp.einsum('bqkgd,bskd->bkgqs', qb, kb, preferred_element_type=F32) * scale
        s_l = jnp.where(valid, s_l, NEG)
        p = sink_softmax(jnp.concatenate([s_c, s_l], -1), sink).astype(v.dtype)
        return (jnp.einsum('bkgqs,bskd->bqkgd', p[..., :lc], vc)
                + jnp.einsum('bkgqs,bskd->bqkgd', p[..., lc:], vb))

    return map_blocks(blk, q, BLK)

def diff_lambda_full(lam, lam_init):
    lam = lam.astype(F32)
    return jnp.exp(jnp.sum(lam[0] * lam[1])) - jnp.exp(jnp.sum(lam[2] * lam[3])) + lam_init

def diff_attention(q, k, v, lam_full):
    scale = HEAD_DIM ** -0.5

    def blk(qb, i):
        s = jnp.einsum('bqhmd,bshmd->bhmqs', qb, k, preferred_element_type=F32) * scale
        p = jax.nn.softmax(s, -1)
        w = (p[:, :, 0] - lam_full * p[:, :, 1]).astype(v.dtype)
        return jnp.einsum('bhqs,bshe->bqhe', w, v)

    return map_blocks(blk, q, BLK)

def dense_attention(q, k, v):
    scale = HEAD_DIM ** -0.5

    def blk(qb, i):
        s = jnp.einsum('bqhd,bshd->bhqs', qb, k, preferred_element_type=F32) * scale
        p = jax.nn.softmax(s, -1).astype(v.dtype)
        return jnp.einsum('bhqs,bshd->bqhd', p, v)

    return map_blocks(blk, q, BLK)

def na_latent(q, k, v, kc, vc, rpb):
    b, L = q.shape[:2]
    rows = L // GRID_W
    wr = min(NA_ROWS, rows)
    lc = kc.shape[1]
    scale = HEAD_DIM ** -0.5
    kg = k.reshape(b, rows, GRID_W, NA_HEADS, HEAD_DIM)
    vg = v.reshape(b, rows, GRID_W, NA_HEADS, HEAD_DIM)
    qcol = jnp.arange(GRID_W)
    cs = jnp.clip(qcol - NA_COLS // 2, 0, GRID_W - NA_COLS)
    kcol = jnp.arange(GRID_W)
    col_ok = (kcol[None, :] >= cs[:, None]) & (kcol[None, :] < cs[:, None] + NA_COLS)
    mask = jnp.broadcast_to(col_ok[:, None, :], (GRID_W, wr, GRID_W)).reshape(GRID_W, wr * GRID_W)
    dc = jnp.clip(kcol[None, :] - qcol[:, None] + NA_COLS - 1, 0, 2 * NA_COLS - 2)

    def blk(qb, r):
        rs = jnp.clip(r - wr // 2, 0, rows - wr)
        kb = lax.dynamic_slice_in_dim(kg, rs, wr, axis=1).reshape(b, wr * GRID_W, NA_HEADS, HEAD_DIM)
        vb = lax.dynamic_slice_in_dim(vg, rs, wr, axis=1).reshape(b, wr * GRID_W, NA_HEADS, HEAD_DIM)
        dr = rs - r + jnp.arange(wr) + NA_ROWS - 1
        bias = rpb[:, dr[None, :, None], dc[:, None, :]].reshape(NA_HEADS, GRID_W, wr * GRID_W)
        s_c = jnp.einsum('bqhd,bshd->bhqs', qb, kc, preferred_element_type=F32) * scale
        s_l = jnp.einsum('bqhd,bshd->bhqs', qb, kb, preferred_element_type=F32) * scale + bias.astype(F32)
        s_l = jnp.where(mask, s_l, NEG)
        p = jax.nn.softmax(jnp.concatenate([s_c, s_l], -1), -1).astype(v.dtype)
        return (jnp.einsum('bhqs,bshd->bqhd', p[..., :lc], vc)
                + jnp.einsum('bhqs,bshd->bqhd', p[..., lc:], vb))

    return map_blocks(blk, q, GRID_W)

def fourier_mix(f):
    y = jnp.fft.fft2(f.astype(F32), axes=(1, 3), norm='ortho')
    return jnp.real(y).astype(f.dtype)

def merge_branches(h, outs, w_branch, w_gate, b_gate, w_out):
    b, L = h.shape[:2]
    br = jnp.stack([o.reshape(b, L, BR_W) for o in outs], axis=2)
    proj = jnp.einsum('blnc,ncd->blnd', br, w_branch)
    gate = jax.nn.sigmoid(h @ w_gate + b_gate).reshape(b, L, N_BRANCH, D_MODEL)
    return jnp.einsum('blnd,blnd->bld', gate, proj) @ w_out

def hier_moe(h, w_rg, b_rg, w_re, b_re, w_eg, w_eu, w_ed):
    shp = h.shape
    t = h.reshape(-1, D_MODEL)
    tf = t.astype(F32)
    pg = jax.nn.softmax(tf @ w_rg.astype(F32) + b_rg.astype(F32), -1)
    pg_top, g_idx = lax.top_k(pg, 1)
    le = (tf @ w_re.astype(F32) + b_re.astype(F32)).reshape(-1, N_GROUPS, EXP_PER_GROUP)
    le_sel = jnp.einsum('tg,tge->te', jax.nn.one_hot(g_idx[:, 0], N_GROUPS, dtype=F32), le)
    pe_top, e_idx = lax.top_k(jax.nn.softmax(le_sel, -1), TOP_K)
    w = pe_top / jnp.sum(pe_top, -1, keepdims=True) * pg_top
    eid = g_idx * EXP_PER_GROUP + e_idx
    combine = jnp.einsum('tk,tke->te', w, jax.nn.one_hot(eid, N_EXPERTS, dtype=F32))
    hid = jax.nn.silu(jnp.einsum('td,edf->tef', t, w_eg)) * jnp.einsum('td,edf->tef', t, w_eu)
    out = jnp.einsum('tef,efd->td', hid * combine[:, :, None].astype(hid.dtype), w_ed)
    return out.reshape(shp)

def layer(x, cond, lp, lam_init, cache, rope):
    sh1, sc1, g1, sh2, sc2, g2 = modulation(cond, lp['w_mod'], lp['b_mod'])
    h = rmsnorm(x, lp['norm1_g']) * (1 + sc1) + sh1
    a_q, a_k, a_v, b_q, b_k, b_v, c_q, c_k, c_v, f = project_in(h, lp['w_in'])
    lam_full = diff_lambda_full(lp['diff_lambda'], lam_init)
    if cache is None:
        o_a = sink_gqa_context(a_q, a_k, a_v, lp['sink'])
        o_b = diff_attention(b_q, b_k, b_v, lam_full)
        o_c = dense_attention(c_q, c_k, c_v)
        ctx = (a_k, a_v, b_k, b_v, c_k, c_v)
    else:
        cos, sin = rope
        ak_c, av_c, bk_c, bv_c, ck_c, cv_c = cache
        o_a = sink_gqa_latent(rope_2d(a_q, cos, sin), rope_2d(a_k, cos, sin), a_v, ak_c, av_c, lp['sink'])
        k_all = jnp.concatenate([bk_c, rope_2d(b_k, cos, sin)], axis=1)
        v_all = jnp.concatenate([bv_c, b_v], axis=1)
        o_b = diff_attention(rope_2d(b_q, cos, sin), k_all, v_all, lam_full)
        o_c = na_latent(c_q, c_k, c_v, ck_c, cv_c, lp['na_rpb'])
        ctx = None
    o_b = rmsnorm(o_b, lp['diff_sub_g']) * (1.0 - lam_init)
    o_f = fourier_mix(f)
    x = x + g1 * merge_branches(h, (o_a, o_b, o_c, o_f), lp['w_branch'], lp['w_gate'], lp['b_gate'], lp['w_out'])
    h2 = rmsnorm(x, lp['norm2_g']) * (1 + sc2) + sh2
    x = x + g2 * hier_moe(h2, lp['w_rg'], lp['b_rg'], lp['w_re'], lp['b_re'], lp['w_eg'], lp['w_eu'], lp['w_ed'])
    return x, ctx

def setup_inputs(seed: int = 0) -> dict:
    key = jax.random.key(seed)
    ks = iter(jax.random.split(key, 40))

    def nrm(shape, scale=1.0):
        return jax.random.normal(next(ks), shape, F32) * scale

    D = D_MODEL
    return {
        'x_prompt': nrm((BATCH, SEQ, D)),
        'x_sample': nrm((DEC_BATCH, DEC_SEQ, D)),
        'cache_attn_k': nrm((DEC_BATCH, DEPTH, PAST_LEN, A_KV_HEADS, HEAD_DIM)),
        'cache_attn_v': nrm((DEC_BATCH, DEPTH, PAST_LEN, A_KV_HEADS, HEAD_DIM)),
        'cache_diff_k': nrm((DEC_BATCH, DEPTH, PAST_LEN, DIFF_HEADS, 2, HEAD_DIM)),
        'cache_diff_v': nrm((DEC_BATCH, DEPTH, PAST_LEN, DIFF_HEADS, DIFF_V_DIM)),
        'cache_na_k': nrm((DEC_BATCH, DEPTH, PAST_LEN, NA_HEADS, HEAD_DIM)),
        'cache_na_v': nrm((DEC_BATCH, DEPTH, PAST_LEN, NA_HEADS, HEAD_DIM)),
        'c': nrm((DEC_BATCH, D)),
        'c_ctx': nrm((D,)),
        'w_mod': nrm((DEPTH, D, 6 * D), D ** -0.5),
        'b_mod': nrm((DEPTH, 6 * D), 0.01),
        'norm1_g': 1.0 + nrm((DEPTH, D), 0.05),
        'w_in': nrm((DEPTH, D, IN_W), D ** -0.5),
        'attn_sink': nrm((DEPTH, A_HEADS)),
        'diff_lambda': nrm((DEPTH, 4, HEAD_DIM), 0.1),
        'diff_sub_g': 1.0 + nrm((DEPTH, DIFF_V_DIM), 0.05),
        'na_rpb': nrm((DEPTH, NA_HEADS, 2 * NA_ROWS - 1, 2 * NA_COLS - 1), 0.1),
        'w_branch': nrm((DEPTH, N_BRANCH, BR_W, D), BR_W ** -0.5),
        'w_gate': nrm((DEPTH, D, N_BRANCH * D), D ** -0.5),
        'b_gate': nrm((DEPTH, N_BRANCH * D), 0.01),
        'w_out': nrm((DEPTH, D, D), D ** -0.5),
        'norm2_g': 1.0 + nrm((DEPTH, D), 0.05),
        'w_router_group': nrm((DEPTH, D, N_GROUPS), D ** -0.5),
        'b_router_group': nrm((DEPTH, N_GROUPS), 0.01),
        'w_router_expert': nrm((DEPTH, D, N_EXPERTS), D ** -0.5),
        'b_router_expert': nrm((DEPTH, N_EXPERTS), 0.01),
        'w_exp_gate': nrm((DEPTH, N_EXPERTS, D, D_EXPERT), D ** -0.5),
        'w_exp_up': nrm((DEPTH, N_EXPERTS, D, D_EXPERT), D ** -0.5),
        'w_exp_down': nrm((DEPTH, N_EXPERTS, D_EXPERT, D), D_EXPERT ** -0.5),
        'final_g': 1.0 + nrm((D,), 0.05),
    }

def reference(x_prompt, x_sample, cache_attn_k, cache_attn_v, cache_diff_k, cache_diff_v, cache_na_k, cache_na_v,
              c, c_ctx, w_mod, b_mod, norm1_g, w_in, attn_sink, diff_lambda, diff_sub_g, na_rpb, w_branch, w_gate,
              b_gate, w_out, norm2_g, w_router_group, b_router_group, w_router_expert, b_router_expert,
              w_exp_gate, w_exp_up, w_exp_down, final_g):
    xp = x_prompt
    xs = x_sample
    rope = rope_2d_tables(x_sample.shape[1])
    new_ak, new_av, new_bk, new_bv, new_ck, new_cv = [], [], [], [], [], []
    for l in range(DEPTH):
        lp = {'w_mod': w_mod[l], 'b_mod': b_mod[l], 'norm1_g': norm1_g[l], 'w_in': w_in[l],
              'sink': attn_sink[l], 'diff_lambda': diff_lambda[l], 'diff_sub_g': diff_sub_g[l],
              'na_rpb': na_rpb[l], 'w_branch': w_branch[l], 'w_gate': w_gate[l], 'b_gate': b_gate[l],
              'w_out': w_out[l], 'norm2_g': norm2_g[l], 'w_rg': w_router_group[l], 'b_rg': b_router_group[l],
              'w_re': w_router_expert[l], 'b_re': b_router_expert[l], 'w_eg': w_exp_gate[l],
              'w_eu': w_exp_up[l], 'w_ed': w_exp_down[l]}
        lam_init = 0.8 - 0.6 * math.exp(-0.3 * l)
        xp, ctx = layer(xp, c_ctx[None, :], lp, lam_init, None, None)
        new_ak.append(ctx[0])
        new_av.append(ctx[1])
        new_bk.append(ctx[2])
        new_bv.append(ctx[3])
        new_ck.append(ctx[4])
        new_cv.append(ctx[5])
        cache_l = (cache_attn_k[:, l], cache_attn_v[:, l], cache_diff_k[:, l], cache_diff_v[:, l],
                   cache_na_k[:, l], cache_na_v[:, l])
        xs, _ = layer(xs, c, lp, lam_init, cache_l, rope)
    y_prompt = rmsnorm(xp, final_g)
    y_sample = rmsnorm(xs, final_g)
    new_attn_k = jnp.stack(new_ak, axis=1)
    new_attn_v = jnp.stack(new_av, axis=1)
    new_diff_k = jnp.stack(new_bk, axis=1)
    new_diff_v = jnp.stack(new_bv, axis=1)
    new_na_k = jnp.stack(new_ck, axis=1)
    new_na_v = jnp.stack(new_cv, axis=1)
    return (y_prompt, y_sample, new_attn_k, new_attn_v, new_diff_k, new_diff_v, new_na_k, new_na_v)


_drawn_inputs = setup_inputs


def setup_inputs(seed=0):
    import zlib

    import numpy as np

    out = dict(_drawn_inputs(seed))
    spreads = {}
    factors = {'b_gate': 3.48,
     'b_router_group': 3.093,
     'attn_sink': 8.0,
     'na_rpb': 2.879,
     'b_router_expert': 3.01}
    for name, (base, spread) in spreads.items():
        noise = np.random.default_rng([zlib.crc32(name.encode()), seed]).standard_normal(out[name].shape)
        drawn = base * np.exp(spread * noise) if base else spread * noise
        out[name] = __import__('jax').numpy.asarray(drawn.astype(out[name].dtype))
    for name, factor in factors.items():
        out[name] = (out[name] * factor).astype(out[name].dtype)
    return out
```

```python
import math
from contextlib import ExitStack

import numpy as np

import concourse.bass as bass
from concourse import mybir

F32 = mybir.dt.float32
F32R = mybir.dt.float32r
U32 = mybir.dt.uint32
ALU = mybir.AluOpType
ACT = mybir.ActivationFunctionType
AX = mybir.AxisListType

P = 128
TILES = 2
PROMPT, SAMPLE = 0, 1
COLS = 512
KB = 4
RAW_SLOTS = 4
SPLIT_SLOTS = 2
HD = 64
EPS = 1e-6
GRID_W = 64
NA_ROWS, NA_COLS = 8, 16
PAD_W = 128


def need(engine, semaphore, count):
    if not (isinstance(count, int) and count <= 0):
        engine.wait_ge(semaphore, count)


class Cursor:

    def __init__(self):
        self.at = {}
        self.loop = None
        self.first = False

    def next(self, name):
        k = self.at.get(name, 0)
        self.at[name] = k + 1
        if self.loop is None:
            return k
        register, first, start, rates = self.loop
        return (register - first) * rates.get(name, 0) + k

    def done(self, name):
        k = self.next(name)
        self.at[name] -= 1
        return k

    def parity(self, name, slots):
        return self.at.get(name, 0) % slots

    def rounds(self, engine, count, body):
        start = dict(self.at)
        self.first = True
        body(0)
        self.first = False
        rates = {n: k - start.get(n, 0) for n, k in self.at.items()}
        start = dict(self.at)
        if count == 1:
            return
        with engine.Fori(1, count) as i:
            self.loop = (i, 1, start, rates)
            body(i)
            self.loop = None
        for n, k in start.items():
            assert self.at[n] - k == rates[n]
            self.at[n] = k + rates[n] * (count - 1)


def shape_constants():
    t = np.arange(P)
    nf = HD // 4
    inv = (np.float32(10000.0) ** (-np.arange(nf, dtype=np.float32) / np.float32(nf))).astype(np.float32)
    pos = np.stack([t // GRID_W, t % GRID_W], -1).astype(np.float32)
    ang = (pos[:, :, None] * inv).astype(np.float32)
    rope = np.concatenate([np.cos(ang).reshape(P, 2 * nf), np.sin(ang).reshape(P, 2 * nf)], 1).astype(np.float32)
    w = 2 * np.pi * ((t[:, None] * t[None, :]) % P) / P
    fourier = np.concatenate([np.cos(w), np.sin(w)], 1).astype(np.float32)
    ident = np.eye(P, dtype=np.float32)
    back = t // GRID_W * GRID_W + GRID_W - 1 - t % GRID_W
    mirror = ident[back]
    qc = t % GRID_W
    cs = np.clip(qc - NA_COLS // 2, 0, GRID_W - NA_COLS)
    ok = (qc[None, :] >= cs[:, None]) & (qc[None, :] < cs[:, None] + NA_COLS)
    mask = np.where(ok, 0.0, -1e30).astype(np.float32)[back]
    pick = np.zeros((P, 4, P), np.float32)
    for b in range(4):
        pick[b, b] = pick[32 + b, b] = 1.0
    fold = np.zeros((P, 2), np.float32)
    fold[0, 0] = fold[2, 0] = fold[1, 1] = fold[3, 1] = 1.0
    which = np.tile(np.arange(16, dtype=np.float32), (P, 1))
    group = np.tile(np.arange(16, dtype=np.float32) // 4, (P, 1))
    parts = {"ident": ident, "rope": rope, "fourier": fourier, "mirror": mirror, "mask": mask,
             "which": which, "group": group, "fold": fold}
    places, at = {}, 0
    for n, a in parts.items():
        places[n] = (at, a.shape[1])
        at += a.shape[1]
    return np.ascontiguousarray(np.concatenate(list(parts.values()), 1)), places, pick.reshape(P, 4 * P)


def trunk(nc, io, places):
    D = io["x_prompt"].shape[2]
    DEPTH = io["w_in"].shape[0]
    IN_W = io["w_in"].shape[2]
    NK = D // P
    NE = io["w_exp_gate"].shape[1]
    DE = io["w_exp_gate"].shape[3]
    NCH = D // COLS
    BR = io["w_branch"].shape[2]
    MODS = 6 * D // COLS
    UPC = NK // KB
    A_H, B_H, C_H = 8, 4, 8
    AQ, AK, AV, BQ, BK, BV, CQ, CK, CV, FF = 0, 512, 640, 768, 1280, 1792, 2304, 2816, 3328, 3840
    IN_CHUNKS = IN_W // COLS
    IN_REST = IN_W - IN_CHUNKS * COLS
    LAYER_CHUNKS = IN_CHUNKS + 1 + 2 * 4 * NCH + NCH + NE + NCH
    LAM = [0.8 - 0.6 * math.exp(-0.3 * l) for l in range(DEPTH)]

    with ExitStack() as ctx:
        spot = [(nc.sbuf_base + 31) // 32 * 32]

        def place(name, shape, dtype=F32, at=None):
            size = 4 * int(np.prod(shape[1:]))
            where = spot[0] if at is None else at
            t = nc.alloc_sbuf_tensor_at(name, shape, dtype, offset=where)
            if at is None:
                spot[0] += (size + 31) // 32 * 32
            return t

        raw_w = place("raw_w", [P, RAW_SLOTS, KB, COLS])
        high_w = place("high_w", [P, SPLIT_SLOTS, KB, COLS], F32R)
        low_w = place("low_w", [P, SPLIT_SLOTS, KB, COLS], F32R)
        x = place("x", [P, TILES, D])
        in_high = place("in_high", [P, NK, TILES, P], F32R)
        in_low = place("in_low", [P, NK, TILES, P], F32R)
        region = spot[0]
        br_high = place("br_high", [P, NK, TILES, P], F32R)
        br_low = place("br_low", [P, NK, TILES, P], F32R)
        proj = place("proj", [P, TILES, IN_W])
        mix = spot[0]
        merged = place("merged", [P, TILES, D])
        hid_high = place("hid_high", [P, NE * 2, TILES, P], F32R, at=region)
        hid_low = place("hid_low", [P, NE * 2, TILES, P], F32R, at=region + 4 * NE * 2 * TILES * P)
        gate_row = place("gate_row", [P, TILES, D], at=mix)
        normed = place("normed", [P, D], at=region + 4 * NE * 4 * TILES * P - 8192)
        router_raw = place("router_raw", [P, NK, 20], at=region + 32768)
        router_high = place("router_high", [P, NK, 20], F32R, at=region + 32768 + 80 * NK)
        router_low = place("router_low", [P, NK, 20], F32R, at=region + 32768 + 160 * NK)
        qk_t = place("qk_t", [P, 2, 12, P], at=mix)
        hankel = place("hankel", [P, C_H, P], at=mix + 8 * 12 * P)
        e_buf = place("e_buf", [P, 2, 1024])
        ones_at = spot[0] - 8192
        sig = place("sig", [P, TILES, COLS], at=spot[0] - 8192)
        prod = place("prod", [P, TILES, COLS], at=spot[0] - 4096)
        p_t = place("p_t", [P, 8, P])
        full = place("full", [P, 2, COLS], at=spot[0] - 4096)
        cache_bc = place("cache_bc", [P, 2, 512])
        bg_split = place("bg_split", [36, COLS], F32R, at=spot[0] - 4096)
        bg_raw = place("bg_raw", [36, COLS])
        lam_in = place("lam_in", [P, 4, HD], at=spot[0] - 2048)
        m4 = place("m4", [4, COLS])
        cache_a = place("cache_a", [P, 2, 128], at=spot[0] - 2048)
        const = place("const", [P, places["fold"][0] + 2])
        pick = place("pick", [36, 4, P], F32R)
        mod = place("mod", [P, 2, MODS * 4, 2])
        b_mod_t = place("b_mod_t", [P, 2, MODS * 4])
        gains = place("gains", [P, 2 * DEPTH, NK])
        scale_t = place("scale_t", [P, NK, TILES])
        cond = place("cond", [P, NK, 4], F32R)
        cond_full = place("cond_full", [P, 2 * NK], at=mix)
        sub_g = place("sub_g", [P, DEPTH])
        sinks = place("sinks", [P, DEPTH, A_H])
        small = place("small", [P, 128])
        comb = place("comb", [P, TILES, 16])
        router_b = place("router_b", [P, DEPTH, 20])
        route = place("route", [P, TILES, 96], at=region + 32768 + 240 * NK)
        ones = place("ones", [P, P], at=ones_at)
        picked = place("picked", [P, TILES, 8])
        picked_at = place("picked_at", [P, TILES, 8], U32)
        assert spot[0] <= nc.sbuf_usable_end, spot[0] - nc.sbuf_usable_end

        sum_sq, rstd = small[:, 0:2], small[:, 2:4]
        lam_sum, lam_exp, lam = small[:, 4:6], small[:, 6:8], small[:, 8:9]
        top = small[:, 16:24]
        neg_top = small[:, 24:32]
        esum = small[:, 32:40]
        rsum = small[:, 40:48]
        esink = small[:, 48:56]
        sub_sq, sub_rstd = small[:, 56:60], small[:, 60:64]

        def constant(name):
            a, n = places[name]
            return const[:, a:a + n]

        ident, mirror, mask = constant("ident"), constant("mirror"), constant("mask")
        fourier = constant("fourier")
        fold = const[:, places["fold"][0]:places["fold"][0] + 2]

        banks = [ctx.enter_context(nc.psum_tensor(f"bank{i}", [P, 512], F32)) for i in range(8)]
        mod_bank, turn_banks, small_bank = banks[4], banks[5:7], banks[7]

        def sem(name):
            return ctx.enter_context(nc.semaphore(name))

        raw_in = [sem(f"raw_in{i}") for i in range(RAW_SLOTS)]
        high_ready, low_ready, unit_used = sem("high_ready"), sem("low_ready"), sem("unit_used")
        chunk_read, gate_ready = sem("chunk_read"), sem("gate_ready")
        mod_copied, mod_turned, mod_stored = sem("mod_copied"), sem("mod_turned"), sem("mod_stored")
        hid_turned, hid_high_ready, hid_stored = sem("hid_turned"), sem("hid_high_ready"), sem("hid_stored")
        start_in, start_turned, cond_sig, cond_full_ready, cond_high, cond_ready = (
            sem("start_in"), sem("start_turned"), sem("cond_sig"), sem("cond_full_ready"), sem("cond_high"), sem("cond_ready"))
        pick_in, pick_ready, vectors_in = sem("pick_in"), sem("pick_ready"), sem("vectors_in")
        bg_in, bg_clear, bg_high, bg_ready = sem("bg_in"), sem("bg_clear"), sem("bg_high"), sem("bg_ready")
        squares, mean_ready, root_ready, normed_ready = sem("squares"), sem("mean_ready"), sem("root_ready"), sem("normed_ready")
        norm_turned, norm_full, norm_high, norm_low = sem("norm_turned"), sem("norm_full"), sem("norm_high"), sem("norm_low")
        roped = sem("roped")
        cache_a_in, cache_bc_in, hankel_in, lam_in_s, router_in = sem("cache_a_in"), sem("cache_bc_in"), sem("hankel_in"), sem("lam_in_s"), sem("router_in")
        lam_sum_ready, lam_exp_ready, lam_ready = sem("lam_sum_ready"), sem("lam_exp_ready"), sem("lam_ready")
        hankel_ready = sem("hankel_ready")
        f_first, f_copied, f_second, f_high, f_low = sem("f_first"), sem("f_copied"), sem("f_second"), sem("f_high"), sem("f_low")
        qk_turned, qk_ready = sem("qk_turned"), sem("qk_ready")
        scored, top_ready, exp_ready, weights_ready = sem("scored"), sem("top_ready"), sem("exp_ready"), sem("weights_ready")
        p_turned, p_ready, pv_done, out_high, out_low = sem("p_turned"), sem("p_ready"), sem("pv_done"), sem("out_high"), sem("out_low")
        sub_squares, sub_mean, sub_root, sub_ready, sub_turned = sem("sub_squares"), sem("sub_mean"), sem("sub_root"), sem("sub_ready"), sem("sub_turned")
        diag_ready, row_summed, row_ready = sem("diag_ready"), sem("row_summed"), sem("row_ready")
        merged_turned, merged_high, merged_low = sem("merged_turned"), sem("merged_high"), sem("merged_low")
        router_high_s, router_ready, routed, route_top, route_exp, comb_ready = (
            sem("router_high_s"), sem("router_ready"), sem("routed"), sem("route_top"), sem("route_exp"), sem("comb_ready"))
        final_in, final_scaled, out_stored, cache_stored = sem("final_in"), sem("final_scaled"), sem("out_stored"), sem("cache_stored")
        x_ready = sem("x_ready")

        def jobs():
            return [(b, t) for b in "ABC" for t in (SAMPLE, PROMPT)]

        def q_blocks(b):
            return 4

        def k_blocks(b):
            return 1 if b == "A" else 4

        def n_blocks(b, t):
            return q_blocks(b) + k_blocks(b) * (2 if t == SAMPLE else 1)

        def heads(b, g):
            if b == "A":
                return [(2 * g + r // 2, 0, r % 2, 2 * g + r // 2 + 4 * (r % 2)) for r in range(4)]
            if b == "B":
                return [(2 * g + r // 2, 2 * g + r // 2, r % 2, 2 * g + r // 2) for r in range(4)]
            return [(2 * g + r // 2, 2 * g + r // 2, r % 2, 4 * g + r) for r in range(4)]

        GROUPS = [(j, b, t, g) for j, (b, t) in enumerate(jobs()) for g in range(2)]
        NG = len(GROUPS)
        TURNS = [(n_blocks(b, t) + 3) // 4 for b, t in jobs()]

        def keys(t):
            return 2 if t == SAMPLE else 1

        def score_row(g, r, t):
            return banks[2 * (g % 2) + r % 2], r // 2 * P * keys(t)

        def value_cols(b, head):
            return (head // 4 * HD, HD) if b == "A" else ((head * P, P) if b == "B" else (head * HD, HD))

        V_AT = {"A": AV, "B": BV, "C": CV}
        BRANCH = {"A": 0, "B": 1, "C": 2, "F": 3}

        def weight_tile(w, l, col, width, block):
            return w[l, block * KB * P:(block + 1) * KB * P, col].rearrange("(k p) n -> p k n", p=P)

        block = ctx.enter_context(nc.Block())

        @block.sync
        def _(sp):
            at = Cursor()

            def load(src, width=COLS):
                slot = at.parity("unit", RAW_SLOTS)
                u = at.next("unit")
                need(sp, low_ready, u - RAW_SLOTS + 1)
                at.next(f"in{slot}")
                sp.dma_start(raw_w[:, slot, :, 0:width], src).then_inc(raw_in[slot], 16)

            def load_mod(l, c):
                for j in range(UPC):
                    load(weight_tile(io["w_mod"], l, bass.ds(c * COLS, COLS), COLS, j))

            sp.dma_start(const[:, :], io["const"]).then_inc(start_in, 16)
            sp.dma_start(normed[0:NK, 0:P], io["c_ctx"].rearrange("(k p) -> k p", p=P)).then_inc(start_in, 16)
            sp.dma_start(normed[NK:2 * NK, 0:P], io["c"].rearrange("a (k p) -> (a k) p", p=P)).then_inc(start_in, 16)
            for l in range(DEPTH):
                sp.dma_start(normed[0:MODS * 4, (1 + l) * P:(2 + l) * P],
                             io["b_mod"][l].rearrange("(k p) -> k p", p=P)).then_inc(start_in, 16)
            for l in range(DEPTH):
                for i, n in enumerate(("norm1_g", "norm2_g")):
                    r = (2 * l + i) * NK
                    sp.dma_start(normed[r:r + NK, 3 * P:4 * P],
                                 io[n][l].rearrange("(k p) -> k p", p=P)).then_inc(start_in, 16)
            sp.dma_start(x[:, PROMPT, :], io["x_prompt"][0]).then_inc(x_ready, 16)
            sp.dma_start(x[:, SAMPLE, :], io["x_sample"][0]).then_inc(x_ready, 16)

            def mod_start(c):
                load_mod(0, c)
            at.rounds(sp, 8, mod_start)
            sp.dma_start(proj[0:36, 0, 0:4 * P], io["pick"][0:36, :]).then_inc(pick_in, 16)
            for l in range(DEPTH):
                sp.dma_start(sub_g[:, l:l + 1], io["diff_sub_g"][l].rearrange("(p a) -> p a", a=1)).then_inc(vectors_in, 16)
                sp.dma_start(sinks[:, l, :], io["attn_sink"][l:l + 1, :].broadcast_to([P, A_H])).then_inc(vectors_in, 16)
                sp.dma_start(router_b[:, l, 0:4], io["b_router_group"][l:l + 1, :].broadcast_to([P, 4])).then_inc(vectors_in, 16)
                sp.dma_start(router_b[:, l, 4:20], io["b_router_expert"][l:l + 1, :].broadcast_to([P, 16])).then_inc(vectors_in, 16)

            for l in range(DEPTH):
                interleave = l == 0

                def w_in_pair(i):
                    for h in range(2):
                        for j in range(UPC):
                            load(weight_tile(io["w_in"], l, bass.ds((i * 2 + h) * COLS, COLS), COLS, j))
                at.rounds(sp, IN_CHUNKS // 2, w_in_pair)
                for j in range(UPC):
                    load(weight_tile(io["w_in"], l, slice(IN_CHUNKS * COLS, IN_W), IN_REST, j), IN_REST)
                if l:
                    sp.wait_ge(chunk_read, LAYER_CHUNKS * l)
                sp.dma_start(cache_a[:, 0, :], io["cache_attn_k"][0, l].rearrange("s h d -> s (h d)")).then_inc(cache_a_in, 16)
                sp.dma_start(cache_a[:, 1, :], io["cache_attn_v"][0, l].rearrange("s h d -> s (h d)")).then_inc(cache_a_in, 16)
                sp.dma_start(cache_bc[:, 0, :], io["cache_diff_k"][0, l].rearrange("s h m d -> s (h m d)")).then_inc(cache_bc_in, 16)
                sp.dma_start(cache_bc[:, 1, :], io["cache_diff_v"][0, l].rearrange("s h d -> s (h d)")).then_inc(cache_bc_in, 16)
                sp.dma_start(lam_in[:, :, :], io["diff_lambda"][l:l + 1].broadcast_to([P, 4, HD])).then_inc(lam_in_s, 16)
                rpb = io["na_rpb"]
                for qr in range(2):
                    for kr in range(2):
                        first = (l * C_H * (2 * NA_ROWS - 1) + NA_ROWS - 1 - qr + kr) * PAD_W
                        src = bass.AP(tensor=rpb.tensor, offset=first,
                                      ap=[[1, GRID_W], [(2 * NA_ROWS - 1) * PAD_W, C_H], [1, GRID_W]])
                        sp.dma_start(hankel[qr * GRID_W:(qr + 1) * GRID_W, :, kr * GRID_W:(kr + 1) * GRID_W],
                                     src).then_inc(hankel_in, 16)
                sp.wait_ge(chunk_read, LAYER_CHUNKS * l + IN_CHUNKS + 1)
                for name, a, n in (("new_attn_k", AK, 128), ("new_attn_v", AV, 128), ("new_diff_k", BK, 512),
                                   ("new_diff_v", BV, 512), ("new_na_k", CK, 512), ("new_na_v", CV, 512)):
                    dst = io[name][0, l]
                    dst = dst.rearrange("s h m d -> s (h m d)") if name == "new_diff_k" else dst.rearrange("s h d -> s (h d)")
                    sp.dma_start(dst, proj[:, PROMPT, a:a + n]).then_inc(cache_stored, 16)
                sp.wait_ge(pv_done, NG * l + 6)
                sp.dma_start(cache_bc[:, 0, :], io["cache_na_k"][0, l].rearrange("s h d -> s (h d)")).then_inc(cache_bc_in, 16)
                sp.dma_start(cache_bc[:, 1, :], io["cache_na_v"][0, l].rearrange("s h d -> s (h d)")).then_inc(cache_bc_in, 16)

                def gates(n):
                    for b in range(4):
                        for j in range(UPC):
                            load(weight_tile(io["w_gate"], l, bass.ds(n * COLS + b * D, COLS), COLS, j))
                        if b == 0:
                            r = at.next("bg")
                            if at.first:
                                sp.wait_ge(bg_clear, l + 1)
                            need(sp, bg_ready, r)
                            for row in (0, 32):
                                sp.dma_start(bg_raw[row:row + 4, :],
                                             io["b_gate"][l].rearrange("(b n) -> b n", b=4)[:, bass.ds(n * COLS, COLS)]
                                             ).then_inc(bg_in, 16)
                        if interleave:
                            load_mod(0, n * 4 + (b + 8))
                        load(io["w_branch"][l, b, :, bass.ds(n * COLS, COLS)].rearrange("(k p) n -> p k n", p=P))
                at.rounds(sp, NCH, gates)

                sp.wait_ge(cache_stored, 16 * 6 * (l + 1))
                sp.dma_start(router_raw[:, :, 0:4], io["w_router_group"][l].rearrange("(k p) n -> p k n", p=P)).then_inc(router_in, 16)
                sp.dma_start(router_raw[:, :, 4:20], io["w_router_expert"][l].rearrange("(k p) n -> p k n", p=P)).then_inc(router_in, 16)

                def w_out(n):
                    for j in range(UPC):
                        load(weight_tile(io["w_out"], l, bass.ds(n * COLS, COLS), COLS, j))
                at.rounds(sp, NCH, w_out)

                def experts(i):
                    for h in range(2):
                        if interleave:
                            load_mod(1, i * 2 + h)
                        for j in range(UPC):
                            slot = at.parity("unit", RAW_SLOTS)
                            u = at.next("unit")
                            need(sp, low_ready, u - RAW_SLOTS + 1)
                            for half, name in enumerate(("w_exp_gate", "w_exp_up")):
                                at.next(f"in{slot}")
                                src = io[name][l][bass.ds(i * 2 + h, 1), j * KB * P:(j + 1) * KB * P, :]
                                sp.dma_start(raw_w[:, slot, :, half * DE:(half + 1) * DE],
                                             src.rearrange("e (k p) f -> p (e k) f", p=P)).then_inc(raw_in[slot], 16)
                at.rounds(sp, NE // 2, experts)

                def down(n):
                    if interleave:
                        for m in range(2):
                            load_mod(1, n * 2 + (NE + m))
                    rows = io["w_exp_down"][l].rearrange("e (k p) n -> p (e k) n", p=P)
                    for j in range(NE * DE // P // KB):
                        load(rows[:, j * KB:(j + 1) * KB, bass.ds(n * COLS, COLS)])
                at.rounds(sp, NCH, down)

            sp.wait_ge(chunk_read, LAYER_CHUNKS * DEPTH)
            sp.dma_start(merged[:, 0, :], io["final_g"].rearrange("(a n) -> a n", a=1).broadcast_to([P, D])).then_inc(final_in, 16)
            for t, name in enumerate(("y_prompt", "y_sample")):
                sp.wait_ge(final_scaled, t + 1)
                sp.dma_start(io[name][0], x[:, t, :]).then_inc(out_stored, 16)
            sp.wait_ge(out_stored, 32)
            sp.wait_ge(cache_stored, 16 * 6 * DEPTH)

        @block.scalar
        def _(act):
            at = Cursor()

            def split_high(width=COLS, loads=1):
                slot, part = at.parity("unit", RAW_SLOTS), at.parity("unit", SPLIT_SLOTS)
                u = at.next("unit")
                for _ in range(loads):
                    k = at.next(f"in{slot}")
                act.wait_ge(raw_in[slot], k * 16 + 16)
                need(act, unit_used, u - SPLIT_SLOTS + 1)
                act.activation(high_w[:, part, :, 0:width], raw_w[:, slot, :, 0:width], ACT.Copy).then_inc(high_ready, 1)

            def norm_scale(t_ready):
                for t in range(TILES):
                    act.activation(normed[:, :], x[:, t, :], ACT.Square, accum_out=sum_sq[:, t:t + 1]).then_inc(squares, 1)
                    act.drain()
                act.wait_ge(mean_ready, at.next("norm") + 1)
                act.activation(rstd, rstd, ACT.Sqrt).then_inc(root_ready, 1)

            def norm():
                norm_scale(None)
                for i in range(2 * KB):
                    t, g = i // KB, i % KB
                    act.wait_ge(norm_full, at.next("norm_group") + 1)
                    act.activation(in_high[:, g * KB:(g + 1) * KB, t, :],
                                   full[:, i % 2, :].rearrange("p (k n) -> p k n", n=P), ACT.Copy).then_inc(norm_high, 1)

            act.wait_ge(start_turned, 1)
            act.activation(sig[:, 0, 0:2 * NK], small_bank[:, 0:2 * NK], ACT.Sigmoid).then_inc(cond_sig, 1)
            act.wait_ge(cond_full_ready, 1)
            act.activation(cond[:, :, 0:2], cond_full[:, :].rearrange("p (w k) -> p k w", w=2), ACT.Copy).then_inc(cond_high, 1)

            def mod_start(c):
                for j in range(UPC):
                    split_high()
            at.rounds(act, 8, mod_start)
            act.wait_ge(pick_in, 16)
            act.activation(pick[:, :, :], proj[0:36, 0, 0:4 * P].rearrange("p (b n) -> p b n", b=4), ACT.Copy).then_inc(pick_ready, 1)
            act.wait_ge(x_ready, 32)

            for l in range(DEPTH):
                interleave = l == 0
                if l:
                    act.wait_ge(chunk_read, LAYER_CHUNKS * l)
                norm()

                def copy_proj(col, width, after):
                    q = at.next("chunk")
                    act.wait_ge(unit_used, at.done("unit") - after)
                    for t in range(TILES):
                        dst, src = proj[:, t, bass.ds(col, width)], banks[copy_proj.pair * 2 + t][:, 0:width]
                        if isinstance(col, int) and col == AQ:
                            dst = dst.rearrange("p (h a d) -> p a h d", a=2, d=HD)
                            src = src.rearrange("p (a h d) -> p a h d", a=2, d=HD)
                        copied = act.activation(dst, src, ACT.Copy)
                        if t == 0:
                            continue
                        copied.then_inc(chunk_read, 1)

                at.at["chunk"] = at.at.get("chunk", 0) - 1

                def w_in_pair(i):
                    for h in range(2):
                        split_high()
                        split_high()
                        if h or not at.first:
                            copy_proj.pair = (l * LAYER_CHUNKS + h + 1) % 2
                            copy_proj((i * 2 + h - 1) * COLS, COLS, 2)
                        else:
                            at.next("chunk")
                        split_high()
                        split_high()
                at.rounds(act, IN_CHUNKS // 2, w_in_pair)
                split_high(IN_REST)
                split_high(IN_REST)
                copy_proj.pair = (l * LAYER_CHUNKS + 1) % 2
                copy_proj((IN_CHUNKS - 1) * COLS, COLS, 2)
                split_high(IN_REST)
                split_high(IN_REST)
                copy_proj.pair = l * LAYER_CHUNKS % 2
                copy_proj(IN_CHUNKS * COLS, IN_REST, 0)

                def out_copy(first, step, t, source, scale=1.0):
                    n = at.next("out")
                    dst = br_high[:, first:first + step * (source.shape[1] - 1) + 1:step, t, :]
                    act.activation(dst, source, ACT.Copy, scale=scale).then_inc(out_high, 1)

                for t in (SAMPLE, PROMPT):
                    n = at.next("fourier")
                    act.wait_ge(f_first, n + 1)
                    for g in range(2):
                        for part, scale in ((0, 1.0 / P), (1, -1.0 / P)):
                            src = banks[g][:, :].rearrange("p (g c n) -> p g c n", g=2, c=2)[:, :, part, :]
                            dst = e_buf[:, t, g * 512:(g + 1) * 512].rearrange("p (g c n) -> p g c n", g=2, c=2)[:, :, part, :]
                            copied = act.activation(dst, src, ACT.Copy, scale=scale)
                    copied.then_inc(f_copied, 1)
                    act.wait_ge(f_second, n + 1)
                    out_copy(4 * BRANCH["F"], 1, t, banks[4][:, :].rearrange("p (g n) -> p g n", n=P))

                act.wait_ge(lam_sum_ready, l + 1)
                act.activation(lam_exp, lam_sum, ACT.Exp).then_inc(lam_exp_ready, 1)

                def copy_qk(j):
                    b, t = jobs()[j]
                    if j >= 2:
                        act.wait_ge(scored, NG * l + 2 * (j - 1))
                    for i in range(TURNS[j]):
                        n = min(4, n_blocks(b, t) - 4 * i)
                        act.wait_ge(qk_turned, at.next("qk") + 1)
                        act.activation(qk_t[:, j % 2, 4 * i:4 * i + n, :],
                                       small_bank[:, 0:n * P].rearrange("p (k n) -> p k n", n=P), ACT.Copy,
                                       scale=HD ** -0.5 if i == 0 else 1.0).then_inc(qk_ready, 1)

                def exps(G):
                    j, b, t, g = GROUPS[G]
                    act.wait_ge(top_ready, NG * l + G + 1)
                    if G >= 2:
                        act.wait_ge(p_turned, NG * l + G - 1)
                    w = P * keys(t)
                    if b == "A":
                        act.activation(esink[:, 4 * (G % 2):4 * (G % 2) + 4], esink[:, 4 * (G % 2):4 * (G % 2) + 4], ACT.Exp)
                    for r in range(4):
                        bank, c = score_row(G, r, t)
                        k = 4 * (G % 2) + r
                        done = act.activation(e_buf[:, G % 2, r * w:(r + 1) * w], bank[:, c:c + w], ACT.Exp,
                                              bias=neg_top[:, k:k + 1], accum_out=esum[:, k:k + 1])
                    done.then_inc(exp_ready, 1)

                def copy_p(G):
                    j, b, t, g = GROUPS[G]
                    n = (2 if b == "B" else 4) * keys(t)
                    act.wait_ge(p_turned, NG * l + G + 1)
                    need(act, pv_done, NG * l + G)
                    for h in range((n + 3) // 4):
                        m = min(4, n - 4 * h)
                        copied = act.activation(p_t[:, 4 * h:4 * h + m, :],
                                                turn_banks[h][:, 0:m * P].rearrange("p (k n) -> p k n", n=P), ACT.Copy)
                    copied.then_inc(p_ready, 1)

                copy_qk(0)
                exps(0)
                for G, (j, b, t, g) in enumerate(GROUPS):
                    if G + 1 < NG:
                        exps(G + 1)
                    copy_p(G)
                    if b != "B":
                        act.wait_ge(pv_done, NG * l + G + 1)
                        first, step = (g, 2) if b == "A" else (8 + 2 * g, 1)
                        out_copy(first, step, t, banks[4][:, 0:2 * P].rearrange("p (k n) -> p k n", n=P))
                    elif g == 1:
                        n = at.next("sub")
                        act.wait_ge(pv_done, NG * l + G + 1)
                        out_b = e_buf[:, G % 2, 0:512]
                        for h in range(B_H):
                            done = act.activation(out_b[:, h * P:(h + 1) * P], banks[4][:, h * P:(h + 1) * P], ACT.Square,
                                                  accum_out=sub_sq[:, h:h + 1])
                        done.then_inc(sub_squares, 1)
                        act.wait_ge(sub_mean, n + 1)
                        act.activation(sub_rstd, sub_rstd, ACT.Sqrt).then_inc(sub_root, 1)
                        act.wait_ge(sub_turned, n + 1)
                        out_copy(4, 1, t, banks[4][:, :].rearrange("p (k n) -> p k n", n=P), scale=sub_g[:, l:l + 1])
                    if g == 0 and j + 1 < len(jobs()):
                        copy_qk(j + 1)

                def gate_pair(b):
                    return (l * LAYER_CHUNKS + IN_CHUNKS + 1 + 2 * b) % 2

                def sigmoids(b, after, done_s, width=COLS):
                    act.wait_ge(unit_used, at.done("unit") - after)
                    need(act, chunk_read, at.done("chunk") - 1)
                    for t in range(TILES):
                        done = act.activation(sig[:, t, 0:width], banks[2 * b + t][:, 0:width], ACT.Sigmoid)
                    done.then_inc(done_s, 1)

                def gates(n):
                    for b in range(4):
                        for j in range(UPC):
                            if b == 0 and j == 2:
                                r = at.next("bg")
                                act.wait_ge(bg_in, r * 32 + 32)
                                need(act, unit_used, at.done("unit") - 3 - UPC * interleave)
                                act.activation(bg_split[:, :], bg_raw[:, :], ACT.Copy).then_inc(bg_high, 1)
                            split_high()
                        at.next("chunk")
                        if interleave:
                            split_high()
                            split_high()
                            sigmoids(gate_pair(b), 2, chunk_read)
                            split_high()
                            split_high()
                            split_high()
                        else:
                            split_high()
                            sigmoids(gate_pair(b), 1, chunk_read)
                        at.next("chunk")
                at.rounds(act, NCH, gates)

                for i in range(2 * KB):
                    t, g = i // KB, i % KB
                    act.wait_ge(merged_turned, at.next("merged") + 1)
                    act.activation(in_high[:, g * KB:(g + 1) * KB, t, :],
                                   turn_banks[i % 2][:, :].rearrange("p (k n) -> p k n", n=P), ACT.Copy).then_inc(merged_high, 1)

                def gate_rows():
                    for i in range(2 * KB):
                        t, g = i // KB, i % KB
                        act.wait_ge(row_summed, at.next("row") + 1)
                        act.activation(gate_row[:, t, g * COLS:(g + 1) * COLS], turn_banks[i % 2][:, :], ACT.Copy).then_inc(row_ready, 1)
                gate_rows()

                def w_out(n):
                    for j in range(UPC):
                        split_high()
                    at.next("chunk")
                at.rounds(act, NCH, w_out)

                act.wait_ge(chunk_read, at.done("chunk"))
                norm()
                act.wait_ge(router_in, 32 * (l + 1))
                act.activation(router_high[:, :, :], router_raw[:, :, :], ACT.Copy).then_inc(router_high_s, 1)
                gate_rows()
                act.wait_ge(route_top, 2 * l + 1)
                for t in range(TILES):
                    done = act.activation(route[:, t, 64:68], route[:, t, 0:4], ACT.Exp, bias=route[:, t, 41:42],
                                          accum_out=route[:, t, 42:43])
                done.then_inc(route_exp, 1)
                act.wait_ge(route_top, 2 * l + 2)
                act.activation(route[:, :, 43:44], route[:, :, 43:44], ACT.Exp).then_inc(route_exp, 1)

                def hid_copy(e):
                    act.wait_ge(hid_turned, at.next("hid") + 1)
                    act.activation(hid_high[:, :, :, :].rearrange("p k t n -> p (k t n)")[:, bass.ds(e * 512, 512)],
                                   turn_banks[hid_copy.bank][:, :], ACT.Copy).then_inc(hid_high_ready, 1)

                def experts(i):
                    for h in range(2):
                        if interleave:
                            for j in range(UPC):
                                split_high()
                        split_high(loads=2)
                        split_high(loads=2)
                        later = h or not at.first
                        if later:
                            sigmoids((l * LAYER_CHUNKS + LAYER_CHUNKS - NCH + h + 1) % 2, 2 + 4 * interleave, gate_ready, DE)
                        split_high(loads=2)
                        split_high(loads=2)
                        hid_copy.bank = (h + 1) % 2
                        if later:
                            hid_copy(i * 2 + (h - 1))
                        else:
                            at.next("hid")
                        at.next("chunk")
                at.at["hid"] = at.at.get("hid", 0) - 1
                at.rounds(act, NE // 2, experts)
                sigmoids((l * LAYER_CHUNKS + LAYER_CHUNKS - NCH + 1) % 2, 0, gate_ready, DE)
                hid_copy.bank = 1
                hid_copy(NE - 1)

                def down(n):
                    for j in range(NE * DE // P // KB + 2 * UPC * interleave):
                        split_high()
                    at.next("chunk")
                at.rounds(act, NCH, down)

            act.wait_ge(chunk_read, LAYER_CHUNKS * DEPTH)
            norm_scale(None)

        @block.vector
        def _(dve):
            at = Cursor()

            def split_low(width=COLS):
                slot, part = at.parity("unit", RAW_SLOTS), at.parity("unit", SPLIT_SLOTS)
                u = at.next("unit")
                dve.wait_ge(high_ready, u + 1)
                dve.tensor_tensor(low_w[:, part, :, 0:width], raw_w[:, slot, :, 0:width],
                                  high_w[:, part, :, 0:width].bitcast(F32), ALU.subtract).then_inc(low_ready, 1)

            def mod_copy(after):
                m = at.next("mod_copy")
                dve.wait_ge(unit_used, at.done("unit") - after)
                need(dve, mod_turned, m)
                dve.tensor_copy(m4[:, :], mod_bank[0:4, :]).then_inc(mod_copied, 1)

            def mod_store(layer, c):
                m = at.next("mod_store")
                dve.wait_ge(mod_turned, m + 1)
                dve.tensor_tensor(mod[:, layer, bass.ds(c * 4, 4), :], small_bank[:, 0:8].rearrange("p (k w) -> p k w", w=2),
                                  b_mod_t[:, layer, bass.ds(c * 4, 4)].unsqueeze(2).broadcast_to([P, 4, 2]),
                                  ALU.add).then_inc(mod_stored, 1)

            def mean_scale(count):
                n = at.next("norm")
                dve.wait_ge(squares, 2 * n + 2)
                dve.tensor_scalar(sum_sq, sum_sq, 1.0 / D, EPS, ALU.mult, ALU.add)
                dve.drain()
                dve.reciprocal(rstd, sum_sq).then_inc(mean_ready, 1)
                dve.wait_ge(root_ready, n + 1)

            def norm(l, which):
                shift, scale, gain = 48 * which, 48 * which + 16, 2 * l + which
                dve.drain()
                dve.scalar_tensor_tensor(scale_t[:, :, :], mod[:, l, scale:scale + NK, :], 1.0,
                                         gains[:, gain, :].unsqueeze(2).broadcast_to([P, NK, 2]), ALU.add, ALU.mult)
                mean_scale(D)

                def low(i):
                    t, g = i // KB, i % KB
                    dve.wait_ge(norm_high, at.next("norm_low") + 1)
                    dst = slice(g * KB, (g + 1) * KB)
                    dve.tensor_tensor(in_low[:, dst, t, :], full[:, i % 2, :].rearrange("p (k n) -> p k n", n=P),
                                      in_high[:, dst, t, :].bitcast(F32), ALU.subtract).then_inc(norm_low, 1)

                for i in range(2 * KB):
                    t, g = i // KB, i % KB
                    n = at.next("norm_group")
                    if g == 0:
                        need(dve, norm_turned, n)
                        dve.tensor_scalar(normed[:, :], x[:, t, :], rstd[:, t:t + 1], None, ALU.mult).then_inc(normed_ready, 1)
                    dve.wait_ge(norm_turned, n + 1)
                    dve.drain()
                    for k in range(KB):
                        kk = g * KB + k
                        done = dve.tensor_scalar(full[:, i % 2, k * P:(k + 1) * P], turn_banks[i % 2][:, k * P:(k + 1) * P],
                                                 scale_t[:, kk, t:t + 1], mod[:, l, shift + kk, t:t + 1], ALU.mult, ALU.add)
                    done.then_inc(norm_full, 1)
                    if i:
                        low(i - 1)
                dve.wait_ge(norm_high, n + 1)
                low(2 * KB - 1)

            dve.wait_ge(cond_sig, 1)
            dve.tensor_copy(b_mod_t[:, :, :].rearrange("p l k -> p (l k)"), small_bank[:, 32:32 + DEPTH * MODS * 4])
            dve.tensor_copy(gains[:, :, :].rearrange("p l k -> p (l k)"), small_bank[:, 224:224 + 4 * NK])
            dve.tensor_tensor(cond_full[:, :], small_bank[:, 0:2 * NK], sig[:, 0, 0:2 * NK], ALU.mult).then_inc(cond_full_ready, 1)
            dve.wait_ge(cond_high, 1)
            dve.tensor_tensor(cond[:, :, 2:4], cond_full[:, :].rearrange("p (w k) -> p k w", w=2),
                              cond[:, :, 0:2].bitcast(F32), ALU.subtract).then_inc(cond_ready, 1)

            def mod_start(c):
                split_low()
                split_low()
                later = not at.first
                if later:
                    mod_copy(2)
                else:
                    at.next("mod_copy")
                split_low()
                split_low()
                if later:
                    mod_store(0, c - 1)
                else:
                    at.next("mod_store")
            at.at["mod_copy"] = at.at["mod_store"] = -1
            at.rounds(dve, 8, mod_start)
            mod_copy(0)
            mod_store(0, 7)
            dve.wait_ge(vectors_in, 16 * 4 * DEPTH)
            for l in range(DEPTH):
                dve.tensor_scalar(sub_g[:, l:l + 1], sub_g[:, l:l + 1], 1.0 - LAM[l], None, ALU.mult)

            for l in range(DEPTH):
                interleave = l == 0
                norm(l, 0)

                def w_in_pair(i):
                    for j in range(2 * UPC):
                        split_low()
                    at.next("chunk")
                    at.next("chunk")
                at.rounds(dve, IN_CHUNKS // 2, w_in_pair)
                for j in range(UPC):
                    split_low(IN_REST)
                at.next("chunk")

                dve.wait_ge(chunk_read, LAYER_CHUNKS * l + IN_CHUNKS + 1)
                cos, sin = (constant("rope")[:, i * 32:(i + 1) * 32].rearrange("p (x f) -> p x f", x=2) for i in range(2))
                for a, n in ((AQ, 10), (BQ, 16)):
                    pair = proj[:, SAMPLE, a:a + n * HD].rearrange("p (h x y f) -> p h x y f", x=2, y=2, f=HD // 4)
                    one, two = pair[:, :, :, 0, :], pair[:, :, :, 1, :]
                    c, s = (v.unsqueeze(1).broadcast_to([P, n, 2, HD // 4]) for v in (cos, sin))
                    flat = p_t[:, :, :].rearrange("p k n -> p (k n)")
                    u, v = (flat[:, i * 512:i * 512 + n * 32].rearrange("p (h x f) -> p h x f", x=2, f=HD // 4) for i in range(2))
                    dve.tensor_tensor(u, one, s, ALU.mult)
                    dve.tensor_tensor(v, two, s, ALU.mult)
                    dve.drain()
                    dve.tensor_tensor(one, one, c, ALU.mult)
                    dve.tensor_tensor(two, two, c, ALU.mult)
                    dve.drain()
                    dve.tensor_tensor(one, one, v, ALU.subtract)
                    dve.tensor_tensor(two, two, u, ALU.add).then_inc(roped, 1)
                    dve.drain()

                dve.wait_ge(lam_in_s, 16 * (l + 1))
                quad = lam_in[:, :, :].rearrange("p (a b) n -> p a b n", b=2)
                dve.tensor_tensor(quad[:, :, 0, :], quad[:, :, 0, :], quad[:, :, 1, :], ALU.mult)
                dve.drain()
                dve.tensor_reduce(lam_sum, quad[:, :, 0, :], AX.X, ALU.add).then_inc(lam_sum_ready, 1)
                dve.wait_ge(hankel_in, 64 * (l + 1))
                dve.tensor_tensor(hankel[:, :, :], hankel[:, :, :], mask.unsqueeze(1).broadcast_to([P, C_H, P]), ALU.add).then_inc(hankel_ready, 1)

                def out_rest(first, step, t, source, scale=None):
                    n = at.next("out")
                    dve.wait_ge(out_high, n + 1)
                    s = slice(first, first + step * (source.shape[1] - 1) + 1, step)
                    if scale is None:
                        done = dve.tensor_tensor(br_low[:, s, t, :], source, br_high[:, s, t, :].bitcast(F32), ALU.subtract)
                    else:
                        done = dve.scalar_tensor_tensor(br_low[:, s, t, :], source, scale, br_high[:, s, t, :].bitcast(F32),
                                                        ALU.mult, ALU.subtract)
                    done.then_inc(out_low, 1)

                for t in (SAMPLE, PROMPT):
                    out_rest(4 * BRANCH["F"], 1, t, banks[4][:, :].rearrange("p (g n) -> p g n", n=P))
                dve.wait_ge(lam_exp_ready, l + 1)
                dve.tensor_tensor(lam, lam_exp[:, 0:1], lam_exp[:, 1:2], ALU.subtract)
                dve.drain()
                dve.tensor_scalar(lam, lam, LAM[l], None, ALU.add)

                def tops(G):
                    j, b, t, g = GROUPS[G]
                    w, k = P * keys(t), 4 * (G % 2)
                    dve.wait_ge(scored, NG * l + G + 1)
                    for h in range(2):
                        bank, _ = score_row(G, h, t)
                        dve.tensor_reduce(top[:, k + h:k + 4:2], bank[:, 0:2 * w].rearrange("p (r n) -> p r n", n=w), AX.X, ALU.max)
                    dve.drain()
                    if b == "A":
                        sink = sinks[:, l, :].rearrange("p (a h) -> p h a", a=2)[:, 2 * g:2 * g + 2, :]
                        v = top[:, k:k + 4].rearrange("p (h a) -> p h a", a=2)
                        dve.tensor_tensor(v, v, sink, ALU.max)
                        dve.drain()
                        dve.tensor_tensor(esink[:, k:k + 4].rearrange("p (h a) -> p h a", a=2), sink, v, ALU.subtract)
                    dve.tensor_scalar(neg_top[:, k:k + 4], top[:, k:k + 4], -1.0, None, ALU.mult).then_inc(top_ready, 1)

                def weights(G):
                    j, b, t, g = GROUPS[G]
                    w, k = P * keys(t), 4 * (G % 2)
                    dve.wait_ge(exp_ready, NG * l + G + 1)
                    if b == "A":
                        dve.tensor_tensor(esum[:, k:k + 4], esum[:, k:k + 4], esink[:, k:k + 4], ALU.add)
                        dve.drain()
                    dve.reciprocal(rsum[:, k:k + 4], esum[:, k:k + 4])
                    dve.drain()
                    e = e_buf[:, G % 2, 0:4 * w].rearrange("p (r n) -> p r n", n=w)
                    if b == "B":
                        odd = rsum[:, k + 1:k + 4:2]
                        dve.tensor_scalar(odd, odd, lam, None, ALU.mult)
                        dve.drain()
                        for h in range(2):
                            dve.tensor_scalar(e[:, 2 * h + 1, :], e[:, 2 * h + 1, :], rsum[:, k + 2 * h + 1:k + 2 * h + 2], None, ALU.mult)
                        dve.drain()
                        for h in range(2):
                            done = dve.scalar_tensor_tensor(e[:, 2 * h, :], e[:, 2 * h, :], rsum[:, k + 2 * h:k + 2 * h + 1],
                                                            e[:, 2 * h + 1, :], ALU.mult, ALU.subtract)
                    else:
                        done = dve.tensor_tensor(e, e, rsum[:, k:k + 4].unsqueeze(2).broadcast_to([P, 4, w]), ALU.mult)
                    done.then_inc(weights_ready, 1)

                tops(0)
                for G, (j, b, t, g) in enumerate(GROUPS):
                    weights(G)
                    if G + 1 < NG:
                        tops(G + 1)
                    if b != "B":
                        first, step = (g, 2) if b == "A" else (8 + 2 * g, 1)
                        out_rest(first, step, t, banks[4][:, 0:2 * P].rearrange("p (k n) -> p k n", n=P))
                    elif g == 1:
                        n = at.next("sub")
                        dve.wait_ge(sub_squares, n + 1)
                        dve.tensor_scalar(sub_sq, sub_sq, 1.0 / P, EPS, ALU.mult, ALU.add)
                        dve.drain()
                        dve.reciprocal(sub_rstd, sub_sq).then_inc(sub_mean, 1)
                        dve.wait_ge(sub_root, n + 1)
                        dve.tensor_tensor(e_buf[:, G % 2, 0:512].rearrange("p (h n) -> p h n", n=P),
                                          banks[4][:, :].rearrange("p (h n) -> p h n", n=P),
                                          sub_rstd.unsqueeze(2).broadcast_to([P, B_H, P]), ALU.mult).then_inc(sub_ready, 1)
                        out_rest(4, 1, t, banks[4][:, :].rearrange("p (k n) -> p k n", n=P), scale=sub_g[:, l:l + 1])

                def merge(pair, b, n, after):
                    m = at.next(f"merge{l}")
                    dve.drain()
                    dve.wait_ge(chunk_read, m * 2 + (LAYER_CHUNKS * l + IN_CHUNKS + 2))
                    dve.wait_ge(unit_used, at.done("unit") - after)
                    cols = bass.ds(n * COLS, COLS)
                    for t in range(TILES):
                        dst = merged[:, t, cols] if b == 0 else prod[:, t, :]
                        done = dve.tensor_tensor(dst, banks[2 * pair + t][:, :], sig[:, t, :], ALU.mult)
                    if b:
                        dve.drain()
                        done = dve.tensor_tensor(merged[:, :, cols], merged[:, :, cols], prod[:, :, :], ALU.add)
                    done.then_inc(chunk_read, 1)

                def proj_pair(b):
                    return (l * LAYER_CHUNKS + IN_CHUNKS + 2 + 2 * b) % 2

                dve.memset(bg_raw[:, :], 0.0).then_inc(bg_clear, 1)

                def gates(n):
                    r = at.next("bg")
                    for b in range(4):
                        later = b or not at.first
                        split_low()
                        if interleave:
                            if later:
                                mod_copy(1 + 1)
                            else:
                                at.next("mod_copy")
                        split_low()
                        if b == 0:
                            dve.wait_ge(bg_high, r + 1)
                            dve.tensor_tensor(bg_split[32:36, :], bg_raw[32:36, :], bg_split[32:36, :].bitcast(F32), ALU.subtract).then_inc(bg_ready, 1)
                        if later:
                            merge(proj_pair((b + 3) % 4), (b + 3) % 4, n if b else n - 1, 2)
                        else:
                            at.next(f"merge{l}")
                        split_low()
                        split_low()
                        if interleave:
                            if later:
                                mod_store(0, n * 4 + (b + 7))
                            else:
                                at.next("mod_store")
                            for j in range(UPC):
                                split_low()
                        split_low()
                at.at[f"merge{l}"] = -1
                if interleave:
                    at.at["mod_copy"] -= 1
                    at.at["mod_store"] -= 1
                at.rounds(dve, NCH, gates)
                if interleave:
                    mod_copy(1)
                merge(proj_pair(3), 3, NCH - 1, 0)
                if interleave:
                    mod_store(0, MODS - 1)

                for i in range(2 * KB):
                    t, g = i // KB, i % KB
                    dve.wait_ge(merged_high, at.next("merged") + 1)
                    s = slice(g * KB, (g + 1) * KB)
                    dve.tensor_tensor(in_low[:, s, t, :], turn_banks[i % 2][:, :].rearrange("p (k n) -> p k n", n=P),
                                      in_high[:, s, t, :].bitcast(F32), ALU.subtract).then_inc(merged_low, 1)

                def gate_rows(first):
                    dve.memset(ones[:, :], 1.0)
                    dve.drain()
                    for i in range(2 * KB):
                        t, g = i // KB, i % KB
                        n = at.next("row")
                        need(dve, row_summed, n - 1)
                        for k in range(KB):
                            done = dve.tensor_scalar(full[:, i % 2, k * P:(k + 1) * P], ident,
                                                     mod[:, l, first + g * KB + k, t:t + 1], None, ALU.mult)
                        done.then_inc(diag_ready, 1)
                gate_rows(32)

                def add_to_x(pair, n, after):
                    dve.drain()
                    dve.wait_ge(unit_used, at.done("unit") - after)
                    cols = bass.ds(n * COLS, COLS)
                    for t in range(TILES):
                        dve.tensor_tensor(prod[:, t, :], banks[2 * pair + t][:, :], gate_row[:, t, cols], ALU.mult)
                    dve.drain()
                    dve.tensor_tensor(x[:, :, cols], x[:, :, cols], prod[:, :, :], ALU.add).then_inc(chunk_read, 1)

                def w_out_pair(i):
                    for h in range(2):
                        split_low()
                        split_low()
                        if h or not at.first:
                            add_to_x((l * LAYER_CHUNKS + LAYER_CHUNKS - NE - 2 * NCH + h + 1) % 2, i * 2 + (h - 1), 2)
                        split_low()
                        split_low()
                dve.wait_ge(row_ready, at.done("row"))
                at.rounds(dve, NCH // 2, w_out_pair)
                add_to_x((l * LAYER_CHUNKS + LAYER_CHUNKS - NE - 2 * NCH + 1) % 2, NCH - 1, 0)

                norm(l, 1)
                dve.wait_ge(router_high_s, l + 1)
                dve.tensor_tensor(router_low[:, :, :], router_raw[:, :, :], router_high[:, :, :].bitcast(F32), ALU.subtract).then_inc(router_ready, 1)
                gate_rows(80)

                dve.memset(route[:, :, 0:8], -3e38)
                dve.drain()
                dve.wait_ge(routed, l + 1)
                logits = small_bank[:, 0:64].rearrange("p (t n) -> p t n", t=2)
                for a, n, c in ((0, 4, 0), (8, 16, 4)):
                    dve.tensor_tensor(route[:, :, a:a + n], logits[:, :, c:c + n],
                                      router_b[:, l, c:c + n].unsqueeze(1).broadcast_to([P, 2, n]), ALU.add)
                dve.drain()

                def best(cols):
                    for t in range(TILES):
                        dve.max(picked[:, t, :], route[:, t, cols])
                    dve.drain()
                    for t in range(TILES):
                        dve.max_index(picked_at[:, t, :], picked[:, t, :], route[:, t, cols])
                    dve.drain()
                best(slice(0, 8))
                dve.tensor_copy(route[:, :, 40:41], picked_at[:, :, 0:1])
                dve.tensor_scalar(route[:, :, 41:42], picked[:, :, 0:1], -1.0, None, ALU.mult).then_inc(route_top, 1)
                dve.drain()
                for t in range(TILES):
                    dve.tensor_scalar(route[:, t, 24:40], constant("group"), route[:, t, 40:41], None, ALU.is_equal)
                dve.drain()
                dve.tensor_scalar(route[:, :, 48:64], route[:, :, 24:40], 1e30, -1e30, ALU.mult, ALU.add)
                dve.tensor_tensor(route[:, :, 24:40], route[:, :, 24:40], route[:, :, 8:24], ALU.mult)
                dve.drain()
                dve.tensor_tensor(route[:, :, 24:40], route[:, :, 24:40], route[:, :, 48:64], ALU.add)
                dve.drain()
                best(slice(24, 40))
                dve.tensor_tensor(route[:, :, 43:44], picked[:, :, 1:2], picked[:, :, 0:1], ALU.subtract).then_inc(route_top, 1)
                dve.tensor_copy(route[:, :, 44:46], picked_at[:, :, 0:2])
                dve.wait_ge(route_exp, 2 * l + 2)
                dve.tensor_scalar(route[:, :, 46:47], route[:, :, 43:44], 1.0, None, ALU.add)
                dve.tensor_copy(route[:, :, 47:48], route[:, :, 42:43])
                dve.drain()
                dve.reciprocal(route[:, :, 46:48], route[:, :, 46:48])
                dve.drain()
                dve.tensor_tensor(route[:, :, 46:47], route[:, :, 46:47], route[:, :, 47:48], ALU.mult)
                dve.drain()
                dve.tensor_tensor(route[:, :, 47:48], route[:, :, 46:47], route[:, :, 43:44], ALU.mult)
                dve.drain()
                for t in range(TILES):
                    dve.tensor_scalar(comb[:, t, :], constant("which"), route[:, t, 44:45], route[:, t, 46:47], ALU.is_equal, ALU.mult)
                    dve.tensor_scalar(route[:, t, 48:64], constant("which"), route[:, t, 45:46], route[:, t, 47:48], ALU.is_equal, ALU.mult)
                dve.drain()
                dve.tensor_tensor(comb[:, :, :], comb[:, :, :], route[:, :, 48:64], ALU.add)
                dve.drain()

                def hidden(pair, e):
                    n = at.next("hidden")
                    dve.drain()
                    dve.wait_ge(gate_ready, at.next("sig_read") + 1)
                    need(dve, hid_turned, n)
                    for t in range(TILES):
                        dve.scalar_tensor_tensor(prod[:, t, 0:DE], banks[2 * pair + t][:, DE:2 * DE], comb[:, t, bass.ds(e, 1)],
                                                 sig[:, t, 0:DE], ALU.mult, ALU.mult)
                    dve.drain()
                    for t in range(TILES):
                        done = dve.tensor_tensor(prod[:, t, DE:2 * DE], banks[2 * pair + t][:, 0:DE], prod[:, t, 0:DE], ALU.mult)
                    done.then_inc(chunk_read, 1)

                def hid_rest(e, bank):
                    dve.wait_ge(hid_high_ready, at.next("hid") + 1)
                    cols = bass.ds(e * 512, 512)
                    dve.tensor_tensor(hid_low[:, :, :, :].rearrange("p k t n -> p (k t n)")[:, cols], turn_banks[bank][:, :],
                                      hid_high[:, :, :, :].rearrange("p k t n -> p (k t n)")[:, cols].bitcast(F32),
                                      ALU.subtract).then_inc(hid_stored, 1)

                first_pair = (l * LAYER_CHUNKS + LAYER_CHUNKS - NCH) % 2

                def experts(i):
                    for h in range(2):
                        later = h or not at.first
                        if interleave:
                            for j in range(UPC):
                                split_low()
                        split_low()
                        split_low()
                        if interleave:
                            mod_copy(2)
                        if later:
                            hidden((first_pair + h + 1) % 2, i * 2 + (h - 1))
                        else:
                            at.next("sig_read")
                            at.next("hidden")
                        split_low()
                        split_low()
                        if interleave:
                            mod_store(1, i * 2 + h)
                        if later:
                            hid_rest(i * 2 + (h - 1), (h + 1) % 2)
                        else:
                            at.next("hid")
                for name in ("sig_read", "hidden", "hid"):
                    at.at[name] = at.at.get(name, 0) - 1
                at.rounds(dve, NE // 2, experts)
                hidden((first_pair + 1) % 2, NE - 1)
                hid_rest(NE - 1, 1)

                def down_pair(i):
                    for h in range(2):
                        later = h or not at.first
                        if interleave:
                            for j in range(UPC + 2):
                                split_low()
                            mod_copy(2)
                            split_low()
                            split_low()
                            mod_store(1, (i * 2 + h) * 2 + NE)
                        split_low()
                        split_low()
                        if interleave:
                            mod_copy(2)
                        if later:
                            add_to_x((first_pair + h + 1) % 2, i * 2 + (h - 1), 2 + 2 * UPC * interleave)
                        split_low()
                        split_low()
                        if interleave:
                            mod_store(1, (i * 2 + h) * 2 + (NE + 1))
                        for j in range(NE * DE // P // KB - 4):
                            split_low()
                dve.wait_ge(row_ready, at.done("row"))
                at.rounds(dve, NCH // 2, down_pair)
                add_to_x((first_pair + 1) % 2, NCH - 1, 0)

            mean_scale(D)
            dve.wait_ge(final_in, 16)
            for t in range(TILES):
                dve.scalar_tensor_tensor(x[:, t, :], x[:, t, :], rstd[:, t:t + 1], merged[:, 0, :], ALU.mult, ALU.mult).then_inc(final_scaled, 1)

        @block.tensor
        def _(pe):
            at = Cursor()

            def next_unit():
                part = at.parity("unit", SPLIT_SLOTS)
                pe.wait_ge(low_ready, at.next("unit") + 1)
                return part

            def chunk(highs, lows, first_block, blocks, width=COLS, bias=None):
                pair = at.parity("chunk", 2)
                need(pe, chunk_read, at.next("chunk") - 1)
                for j in range(blocks // KB):
                    if j == 2 and chunk.between is not None:
                        chunk.between()
                    part = next_unit()
                    for k in range(KB):
                        kk = first_block + j * KB + k
                        for t in range(TILES):
                            out = banks[2 * pair + t][:, 0:width]
                            start = j == 0 and k == 0
                            stop = j == blocks // KB - 1 and k == KB - 1
                            pe.matmul(out, highs[:, kk, t, :], high_w[:, part, k, 0:width], start=start, stop=False)
                            pe.matmul(out, highs[:, kk, t, :], low_w[:, part, k, 0:width], start=False, stop=False)
                            done = pe.matmul(out, lows[:, kk, t, :], high_w[:, part, k, 0:width], start=False, stop=stop)
                    done.then_inc(unit_used, 1)
                    if j == 2 and bias is not None:
                        bias(pair)
            chunk.between = None

            def mod_chunk():
                need(pe, mod_copied, at.next("mod"))
                for j in range(UPC):
                    part = next_unit()
                    for k in range(KB):
                        kk = j * KB + k
                        pe.matmul(mod_bank[0:4, :], cond[:, kk, :], high_w[:, part, k, :], start=kk == 0, stop=False)
                        done = pe.matmul(mod_bank[0:4, :], cond[:, kk, :], low_w[:, part, k, :], start=False, stop=kk == NK - 1)
                    done.then_inc(unit_used, 1)
                    if j == 1 and mod_chunk.between is not None:
                        mod_chunk.between()
            mod_chunk.between = None

            def mod_turn():
                m = at.next("mod_turn")
                pe.wait_ge(mod_copied, m + 1)
                need(pe, mod_stored, m)
                for k in range(4):
                    done = pe.matmul(small_bank[:, 2 * k:2 * k + 2], m4[:, k * P:(k + 1) * P], fold[0:4, :], start=True, stop=True)
                done.then_inc(mod_turned, 1)

            def turn(bank, col, src, width=P):
                return pe.transpose(bank[:, col:col + width], src, ident[0:src.shape[0], 0:src.shape[0]])

            def norm():
                for i in range(2 * KB):
                    t, g = i // KB, i % KB
                    n = at.next("norm_group")
                    if g == 0:
                        pe.wait_ge(normed_ready, at.next("norm") + 1)
                    need(pe, norm_full, n - 1)
                    for k in range(KB):
                        done = turn(turn_banks[i % 2], k * P, normed[:, (g * KB + k) * P:(g * KB + k + 1) * P])
                    done.then_inc(norm_turned, 1)
                pe.wait_ge(norm_low, at.done("norm_group"))

            def gate_rows():
                for i in range(2 * KB):
                    n = at.next("row")
                    pe.wait_ge(diag_ready, n + 1)
                    need(pe, row_ready, n - 1)
                    pe.matmul(turn_banks[i % 2][:, :], ones[:, :], full[:, i % 2, :], start=True, stop=True).then_inc(row_summed, 1)

            pe.wait_ge(start_in, 16 * (3 + DEPTH + 2 * DEPTH))
            turn(small_bank, 0, normed[0:2 * NK, 0:P], 2 * NK)
            for l in range(DEPTH):
                turn(small_bank, 32 + l * MODS * 4, normed[0:MODS * 4, (1 + l) * P:(2 + l) * P], MODS * 4)
            turn(small_bank, 224, normed[0:4 * NK, 3 * P:4 * P], 4 * NK).then_inc(start_turned, 1)
            pe.wait_ge(cond_ready, 1)

            def mod_start(c):
                later = not at.first
                if later:
                    mod_chunk.between = mod_turn
                else:
                    at.next("mod_turn")
                mod_chunk()
                mod_chunk.between = None
            at.at["mod_turn"] = -1
            at.rounds(pe, 8, mod_start)
            mod_turn()
            pe.wait_ge(pick_ready, 1)

            for l in range(DEPTH):
                interleave = l == 0
                norm()

                def w_in_pair(i):
                    for h in range(2):
                        chunk(in_high, in_low, 0, NK)
                at.rounds(pe, IN_CHUNKS // 2, w_in_pair)
                chunk(in_high, in_low, 0, NK, IN_REST)
                pe.wait_ge(chunk_read, LAYER_CHUNKS * l + IN_CHUNKS + 1)
                pe.wait_ge(mod_stored, at.done("mod_turn"))

                for t in (SAMPLE, PROMPT):
                    n = at.next("fourier")
                    need(pe, f_copied, n)
                    for g in range(4):
                        done = pe.matmul(banks[g // 2][:, g % 2 * 256:g % 2 * 256 + 256],
                                         proj[:, t, FF + g * P:FF + (g + 1) * P], fourier, start=True, stop=True)
                    done.then_inc(f_first, 1)
                    pe.wait_ge(f_copied, n + 1)
                    need(pe, out_low, at.next("out"))
                    half = e_buf[:, t, :].rearrange("p (g c n) -> p g c n", g=4, c=2)
                    pe.matmul(banks[4][:, :], fourier[:, 0:P], half[:, :, 0, :], start=True, stop=False)
                    pe.matmul(banks[4][:, :], fourier[:, P:2 * P], half[:, :, 1, :], start=False, stop=True).then_inc(f_second, 1)

                def turn_qk(j):
                    b, t = jobs()[j]
                    row = proj[:, t, :]
                    if b == "A":
                        srcs = [row[:, AQ + i * P:AQ + (i + 1) * P] for i in range(5)]
                        cached = [cache_a[:, 0, :]]
                    else:
                        q, k = (BQ, BK) if b == "B" else (CQ, CK)
                        srcs = [row[:, a + i * P:a + (i + 1) * P] for a in (q, k) for i in range(4)]
                        cached = [cache_bc[:, 0, i * P:(i + 1) * P] for i in range(4)]
                    if t == SAMPLE:
                        srcs += cached
                        if b == "A":
                            pe.wait_ge(roped, 2 * l + 1)
                            pe.wait_ge(cache_a_in, 32 * (l + 1))
                        elif b == "B":
                            pe.wait_ge(roped, 2 * l + 2)
                            pe.wait_ge(cache_bc_in, 64 * l + 32)
                        else:
                            pe.wait_ge(cache_bc_in, 64 * l + 64)
                            pe.wait_ge(hankel_ready, l + 1)
                    for i in range(TURNS[j]):
                        need(pe, qk_ready, at.next("qk"))
                        for k, src in enumerate(srcs[4 * i:4 * i + 4]):
                            done = turn(small_bank, k * P, src)
                        done.then_inc(qk_turned, 1)

                def scores(G):
                    j, b, t, g = GROUPS[G]
                    pe.wait_ge(qk_ready, l * sum(TURNS) + sum(TURNS[:j + 1]))
                    if G >= 2:
                        pe.wait_ge(exp_ready, NG * l + G - 1)
                    for r, (q, k, half, head) in enumerate(heads(b, g)):
                        rows = slice(half * HD, (half + 1) * HD)
                        bank, c = score_row(G, r, t)
                        new, old = 4 + k, 4 + k_blocks(b) + k
                        for i, kb in enumerate((old, new) if t == SAMPLE else (new,)):
                            biased = b == "C" and t == SAMPLE and kb == new
                            out = bank[:, c + i * P:c + (i + 1) * P]
                            done = pe.matmul(out, qk_t[rows, j % 2, q, :], qk_t[rows, j % 2, kb, :], start=True, stop=not biased)
                            if biased:
                                done = pe.matmul(out, mirror, hankel[:, head, :], start=False, stop=True)
                    done.then_inc(scored, 1)

                def turn_weights(G):
                    j, b, t, g = GROUPS[G]
                    w = P * keys(t)
                    pe.wait_ge(weights_ready, NG * l + G + 1)
                    need(pe, p_ready, NG * l + G)
                    rows = (0, 2) if b == "B" else range(4)
                    n = 0
                    for r in rows:
                        for i in range(keys(t)):
                            c = r * w + i * P
                            done = turn(turn_banks[n // 4], n % 4 * P, e_buf[:, G % 2, c:c + P])
                            n += 1
                    done.then_inc(p_turned, 1)

                def values(G):
                    j, b, t, g = GROUPS[G]
                    pe.wait_ge(p_ready, NG * l + G + 1)
                    if not (b == "B" and g == 1):
                        need(pe, out_low, at.next("out"))
                    new = proj[:, t, V_AT[b]:V_AT[b] + (128 if b == "A" else 512)]
                    old = cache_a[:, 1, :] if b == "A" else cache_bc[:, 1, :]
                    rows = heads(b, g)
                    n = 0
                    for r in ((0, 2) if b == "B" else range(4)):
                        head = rows[r][3]
                        a, width = value_cols(b, head)
                        vals = [v[:, a:a + width] for v in ((old, new) if t == SAMPLE else (new,))]
                        for i, v in enumerate(vals):
                            ends = dict(start=i == 0, stop=i == len(vals) - 1)
                            if b == "B":
                                done = pe.matmul(banks[4][:, head * P:(head + 1) * P], p_t[:, n, :], v, **ends)
                            else:
                                half, slot = head % 2, (head // 4 if b == "A" else r // 2)
                                done = pe.matmul(banks[4][half * HD:(half + 1) * HD, slot * P:(slot + 1) * P], v, p_t[:, n, :], **ends)
                            n += 1
                    done.then_inc(pv_done, 1)
                    if b == "B" and g == 1:
                        pe.wait_ge(sub_ready, at.next("sub") + 1)
                        for h in range(B_H):
                            done = turn(banks[4], h * P, e_buf[:, G % 2, h * P:(h + 1) * P])
                        done.then_inc(sub_turned, 1)

                turn_qk(0)
                scores(0)
                for G, (j, b, t, g) in enumerate(GROUPS):
                    if G + 1 < NG:
                        scores(G + 1)
                    turn_weights(G)
                    values(G)
                    if g == 0 and j + 1 < len(jobs()):
                        turn_qk(j + 1)
                pe.wait_ge(out_low, at.done("out"))

                def gate_bias(pair, b):
                    if b == 0:
                        pe.wait_ge(bg_ready, at.next("bg") + 1)
                    for t in range(TILES):
                        pe.matmul(banks[2 * pair + t][:, :], pick[:, b, :], bg_split[:, :], start=False, stop=False)

                def gates(n):
                    for b in range(4):
                        later = b or not at.first
                        if interleave:
                            if later:
                                chunk.between = mod_turn
                            else:
                                at.next("mod_turn")
                        chunk(in_high, in_low, 0, NK, bias=lambda pair: gate_bias(pair, b))
                        chunk.between = None
                        if interleave:
                            mod_chunk()
                        chunk(br_high, br_low, 4 * b, KB)
                if interleave:
                    at.at["mod_turn"] -= 1
                at.rounds(pe, NCH, gates)
                if interleave:
                    mod_turn()

                pe.wait_ge(chunk_read, at.done("chunk"))
                for i in range(2 * KB):
                    t, g = i // KB, i % KB
                    n = at.next("merged")
                    need(pe, merged_low, n - 1)
                    for k in range(KB):
                        done = turn(turn_banks[i % 2], k * P, merged[:, t, (g * KB + k) * P:(g * KB + k + 1) * P])
                    done.then_inc(merged_turned, 1)
                pe.wait_ge(merged_low, at.done("merged"))
                gate_rows()

                def w_out_pair(i):
                    for h in range(2):
                        chunk(in_high, in_low, 0, NK)
                at.rounds(pe, NCH // 2, w_out_pair)

                norm()
                pe.wait_ge(router_ready, l + 1)
                pe.wait_ge(mod_stored, at.done("mod_turn"))
                for t in range(TILES):
                    for k in range(NK):
                        out = small_bank[:, t * 32:t * 32 + 20]
                        pe.matmul(out, in_high[:, k, t, :], router_high[:, k, :], start=k == 0, stop=False)
                        pe.matmul(out, in_high[:, k, t, :], router_low[:, k, :], start=False, stop=False)
                        done = pe.matmul(out, in_low[:, k, t, :], router_high[:, k, :], start=False, stop=k == NK - 1)
                done.then_inc(routed, 1)
                gate_rows()
                pe.wait_ge(route_top, 2 * l + 1)

                def hid_turn(bank, half):
                    n = at.next("hid")
                    pe.wait_ge(chunk_read, at.done("chunk") - half)
                    need(pe, hid_stored, n - 1)
                    for k in range(2):
                        for t in range(TILES):
                            done = turn(turn_banks[bank], (k * 2 + t) * P, prod[:, t, DE + k * P:DE + (k + 1) * P])
                    done.then_inc(hid_turned, 1)

                def expert_chunk(turned_bank):
                    pair = at.parity("chunk", 2)
                    need(pe, chunk_read, at.next("chunk") - 1)
                    for j in range(UPC):
                        if j == 2 and interleave:
                            mod_turn()
                        if j == 3 and turned_bank is not None:
                            hid_turn(turned_bank, 1)
                        part = next_unit()
                        for k in range(KB):
                            kk = j * KB + k
                            for t in range(TILES):
                                out = banks[2 * pair + t][:, :]
                                pe.matmul(out, in_high[:, kk, t, :], high_w[:, part, k, :], start=kk == 0, stop=False)
                                pe.matmul(out, in_high[:, kk, t, :], low_w[:, part, k, :], start=False, stop=False)
                                done = pe.matmul(out, in_low[:, kk, t, :], high_w[:, part, k, :], start=False, stop=kk == NK - 1)
                        done.then_inc(unit_used, 1)

                def experts(i):
                    for h in range(2):
                        if interleave:
                            mod_chunk()
                        if h or not at.first:
                            expert_chunk((h + 1) % 2)
                        else:
                            at.next("hid")
                            expert_chunk(None)
                at.at["hid"] = at.at.get("hid", 0) - 1
                at.rounds(pe, NE // 2, experts)
                hid_turn(1, 0)
                pe.wait_ge(hid_stored, at.done("hid"))

                def down_pair(i):
                    for h in range(2):
                        if interleave:
                            mod_chunk()
                            mod_chunk.between = mod_turn
                            mod_chunk()
                            mod_chunk.between = None
                            chunk.between = mod_turn
                        chunk(hid_high, hid_low, 0, NE * DE // P)
                        chunk.between = None
                at.rounds(pe, NCH // 2, down_pair)


def kernel(**inputs):
    import concourse.bacc as bacc
    from concourse.bass_utils import run_bass_kernel_spmd

    const, places, pick = shape_constants()
    nc = bacc.Bacc("TRN2", target_bir_lowering=False, num_devices=1, dynamic_dma_scratch_size=64)
    arrays = {n: np.ascontiguousarray(a) for n, a in inputs.items()}
    rpb = arrays["na_rpb"]
    arrays["na_rpb"] = np.pad(rpb, [(0, 0)] * 3 + [(GRID_W - NA_COLS, PAD_W - (GRID_W - NA_COLS) - rpb.shape[-1])])
    arrays["const"], arrays["pick"] = const, pick
    depth, d = inputs["w_in"].shape[:2]
    outs = {
        "y_prompt": inputs["x_prompt"].shape, "y_sample": inputs["x_sample"].shape,
        "new_attn_k": (1, depth, P) + inputs["cache_attn_k"].shape[3:],
        "new_attn_v": (1, depth, P) + inputs["cache_attn_v"].shape[3:],
        "new_diff_k": (1, depth, P) + inputs["cache_diff_k"].shape[3:],
        "new_diff_v": (1, depth, P) + inputs["cache_diff_v"].shape[3:],
        "new_na_k": (1, depth, P) + inputs["cache_na_k"].shape[3:],
        "new_na_v": (1, depth, P) + inputs["cache_na_v"].shape[3:],
    }
    io = {n: nc.dram_tensor("in_" + n, a.shape, F32, kind="ExternalInput").ap() for n, a in arrays.items()}
    io |= {n: nc.dram_tensor("out_" + n, s, F32, kind="ExternalOutput").ap() for n, s in outs.items()}
    trunk(nc, io, places)
    r = run_bass_kernel_spmd(nc, [{"in_" + n: a for n, a in arrays.items()}], core_ids=[0])
    return tuple(r.results[0]["out_" + n] for n in outs)
```

```python
import math
from contextlib import ExitStack

import numpy as np

import concourse.bass as bass
from concourse import mybir

F32 = mybir.dt.float32
F32R = mybir.dt.float32r
U32 = mybir.dt.uint32
ALU = mybir.AluOpType
ACT = mybir.ActivationFunctionType
AX = mybir.AxisListType

P = 128
TILES = 2
PROMPT, SAMPLE = 0, 1
COLS = 512
KB = 4
RAW_SLOTS = 4
SPLIT_SLOTS = 2
MOD_SLOTS = 4
HD = 64
EPS = 1e-6
GRID_W = 64
NA_ROWS, NA_COLS = 8, 16
PAD_W = 128


def need(engine, semaphore, count):
    if not (isinstance(count, int) and count <= 0):
        engine.wait_ge(semaphore, count)


class Cursor:

    def __init__(self):
        self.at = {}
        self.loop = None
        self.first = False

    def next(self, name):
        k = self.at.get(name, 0)
        self.at[name] = k + 1
        if self.loop is None:
            return k
        register, first, start, rates = self.loop
        return (register - first) * rates.get(name, 0) + k

    def done(self, name):
        k = self.next(name)
        self.at[name] -= 1
        return k

    def parity(self, name, slots):
        return self.at.get(name, 0) % slots

    def rounds(self, engine, count, body):
        start = dict(self.at)
        self.first = True
        body(0)
        self.first = False
        rates = {n: k - start.get(n, 0) for n, k in self.at.items()}
        start = dict(self.at)
        if count == 1:
            return
        with engine.Fori(1, count) as i:
            self.loop = (i, 1, start, rates)
            body(i)
            self.loop = None
        for n, k in start.items():
            assert self.at[n] - k == rates[n]
            self.at[n] = k + rates[n] * (count - 1)


def shape_constants():
    t = np.arange(P)
    nf = HD // 4
    inv = (np.float32(10000.0) ** (-np.arange(nf, dtype=np.float32) / np.float32(nf))).astype(np.float32)
    pos = np.stack([t // GRID_W, t % GRID_W], -1).astype(np.float32)
    ang = (pos[:, :, None] * inv).astype(np.float32)
    rope = np.concatenate([np.cos(ang).reshape(P, 2 * nf), np.sin(ang).reshape(P, 2 * nf)], 1).astype(np.float32)
    w = 2 * np.pi * ((t[:, None] * t[None, :]) % P) / P
    fourier = np.concatenate([np.cos(w), np.sin(w)], 1).astype(np.float32)
    ident = np.eye(P, dtype=np.float32)
    back = t // GRID_W * GRID_W + GRID_W - 1 - t % GRID_W
    mirror = ident[back]
    qc = t % GRID_W
    cs = np.clip(qc - NA_COLS // 2, 0, GRID_W - NA_COLS)
    ok = (qc[None, :] >= cs[:, None]) & (qc[None, :] < cs[:, None] + NA_COLS)
    mask = np.where(ok, 0.0, -1e30).astype(np.float32)[back]
    pick = np.zeros((P, 4, P), np.float32)
    for b in range(4):
        pick[b, b] = pick[32 + b, b] = 1.0
    fold = np.zeros((P, 2), np.float32)
    for w in range(2):
        fold[w::32, w] = 1.0
    which = np.tile(np.arange(16, dtype=np.float32), (P, 1))
    group = np.tile(np.arange(16, dtype=np.float32) // 4, (P, 1))
    parts = {"ident": ident, "rope": rope, "fourier": fourier, "mirror": mirror, "mask": mask,
             "which": which, "group": group, "fold": fold}
    places, at = {}, 0
    for n, a in parts.items():
        places[n] = (at, a.shape[1])
        at += a.shape[1]
    return np.ascontiguousarray(np.concatenate(list(parts.values()), 1)), places, pick.reshape(P, 4 * P)


def trunk(nc, io, places):
    D = io["x_prompt"].shape[2]
    DEPTH = io["w_in"].shape[0]
    IN_W = io["w_in"].shape[2]
    NK = D // P
    NE = io["w_exp_gate"].shape[1]
    DE = io["w_exp_gate"].shape[3]
    NCH = D // COLS
    BR = io["w_branch"].shape[2]
    MODS = 6 * D // COLS
    UPC = NK // KB
    FIRST = 2 * D // COLS

    def mod_stage(l, stage):
        after = l + 1 < DEPTH
        a, b = {"fourier": (FIRST, FIRST + 2), "attention": (FIRST + 2, MODS - 2), "merge": (MODS - 2, MODS),
                "mixer rows": (0, 2), "norm": (2, FIRST - 2), "expert rows": (FIRST - 2, FIRST)}[stage]
        if stage in ("fourier", "attention", "merge"):
            return [(l, c) for c in range(a, b)]
        return [(l + 1, c) for c in range(a, b)] if after else []

    STAGES = ("fourier", "attention", "merge", "mixer rows", "norm", "expert rows")
    MOD_ORDER = [(0, c) for c in range(FIRST)] + [m for l in range(DEPTH) for s in STAGES for m in mod_stage(l, s)]
    A_H, B_H, C_H = 8, 4, 8
    AQ, AK, AV, BQ, BK, BV, CQ, CK, CV, FF = 0, 512, 640, 768, 1280, 1792, 2304, 2816, 3328, 3840
    IN_CHUNKS = IN_W // COLS
    IN_REST = IN_W - IN_CHUNKS * COLS
    LAYER_CHUNKS = IN_CHUNKS + 1 + 2 * 4 * NCH + NCH + NE + NCH
    LAM = [0.8 - 0.6 * math.exp(-0.3 * l) for l in range(DEPTH)]

    with ExitStack() as ctx:
        spot = [(nc.sbuf_base + 31) // 32 * 32]

        def place(name, shape, dtype=F32, at=None):
            size = 4 * int(np.prod(shape[1:]))
            where = spot[0] if at is None else at
            t = nc.alloc_sbuf_tensor_at(name, shape, dtype, offset=where)
            if at is None:
                spot[0] += (size + 31) // 32 * 32
            return t

        raw_w = place("raw_w", [P, RAW_SLOTS, KB, COLS])
        high_w = place("high_w", [P, SPLIT_SLOTS, KB, COLS], F32R)
        low_w = place("low_w", [P, SPLIT_SLOTS, KB, COLS], F32R)
        mod_w = place("mod_w", [P, MOD_SLOTS, KB, COLS], at=spot[0] - 4 * MOD_SLOTS * KB * COLS)
        x = place("x", [P, TILES, D])
        in_high = place("in_high", [P, NK, TILES, P], F32R)
        in_low = place("in_low", [P, NK, TILES, P], F32R)
        region = spot[0]
        br_high = place("br_high", [P, NK, TILES, P], F32R)
        br_low = place("br_low", [P, NK, TILES, P], F32R)
        proj = place("proj", [P, TILES, IN_W])
        mix = spot[0]
        merged = place("merged", [P, TILES, D])
        hid_high = place("hid_high", [P, NE * 2, TILES, P], F32R, at=region)
        hid_low = place("hid_low", [P, NE * 2, TILES, P], F32R, at=region + 4 * NE * 2 * TILES * P)
        gate_row = place("gate_row", [P, TILES, D], at=mix)
        normed = place("normed", [P, D], at=region + 4 * NE * 4 * TILES * P - 8192)
        router_raw = place("router_raw", [P, NK, 20], at=region + 32768)
        router_high = place("router_high", [P, NK, 20], F32R, at=region + 32768 + 80 * NK)
        router_low = place("router_low", [P, NK, 20], F32R, at=region + 32768 + 160 * NK)
        qk_t = place("qk_t", [P, 2, 12, P], at=mix)
        hankel = place("hankel", [P, C_H, P], at=mix + 8 * 12 * P)
        e_buf = place("e_buf", [P, 2, 1024])
        ones_at = spot[0] - 8192
        sig = place("sig", [P, TILES, COLS], at=spot[0] - 8192)
        prod = place("prod", [P, TILES, COLS], at=spot[0] - 4096)
        p_t = place("p_t", [P, 8, P])
        full = place("full", [P, 2, COLS], at=spot[0] - 4096)
        cache_bc = place("cache_bc", [P, 2, 512])
        bg_split = place("bg_split", [36, COLS], F32R, at=spot[0] - 4096)
        bg_raw = place("bg_raw", [36, COLS])
        lam_in = place("lam_in", [P, 4, HD], at=spot[0] - 2048)
        cache_a = place("cache_a", [P, 2, 128], at=spot[0] - 1024)
        mod_sums = place("mod_sums", [P, COLS])
        const = place("const", [P, places["fold"][0] + 2])
        pick = place("pick", [36, 4, P], F32R)
        mod = place("mod", [P, 2, MODS * 4, 2])
        gains = place("gains", [P, 2 * DEPTH, NK])
        scale_t = place("scale_t", [P, NK, TILES])
        cond = place("cond", [P, NK, 32])
        sub_g = place("sub_g", [P, DEPTH])
        sinks = place("sinks", [P, DEPTH, A_H])
        small = place("small", [P, 128])
        comb = place("comb", [P, TILES, 16])
        router_b = place("router_b", [P, DEPTH, 20])
        route = place("route", [P, TILES, 96], at=region + 32768 + 240 * NK)
        ones = place("ones", [P, P], at=ones_at)
        picked = place("picked", [P, TILES, 8])
        picked_at = place("picked_at", [P, TILES, 8], U32)
        assert spot[0] <= nc.sbuf_usable_end, spot[0] - nc.sbuf_usable_end

        sum_sq, rstd = small[:, 0:2], small[:, 2:4]
        lam_sum, lam_exp, lam = small[:, 4:6], small[:, 6:8], small[:, 8:9]
        top = small[:, 16:24]
        neg_top = small[:, 24:32]
        esum = small[:, 32:40]
        rsum = small[:, 40:48]
        esink = small[:, 48:56]
        sub_sq, sub_rstd = small[:, 56:60], small[:, 60:64]

        def constant(name):
            a, n = places[name]
            return const[:, a:a + n]

        ident, mirror, mask = constant("ident"), constant("mirror"), constant("mask")
        fourier = constant("fourier")
        fold = const[:, places["fold"][0]:places["fold"][0] + 2]

        banks = [ctx.enter_context(nc.psum_tensor(f"bank{i}", [P, 512], F32)) for i in range(8)]
        turn_banks, mod_bank = banks[5:7], banks[7]

        def sem(name):
            return ctx.enter_context(nc.semaphore(name))

        raw_in = [sem(f"raw_in{i}") for i in range(RAW_SLOTS)]
        high_ready, low_ready, unit_used = sem("high_ready"), sem("low_ready"), sem("unit_used")
        chunk_read, gate_ready = sem("chunk_read"), sem("gate_ready")
        mod_in = [sem(f"mod_in{i}") for i in range(MOD_SLOTS)]
        mod_used, mod_copied, mod_turned, mod_stored = sem("mod_used"), sem("mod_copied"), sem("mod_turned"), sem("mod_stored")
        hid_turned, hid_high_ready, hid_stored = sem("hid_turned"), sem("hid_high_ready"), sem("hid_stored")
        start_in, start_turned, cond_sig, cond_ready = sem("start_in"), sem("start_turned"), sem("cond_sig"), sem("cond_ready")
        pick_in, pick_ready, vectors_in = sem("pick_in"), sem("pick_ready"), sem("vectors_in")
        bg_in, bg_clear, bg_high, bg_ready = sem("bg_in"), sem("bg_clear"), sem("bg_high"), sem("bg_ready")
        squares, mean_ready, root_ready, normed_ready = sem("squares"), sem("mean_ready"), sem("root_ready"), sem("normed_ready")
        norm_turned, norm_full, norm_high, norm_low = sem("norm_turned"), sem("norm_full"), sem("norm_high"), sem("norm_low")
        roped = sem("roped")
        cache_a_in, cache_bc_in, hankel_in, lam_in_s, router_in = sem("cache_a_in"), sem("cache_bc_in"), sem("hankel_in"), sem("lam_in_s"), sem("router_in")
        lam_sum_ready, lam_exp_ready, lam_ready = sem("lam_sum_ready"), sem("lam_exp_ready"), sem("lam_ready")
        hankel_ready = sem("hankel_ready")
        f_first, f_copied, f_second, f_high, f_low = sem("f_first"), sem("f_copied"), sem("f_second"), sem("f_high"), sem("f_low")
        qk_turned, qk_ready = sem("qk_turned"), sem("qk_ready")
        scored, top_ready, exp_ready, weights_ready = sem("scored"), sem("top_ready"), sem("exp_ready"), sem("weights_ready")
        p_turned, p_ready, pv_done, out_high, out_low = sem("p_turned"), sem("p_ready"), sem("pv_done"), sem("out_high"), sem("out_low")
        sub_squares, sub_mean, sub_root, sub_ready, sub_turned = sem("sub_squares"), sem("sub_mean"), sem("sub_root"), sem("sub_ready"), sem("sub_turned")
        diag_ready, row_summed, row_ready = sem("diag_ready"), sem("row_summed"), sem("row_ready")
        merged_turned, merged_high, merged_low = sem("merged_turned"), sem("merged_high"), sem("merged_low")
        router_high_s, router_ready, routed, route_top, route_exp, comb_ready = (
            sem("router_high_s"), sem("router_ready"), sem("routed"), sem("route_top"), sem("route_exp"), sem("comb_ready"))
        final_in, final_scaled, out_stored, cache_stored = sem("final_in"), sem("final_scaled"), sem("out_stored"), sem("cache_stored")
        x_ready = sem("x_ready")

        def jobs():
            return [(b, t) for b in "ABC" for t in (SAMPLE, PROMPT)]

        def q_blocks(b):
            return 4

        def k_blocks(b):
            return 1 if b == "A" else 4

        def n_blocks(b, t):
            return q_blocks(b) + k_blocks(b) * (2 if t == SAMPLE else 1)

        def heads(b, g):
            if b == "A":
                return [(2 * g + r // 2, 0, r % 2, 2 * g + r // 2 + 4 * (r % 2)) for r in range(4)]
            if b == "B":
                return [(2 * g + r // 2, 2 * g + r // 2, r % 2, 2 * g + r // 2) for r in range(4)]
            return [(2 * g + r // 2, 2 * g + r // 2, r % 2, 4 * g + r) for r in range(4)]

        GROUPS = [(j, b, t, g) for j, (b, t) in enumerate(jobs()) for g in range(2)]
        NG = len(GROUPS)
        TURNS = [(n_blocks(b, t) + 3) // 4 for b, t in jobs()]

        def keys(t):
            return 2 if t == SAMPLE else 1

        def score_row(g, r, t):
            return banks[2 * (g % 2) + r % 2], r // 2 * P * keys(t)

        def value_cols(b, head):
            return (head // 4 * HD, HD) if b == "A" else ((head * P, P) if b == "B" else (head * HD, HD))

        V_AT = {"A": AV, "B": BV, "C": CV}
        BRANCH = {"A": 0, "B": 1, "C": 2, "F": 3}

        def weight_tile(w, l, col, width, block):
            return w[l, block * KB * P:(block + 1) * KB * P, col].rearrange("(k p) n -> p k n", p=P)

        block = ctx.enter_context(nc.Block())

        @block.sync
        def _(sp):
            at = Cursor()

            def load(src, width=COLS):
                slot = at.parity("unit", RAW_SLOTS)
                u = at.next("unit")
                need(sp, low_ready, u - RAW_SLOTS + 1)
                at.next(f"in{slot}")
                sp.dma_start(raw_w[:, slot, :, 0:width], src).then_inc(raw_in[slot], 16)

            def load_mod(l, c):
                for j in range(UPC):
                    slot = at.parity("mod_unit", MOD_SLOTS)
                    need(sp, mod_used, at.next("mod_unit") - MOD_SLOTS + 1)
                    sp.dma_start(mod_w[:, slot, :, :], weight_tile(io["w_mod"], l, bass.ds(c * COLS, COLS), COLS, j)
                                 ).then_inc(mod_in[slot], 16)

            def load_mods(chunks):
                need(sp, unit_used, at.done("unit") if chunks else 0)
                for l, c in chunks:
                    load_mod(l, c)

            sp.dma_start(const[:, :], io["const"]).then_inc(start_in, 16)
            sp.dma_start(normed[0:NK, 0:P], io["c_ctx"].rearrange("(k p) -> k p", p=P)).then_inc(start_in, 16)
            sp.dma_start(normed[NK:2 * NK, 0:P], io["c"].rearrange("a (k p) -> (a k) p", p=P)).then_inc(start_in, 16)
            for l in range(DEPTH):
                sp.dma_start(normed[0:MODS * 4, (1 + l) * P:(2 + l) * P],
                             io["b_mod"][l].rearrange("(k p) -> k p", p=P)).then_inc(start_in, 16)
            for l in range(DEPTH):
                for i, n in enumerate(("norm1_g", "norm2_g")):
                    r = (2 * l + i) * NK
                    sp.dma_start(normed[r:r + NK, 3 * P:4 * P],
                                 io[n][l].rearrange("(k p) -> k p", p=P)).then_inc(start_in, 16)
            sp.dma_start(x[:, PROMPT, :], io["x_prompt"][0]).then_inc(x_ready, 16)
            sp.dma_start(x[:, SAMPLE, :], io["x_sample"][0]).then_inc(x_ready, 16)

            def mod_start(c):
                load_mod(0, c)
            at.rounds(sp, FIRST, mod_start)
            sp.dma_start(proj[0:36, 0, 0:4 * P], io["pick"][0:36, :]).then_inc(pick_in, 16)
            for l in range(DEPTH):
                sp.dma_start(sub_g[:, l:l + 1], io["diff_sub_g"][l].rearrange("(p a) -> p a", a=1)).then_inc(vectors_in, 16)
                sp.dma_start(sinks[:, l, :], io["attn_sink"][l:l + 1, :].broadcast_to([P, A_H])).then_inc(vectors_in, 16)
                sp.dma_start(router_b[:, l, 0:4], io["b_router_group"][l:l + 1, :].broadcast_to([P, 4])).then_inc(vectors_in, 16)
                sp.dma_start(router_b[:, l, 4:20], io["b_router_expert"][l:l + 1, :].broadcast_to([P, 16])).then_inc(vectors_in, 16)

            for l in range(DEPTH):

                def w_in_pair(i):
                    for h in range(2):
                        for j in range(UPC):
                            load(weight_tile(io["w_in"], l, bass.ds((i * 2 + h) * COLS, COLS), COLS, j))
                at.rounds(sp, IN_CHUNKS // 2, w_in_pair)
                for j in range(UPC):
                    load(weight_tile(io["w_in"], l, slice(IN_CHUNKS * COLS, IN_W), IN_REST, j), IN_REST)
                if l:
                    sp.wait_ge(chunk_read, LAYER_CHUNKS * l)
                sp.dma_start(cache_a[:, 0, :], io["cache_attn_k"][0, l].rearrange("s h d -> s (h d)")).then_inc(cache_a_in, 16)
                sp.dma_start(cache_a[:, 1, :], io["cache_attn_v"][0, l].rearrange("s h d -> s (h d)")).then_inc(cache_a_in, 16)
                sp.dma_start(cache_bc[:, 0, :], io["cache_diff_k"][0, l].rearrange("s h m d -> s (h m d)")).then_inc(cache_bc_in, 16)
                sp.dma_start(cache_bc[:, 1, :], io["cache_diff_v"][0, l].rearrange("s h d -> s (h d)")).then_inc(cache_bc_in, 16)
                sp.dma_start(lam_in[:, :, :], io["diff_lambda"][l:l + 1].broadcast_to([P, 4, HD])).then_inc(lam_in_s, 16)
                rpb = io["na_rpb"]
                for qr in range(2):
                    for kr in range(2):
                        first = (l * C_H * (2 * NA_ROWS - 1) + NA_ROWS - 1 - qr + kr) * PAD_W
                        src = bass.AP(tensor=rpb.tensor, offset=first,
                                      ap=[[1, GRID_W], [(2 * NA_ROWS - 1) * PAD_W, C_H], [1, GRID_W]])
                        sp.dma_start(hankel[qr * GRID_W:(qr + 1) * GRID_W, :, kr * GRID_W:(kr + 1) * GRID_W],
                                     src).then_inc(hankel_in, 16)
                sp.wait_ge(chunk_read, LAYER_CHUNKS * l + IN_CHUNKS + 1)
                for name, a, n in (("new_attn_k", AK, 128), ("new_attn_v", AV, 128), ("new_diff_k", BK, 512),
                                   ("new_diff_v", BV, 512), ("new_na_k", CK, 512), ("new_na_v", CV, 512)):
                    dst = io[name][0, l]
                    dst = dst.rearrange("s h m d -> s (h m d)") if name == "new_diff_k" else dst.rearrange("s h d -> s (h d)")
                    sp.dma_start(dst, proj[:, PROMPT, a:a + n]).then_inc(cache_stored, 16)
                beside = mod_stage(l, "fourier") + mod_stage(l, "attention")
                load_mods(beside[:8])
                sp.wait_ge(pv_done, NG * l + 6)
                sp.dma_start(cache_bc[:, 0, :], io["cache_na_k"][0, l].rearrange("s h d -> s (h d)")).then_inc(cache_bc_in, 16)
                sp.dma_start(cache_bc[:, 1, :], io["cache_na_v"][0, l].rearrange("s h d -> s (h d)")).then_inc(cache_bc_in, 16)
                load_mods(beside[8:])

                def gates(n):
                    for b in range(4):
                        for j in range(UPC):
                            load(weight_tile(io["w_gate"], l, bass.ds(n * COLS + b * D, COLS), COLS, j))
                        if b == 0:
                            r = at.next("bg")
                            if at.first:
                                sp.wait_ge(bg_clear, l + 1)
                            need(sp, bg_ready, r)
                            for row in (0, 32):
                                sp.dma_start(bg_raw[row:row + 4, :],
                                             io["b_gate"][l].rearrange("(b n) -> b n", b=4)[:, bass.ds(n * COLS, COLS)]
                                             ).then_inc(bg_in, 16)
                        load(io["w_branch"][l, b, :, bass.ds(n * COLS, COLS)].rearrange("(k p) n -> p k n", p=P))
                at.rounds(sp, NCH, gates)

                sp.wait_ge(cache_stored, 16 * 6 * (l + 1))
                sp.dma_start(router_raw[:, :, 0:4], io["w_router_group"][l].rearrange("(k p) n -> p k n", p=P)).then_inc(router_in, 16)
                sp.dma_start(router_raw[:, :, 4:20], io["w_router_expert"][l].rearrange("(k p) n -> p k n", p=P)).then_inc(router_in, 16)

                load_mods(mod_stage(l, "merge") + mod_stage(l, "mixer rows"))

                def w_out(n):
                    for j in range(UPC):
                        load(weight_tile(io["w_out"], l, bass.ds(n * COLS, COLS), COLS, j))
                at.rounds(sp, NCH, w_out)
                load_mods(mod_stage(l, "norm") + mod_stage(l, "expert rows"))

                def experts(i):
                    for h in range(2):
                        for j in range(UPC):
                            slot = at.parity("unit", RAW_SLOTS)
                            u = at.next("unit")
                            need(sp, low_ready, u - RAW_SLOTS + 1)
                            for half, name in enumerate(("w_exp_gate", "w_exp_up")):
                                at.next(f"in{slot}")
                                src = io[name][l][bass.ds(i * 2 + h, 1), j * KB * P:(j + 1) * KB * P, :]
                                sp.dma_start(raw_w[:, slot, :, half * DE:(half + 1) * DE],
                                             src.rearrange("e (k p) f -> p (e k) f", p=P)).then_inc(raw_in[slot], 16)
                at.rounds(sp, NE // 2, experts)

                def down(n):
                    rows = io["w_exp_down"][l].rearrange("e (k p) n -> p (e k) n", p=P)
                    for j in range(NE * DE // P // KB):
                        load(rows[:, j * KB:(j + 1) * KB, bass.ds(n * COLS, COLS)])
                at.rounds(sp, NCH, down)

            sp.wait_ge(chunk_read, LAYER_CHUNKS * DEPTH)
            sp.dma_start(merged[:, 0, :], io["final_g"].rearrange("(a n) -> a n", a=1).broadcast_to([P, D])).then_inc(final_in, 16)
            for t, name in enumerate(("y_prompt", "y_sample")):
                sp.wait_ge(final_scaled, t + 1)
                sp.dma_start(io[name][0], x[:, t, :]).then_inc(out_stored, 16)
            sp.wait_ge(out_stored, 32)
            sp.wait_ge(cache_stored, 16 * 6 * DEPTH)

        @block.scalar
        def _(act):
            at = Cursor()

            def split_high(width=COLS, loads=1):
                slot, part = at.parity("unit", RAW_SLOTS), at.parity("unit", SPLIT_SLOTS)
                u = at.next("unit")
                for _ in range(loads):
                    k = at.next(f"in{slot}")
                act.wait_ge(raw_in[slot], k * 16 + 16)
                need(act, unit_used, u - SPLIT_SLOTS + 1)
                act.activation(high_w[:, part, :, 0:width], raw_w[:, slot, :, 0:width], ACT.Copy).then_inc(high_ready, 1)

            def mods_done(*stages):
                act.wait_ge(mod_used, mods_done.units)
            mods_done.units = UPC * FIRST

            def norm_scale(t_ready):
                for t in range(TILES):
                    act.activation(normed[:, :], x[:, t, :], ACT.Square, accum_out=sum_sq[:, t:t + 1]).then_inc(squares, 1)
                    act.drain()
                act.wait_ge(mean_ready, at.next("norm") + 1)
                act.activation(rstd, rstd, ACT.Sqrt).then_inc(root_ready, 1)

            def norm():
                norm_scale(None)
                for i in range(2 * KB):
                    t, g = i // KB, i % KB
                    act.wait_ge(norm_full, at.next("norm_group") + 1)
                    act.activation(in_high[:, g * KB:(g + 1) * KB, t, :],
                                   full[:, i % 2, :].rearrange("p (k n) -> p k n", n=P), ACT.Copy).then_inc(norm_high, 1)

            act.wait_ge(start_turned, 1)
            act.activation(sig[:, 0, 0:2 * NK], mod_bank[:, 0:2 * NK], ACT.Sigmoid).then_inc(cond_sig, 1)
            act.wait_ge(pick_in, 16)
            act.activation(pick[:, :, :], proj[0:36, 0, 0:4 * P].rearrange("p (b n) -> p b n", b=4), ACT.Copy).then_inc(pick_ready, 1)
            act.wait_ge(x_ready, 32)

            for l in range(DEPTH):
                if l:
                    act.wait_ge(chunk_read, LAYER_CHUNKS * l)
                norm()

                def copy_proj(col, width, after):
                    q = at.next("chunk")
                    act.wait_ge(unit_used, at.done("unit") - after)
                    for t in range(TILES):
                        dst, src = proj[:, t, bass.ds(col, width)], banks[copy_proj.pair * 2 + t][:, 0:width]
                        if isinstance(col, int) and col == AQ:
                            dst = dst.rearrange("p (h a d) -> p a h d", a=2, d=HD)
                            src = src.rearrange("p (a h d) -> p a h d", a=2, d=HD)
                        copied = act.activation(dst, src, ACT.Copy)
                        if t == 0:
                            continue
                        copied.then_inc(chunk_read, 1)

                at.at["chunk"] = at.at.get("chunk", 0) - 1
                mods_done()

                def w_in_pair(i):
                    for h in range(2):
                        split_high()
                        split_high()
                        if h or not at.first:
                            copy_proj.pair = (l * LAYER_CHUNKS + h + 1) % 2
                            copy_proj((i * 2 + h - 1) * COLS, COLS, 2)
                        else:
                            at.next("chunk")
                        split_high()
                        split_high()
                at.rounds(act, IN_CHUNKS // 2, w_in_pair)
                split_high(IN_REST)
                split_high(IN_REST)
                copy_proj.pair = (l * LAYER_CHUNKS + 1) % 2
                copy_proj((IN_CHUNKS - 1) * COLS, COLS, 2)
                split_high(IN_REST)
                split_high(IN_REST)
                copy_proj.pair = l * LAYER_CHUNKS % 2
                copy_proj(IN_CHUNKS * COLS, IN_REST, 0)

                def out_copy(first, step, t, source, scale=1.0):
                    n = at.next("out")
                    dst = br_high[:, first:first + step * (source.shape[1] - 1) + 1:step, t, :]
                    act.activation(dst, source, ACT.Copy, scale=scale).then_inc(out_high, 1)

                for t in (SAMPLE, PROMPT):
                    n = at.next("fourier")
                    act.wait_ge(f_first, n + 1)
                    for g in range(2):
                        for part, scale in ((0, 1.0 / P), (1, -1.0 / P)):
                            src = banks[g][:, :].rearrange("p (g c n) -> p g c n", g=2, c=2)[:, :, part, :]
                            dst = e_buf[:, t, g * 512:(g + 1) * 512].rearrange("p (g c n) -> p g c n", g=2, c=2)[:, :, part, :]
                            copied = act.activation(dst, src, ACT.Copy, scale=scale)
                    copied.then_inc(f_copied, 1)
                    act.wait_ge(f_second, n + 1)
                    out_copy(4 * BRANCH["F"], 1, t, banks[4][:, :].rearrange("p (g n) -> p g n", n=P))

                act.wait_ge(lam_sum_ready, l + 1)
                act.activation(lam_exp, lam_sum, ACT.Exp).then_inc(lam_exp_ready, 1)

                def copy_qk(j):
                    b, t = jobs()[j]
                    if j >= 2:
                        act.wait_ge(scored, NG * l + 2 * (j - 1))
                    for i in range(TURNS[j]):
                        n = min(4, n_blocks(b, t) - 4 * i)
                        act.wait_ge(qk_turned, at.next("qk") + 1)
                        act.activation(qk_t[:, j % 2, 4 * i:4 * i + n, :],
                                       turn_banks[i % 2][:, 0:n * P].rearrange("p (k n) -> p k n", n=P), ACT.Copy,
                                       scale=HD ** -0.5 if i == 0 else 1.0).then_inc(qk_ready, 1)

                def exps(G):
                    j, b, t, g = GROUPS[G]
                    act.wait_ge(top_ready, NG * l + G + 1)
                    if G >= 2:
                        act.wait_ge(p_turned, NG * l + G - 1)
                    w = P * keys(t)
                    if b == "A":
                        act.activation(esink[:, 4 * (G % 2):4 * (G % 2) + 4], esink[:, 4 * (G % 2):4 * (G % 2) + 4], ACT.Exp)
                    for r in range(4):
                        bank, c = score_row(G, r, t)
                        k = 4 * (G % 2) + r
                        done = act.activation(e_buf[:, G % 2, r * w:(r + 1) * w], bank[:, c:c + w], ACT.Exp,
                                              bias=neg_top[:, k:k + 1], accum_out=esum[:, k:k + 1])
                    done.then_inc(exp_ready, 1)

                def copy_p(G):
                    j, b, t, g = GROUPS[G]
                    n = (2 if b == "B" else 4) * keys(t)
                    act.wait_ge(p_turned, NG * l + G + 1)
                    need(act, pv_done, NG * l + G)
                    for h in range((n + 3) // 4):
                        m = min(4, n - 4 * h)
                        copied = act.activation(p_t[:, 4 * h:4 * h + m, :],
                                                turn_banks[h][:, 0:m * P].rearrange("p (k n) -> p k n", n=P), ACT.Copy)
                    copied.then_inc(p_ready, 1)

                copy_qk(0)
                exps(0)
                for G, (j, b, t, g) in enumerate(GROUPS):
                    if G + 1 < NG:
                        exps(G + 1)
                    copy_p(G)
                    if b != "B":
                        act.wait_ge(pv_done, NG * l + G + 1)
                        first, step = (g, 2) if b == "A" else (8 + 2 * g, 1)
                        out_copy(first, step, t, banks[4][:, 0:2 * P].rearrange("p (k n) -> p k n", n=P))
                    elif g == 1:
                        n = at.next("sub")
                        act.wait_ge(pv_done, NG * l + G + 1)
                        out_b = e_buf[:, G % 2, 0:512]
                        for h in range(B_H):
                            done = act.activation(out_b[:, h * P:(h + 1) * P], banks[4][:, h * P:(h + 1) * P], ACT.Square,
                                                  accum_out=sub_sq[:, h:h + 1])
                        done.then_inc(sub_squares, 1)
                        act.wait_ge(sub_mean, n + 1)
                        act.activation(sub_rstd, sub_rstd, ACT.Sqrt).then_inc(sub_root, 1)
                        act.wait_ge(sub_turned, n + 1)
                        out_copy(4, 1, t, banks[4][:, :].rearrange("p (k n) -> p k n", n=P), scale=sub_g[:, l:l + 1])
                    if g == 0 and j + 1 < len(jobs()):
                        copy_qk(j + 1)

                def gate_pair(b):
                    return (l * LAYER_CHUNKS + IN_CHUNKS + 1 + 2 * b) % 2

                def sigmoids(b, after, done_s, width=COLS):
                    act.wait_ge(unit_used, at.done("unit") - after)
                    need(act, chunk_read, at.done("chunk") - 1)
                    for t in range(TILES):
                        done = act.activation(sig[:, t, 0:width], banks[2 * b + t][:, 0:width], ACT.Sigmoid)
                    done.then_inc(done_s, 1)

                mods_done.units += UPC * len(mod_stage(l, "fourier") + mod_stage(l, "attention"))
                mods_done()

                def gates(n):
                    for b in range(4):
                        for j in range(UPC):
                            if b == 0 and j == 2:
                                r = at.next("bg")
                                act.wait_ge(bg_in, r * 32 + 32)
                                need(act, unit_used, at.done("unit") - 3)
                                act.activation(bg_split[:, :], bg_raw[:, :], ACT.Copy).then_inc(bg_high, 1)
                            split_high()
                        at.next("chunk")
                        split_high()
                        sigmoids(gate_pair(b), 1, chunk_read)
                        at.next("chunk")
                at.rounds(act, NCH, gates)

                for i in range(2 * KB):
                    t, g = i // KB, i % KB
                    act.wait_ge(merged_turned, at.next("merged") + 1)
                    act.activation(in_high[:, g * KB:(g + 1) * KB, t, :],
                                   turn_banks[i % 2][:, :].rearrange("p (k n) -> p k n", n=P), ACT.Copy).then_inc(merged_high, 1)

                def gate_rows():
                    for i in range(2 * KB):
                        t, g = i // KB, i % KB
                        act.wait_ge(row_summed, at.next("row") + 1)
                        act.activation(gate_row[:, t, g * COLS:(g + 1) * COLS], turn_banks[i % 2][:, :], ACT.Copy).then_inc(row_ready, 1)
                gate_rows()
                mods_done.units += UPC * len(mod_stage(l, "merge") + mod_stage(l, "mixer rows"))
                mods_done()

                def w_out(n):
                    for j in range(UPC):
                        split_high()
                    at.next("chunk")
                at.rounds(act, NCH, w_out)

                act.wait_ge(chunk_read, at.done("chunk"))
                norm()
                act.wait_ge(router_in, 32 * (l + 1))
                act.activation(router_high[:, :, :], router_raw[:, :, :], ACT.Copy).then_inc(router_high_s, 1)
                gate_rows()
                act.wait_ge(route_top, 2 * l + 1)
                for t in range(TILES):
                    done = act.activation(route[:, t, 64:68], route[:, t, 0:4], ACT.Exp, bias=route[:, t, 41:42],
                                          accum_out=route[:, t, 42:43])
                done.then_inc(route_exp, 1)
                act.wait_ge(route_top, 2 * l + 2)
                act.activation(route[:, :, 43:44], route[:, :, 43:44], ACT.Exp).then_inc(route_exp, 1)

                mods_done.units += UPC * len(mod_stage(l, "norm") + mod_stage(l, "expert rows"))
                mods_done()

                def hid_copy(e):
                    act.wait_ge(hid_turned, at.next("hid") + 1)
                    act.activation(hid_high[:, :, :, :].rearrange("p k t n -> p (k t n)")[:, bass.ds(e * 512, 512)],
                                   turn_banks[hid_copy.bank][:, :], ACT.Copy).then_inc(hid_high_ready, 1)

                def experts(i):
                    for h in range(2):
                        split_high(loads=2)
                        split_high(loads=2)
                        later = h or not at.first
                        if later:
                            sigmoids((l * LAYER_CHUNKS + LAYER_CHUNKS - NCH + h + 1) % 2, 2, gate_ready, DE)
                        split_high(loads=2)
                        split_high(loads=2)
                        hid_copy.bank = (h + 1) % 2
                        if later:
                            hid_copy(i * 2 + (h - 1))
                        else:
                            at.next("hid")
                        at.next("chunk")
                at.at["hid"] = at.at.get("hid", 0) - 1
                at.rounds(act, NE // 2, experts)
                sigmoids((l * LAYER_CHUNKS + LAYER_CHUNKS - NCH + 1) % 2, 0, gate_ready, DE)
                hid_copy.bank = 1
                hid_copy(NE - 1)

                def down(n):
                    for j in range(NE * DE // P // KB):
                        split_high()
                    at.next("chunk")
                at.rounds(act, NCH, down)

            act.wait_ge(chunk_read, LAYER_CHUNKS * DEPTH)
            norm_scale(None)

        @block.vector
        def _(dve):
            at = Cursor()

            def split_low(width=COLS):
                slot, part = at.parity("unit", RAW_SLOTS), at.parity("unit", SPLIT_SLOTS)
                u = at.next("unit")
                dve.wait_ge(high_ready, u + 1)
                dve.tensor_tensor(low_w[:, part, :, 0:width], raw_w[:, slot, :, 0:width],
                                  high_w[:, part, :, 0:width].bitcast(F32), ALU.subtract).then_inc(low_ready, 1)

            def mod_copy():
                m = at.next("mod_copy")
                dve.wait_ge(mod_used, m * UPC + UPC)
                need(dve, mod_turned, m)
                dve.tensor_copy(mod_sums[:, :], mod_bank[:, :]).then_inc(mod_copied, 1)

            def mod_store(layer, c):
                m = at.next("mod_store")
                dve.wait_ge(mod_turned, m + 1)
                own = mod[:, layer, bass.ds(c * 4, 4), :]
                dve.tensor_tensor(own, own, mod_bank[:, 0:8].rearrange("p (k w) -> p k w", w=2), ALU.add).then_inc(mod_stored, 1)

            def mod_step(units):
                if at.done("mod_store") < at.done("mod_copy"):
                    mod_store(*MOD_ORDER[at.done("mod_store")])
                at.at["mod_unit"] = at.done("mod_unit") + units
                if at.done("mod_unit") // UPC > at.done("mod_copy"):
                    mod_copy()

            def mean_scale(count):
                n = at.next("norm")
                dve.wait_ge(squares, 2 * n + 2)
                dve.tensor_scalar(sum_sq, sum_sq, 1.0 / D, EPS, ALU.mult, ALU.add)
                dve.drain()
                dve.reciprocal(rstd, sum_sq).then_inc(mean_ready, 1)
                dve.wait_ge(root_ready, n + 1)

            def norm(l, which, mod_units=0):
                shift, scale, gain = 48 * which, 48 * which + 16, 2 * l + which
                dve.drain()
                dve.scalar_tensor_tensor(scale_t[:, :, :], mod[:, l, scale:scale + NK, :], 1.0,
                                         gains[:, gain, :].unsqueeze(2).broadcast_to([P, NK, 2]), ALU.add, ALU.mult)
                mean_scale(D)

                def low(i):
                    t, g = i // KB, i % KB
                    dve.wait_ge(norm_high, at.next("norm_low") + 1)
                    dst = slice(g * KB, (g + 1) * KB)
                    dve.tensor_tensor(in_low[:, dst, t, :], full[:, i % 2, :].rearrange("p (k n) -> p k n", n=P),
                                      in_high[:, dst, t, :].bitcast(F32), ALU.subtract).then_inc(norm_low, 1)

                for i in range(2 * KB):
                    t, g = i // KB, i % KB
                    n = at.next("norm_group")
                    if g == 0:
                        need(dve, norm_turned, n)
                        dve.tensor_scalar(normed[:, :], x[:, t, :], rstd[:, t:t + 1], None, ALU.mult).then_inc(normed_ready, 1)
                    dve.wait_ge(norm_turned, n + 1)
                    dve.drain()
                    for k in range(KB):
                        kk = g * KB + k
                        done = dve.tensor_scalar(full[:, i % 2, k * P:(k + 1) * P], turn_banks[i % 2][:, k * P:(k + 1) * P],
                                                 scale_t[:, kk, t:t + 1], mod[:, l, shift + kk, t:t + 1], ALU.mult, ALU.add)
                    done.then_inc(norm_full, 1)
                    if i:
                        low(i - 1)
                    mod_step(mod_units)
                dve.wait_ge(norm_high, n + 1)
                low(2 * KB - 1)

            dve.wait_ge(cond_sig, 1)
            dve.memset(cond[:, :, :], 0.0)
            dve.drain()
            dve.tensor_copy(mod[:, :, :, :].rearrange("p l k w -> p (l k) w"),
                            mod_bank[:, 32:32 + DEPTH * MODS * 4].unsqueeze(2).broadcast_to([P, DEPTH * MODS * 4, 2]))
            dve.tensor_copy(gains[:, :, :].rearrange("p l k -> p (l k)"), mod_bank[:, 224:224 + 4 * NK])
            dve.tensor_tensor(cond[:, :, 0:2].rearrange("p k w -> p w k"),
                              mod_bank[:, 0:2 * NK].rearrange("p (w k) -> p w k", w=2),
                              sig[:, 0, 0:2 * NK].rearrange("p (w k) -> p w k", w=2), ALU.mult).then_inc(cond_ready, 1)

            def mod_start(c):
                mod_copy()
                mod_store(0, c)
            at.rounds(dve, FIRST, mod_start)
            at.at["mod_unit"] = UPC * FIRST
            dve.wait_ge(vectors_in, 16 * 4 * DEPTH)
            for l in range(DEPTH):
                dve.tensor_scalar(sub_g[:, l:l + 1], sub_g[:, l:l + 1], 1.0 - LAM[l], None, ALU.mult)

            for l in range(DEPTH):
                norm(l, 0)

                def w_in_pair(i):
                    for j in range(2 * UPC):
                        split_low()
                    at.next("chunk")
                    at.next("chunk")
                at.rounds(dve, IN_CHUNKS // 2, w_in_pair)
                for j in range(UPC):
                    split_low(IN_REST)
                at.next("chunk")

                dve.wait_ge(chunk_read, LAYER_CHUNKS * l + IN_CHUNKS + 1)
                cos, sin = (constant("rope")[:, i * 32:(i + 1) * 32].rearrange("p (x f) -> p x f", x=2) for i in range(2))
                for a, n in ((AQ, 10), (BQ, 16)):
                    pair = proj[:, SAMPLE, a:a + n * HD].rearrange("p (h x y f) -> p h x y f", x=2, y=2, f=HD // 4)
                    one, two = pair[:, :, :, 0, :], pair[:, :, :, 1, :]
                    c, s = (v.unsqueeze(1).broadcast_to([P, n, 2, HD // 4]) for v in (cos, sin))
                    flat = p_t[:, :, :].rearrange("p k n -> p (k n)")
                    u, v = (flat[:, i * 512:i * 512 + n * 32].rearrange("p (h x f) -> p h x f", x=2, f=HD // 4) for i in range(2))
                    dve.tensor_tensor(u, one, s, ALU.mult)
                    dve.tensor_tensor(v, two, s, ALU.mult)
                    dve.drain()
                    dve.tensor_tensor(one, one, c, ALU.mult)
                    dve.tensor_tensor(two, two, c, ALU.mult)
                    dve.drain()
                    dve.tensor_tensor(one, one, v, ALU.subtract)
                    dve.tensor_tensor(two, two, u, ALU.add).then_inc(roped, 1)
                    dve.drain()

                dve.wait_ge(lam_in_s, 16 * (l + 1))
                quad = lam_in[:, :, :].rearrange("p (a b) n -> p a b n", b=2)
                dve.tensor_tensor(quad[:, :, 0, :], quad[:, :, 0, :], quad[:, :, 1, :], ALU.mult)
                dve.drain()
                dve.tensor_reduce(lam_sum, quad[:, :, 0, :], AX.X, ALU.add).then_inc(lam_sum_ready, 1)
                dve.wait_ge(hankel_in, 64 * (l + 1))
                dve.tensor_tensor(hankel[:, :, :], hankel[:, :, :], mask.unsqueeze(1).broadcast_to([P, C_H, P]), ALU.add).then_inc(hankel_ready, 1)

                def out_rest(first, step, t, source, scale=None):
                    n = at.next("out")
                    dve.wait_ge(out_high, n + 1)
                    s = slice(first, first + step * (source.shape[1] - 1) + 1, step)
                    if scale is None:
                        done = dve.tensor_tensor(br_low[:, s, t, :], source, br_high[:, s, t, :].bitcast(F32), ALU.subtract)
                    else:
                        done = dve.scalar_tensor_tensor(br_low[:, s, t, :], source, scale, br_high[:, s, t, :].bitcast(F32),
                                                        ALU.mult, ALU.subtract)
                    done.then_inc(out_low, 1)

                for t in (SAMPLE, PROMPT):
                    mod_step(UPC)
                    out_rest(4 * BRANCH["F"], 1, t, banks[4][:, :].rearrange("p (g n) -> p g n", n=P))
                mod_step(0)
                dve.wait_ge(lam_exp_ready, l + 1)
                dve.tensor_tensor(lam, lam_exp[:, 0:1], lam_exp[:, 1:2], ALU.subtract)
                dve.drain()
                dve.tensor_scalar(lam, lam, LAM[l], None, ALU.add)

                def tops(G):
                    j, b, t, g = GROUPS[G]
                    w, k = P * keys(t), 4 * (G % 2)
                    dve.wait_ge(scored, NG * l + G + 1)
                    for h in range(2):
                        bank, _ = score_row(G, h, t)
                        dve.tensor_reduce(top[:, k + h:k + 4:2], bank[:, 0:2 * w].rearrange("p (r n) -> p r n", n=w), AX.X, ALU.max)
                    dve.drain()
                    if b == "A":
                        sink = sinks[:, l, :].rearrange("p (a h) -> p h a", a=2)[:, 2 * g:2 * g + 2, :]
                        v = top[:, k:k + 4].rearrange("p (h a) -> p h a", a=2)
                        dve.tensor_tensor(v, v, sink, ALU.max)
                        dve.drain()
                        dve.tensor_tensor(esink[:, k:k + 4].rearrange("p (h a) -> p h a", a=2), sink, v, ALU.subtract)
                    dve.tensor_scalar(neg_top[:, k:k + 4], top[:, k:k + 4], -1.0, None, ALU.mult).then_inc(top_ready, 1)

                def weights(G):
                    j, b, t, g = GROUPS[G]
                    w, k = P * keys(t), 4 * (G % 2)
                    dve.wait_ge(exp_ready, NG * l + G + 1)
                    if b == "A":
                        dve.tensor_tensor(esum[:, k:k + 4], esum[:, k:k + 4], esink[:, k:k + 4], ALU.add)
                        dve.drain()
                    dve.reciprocal(rsum[:, k:k + 4], esum[:, k:k + 4])
                    dve.drain()
                    e = e_buf[:, G % 2, 0:4 * w].rearrange("p (r n) -> p r n", n=w)
                    if b == "B":
                        odd = rsum[:, k + 1:k + 4:2]
                        dve.tensor_scalar(odd, odd, lam, None, ALU.mult)
                        dve.drain()
                        for h in range(2):
                            dve.tensor_scalar(e[:, 2 * h + 1, :], e[:, 2 * h + 1, :], rsum[:, k + 2 * h + 1:k + 2 * h + 2], None, ALU.mult)
                        dve.drain()
                        for h in range(2):
                            done = dve.scalar_tensor_tensor(e[:, 2 * h, :], e[:, 2 * h, :], rsum[:, k + 2 * h:k + 2 * h + 1],
                                                            e[:, 2 * h + 1, :], ALU.mult, ALU.subtract)
                    else:
                        done = dve.tensor_tensor(e, e, rsum[:, k:k + 4].unsqueeze(2).broadcast_to([P, 4, w]), ALU.mult)
                    done.then_inc(weights_ready, 1)

                tops(0)
                for G, (j, b, t, g) in enumerate(GROUPS):
                    weights(G)
                    if G + 1 < NG:
                        tops(G + 1)
                    mod_step(UPC)
                    if b != "B":
                        first, step = (g, 2) if b == "A" else (8 + 2 * g, 1)
                        out_rest(first, step, t, banks[4][:, 0:2 * P].rearrange("p (k n) -> p k n", n=P))
                    elif g == 1:
                        n = at.next("sub")
                        dve.wait_ge(sub_squares, n + 1)
                        dve.tensor_scalar(sub_sq, sub_sq, 1.0 / P, EPS, ALU.mult, ALU.add)
                        dve.drain()
                        dve.reciprocal(sub_rstd, sub_sq).then_inc(sub_mean, 1)
                        dve.wait_ge(sub_root, n + 1)
                        dve.tensor_tensor(e_buf[:, G % 2, 0:512].rearrange("p (h n) -> p h n", n=P),
                                          banks[4][:, :].rearrange("p (h n) -> p h n", n=P),
                                          sub_rstd.unsqueeze(2).broadcast_to([P, B_H, P]), ALU.mult).then_inc(sub_ready, 1)
                        out_rest(4, 1, t, banks[4][:, :].rearrange("p (k n) -> p k n", n=P), scale=sub_g[:, l:l + 1])
                    mod_step(0)

                def merge(pair, b, n, after):
                    m = at.next(f"merge{l}")
                    dve.drain()
                    dve.wait_ge(chunk_read, m * 2 + (LAYER_CHUNKS * l + IN_CHUNKS + 2))
                    dve.wait_ge(unit_used, at.done("unit") - after)
                    cols = bass.ds(n * COLS, COLS)
                    for t in range(TILES):
                        dst = merged[:, t, cols] if b == 0 else prod[:, t, :]
                        done = dve.tensor_tensor(dst, banks[2 * pair + t][:, :], sig[:, t, :], ALU.mult)
                    if b:
                        dve.drain()
                        done = dve.tensor_tensor(merged[:, :, cols], merged[:, :, cols], prod[:, :, :], ALU.add)
                    done.then_inc(chunk_read, 1)

                def proj_pair(b):
                    return (l * LAYER_CHUNKS + IN_CHUNKS + 2 + 2 * b) % 2

                dve.memset(bg_raw[:, :], 0.0).then_inc(bg_clear, 1)

                def gates(n):
                    r = at.next("bg")
                    for b in range(4):
                        later = b or not at.first
                        split_low()
                        split_low()
                        if b == 0:
                            dve.wait_ge(bg_high, r + 1)
                            dve.tensor_tensor(bg_split[32:36, :], bg_raw[32:36, :], bg_split[32:36, :].bitcast(F32), ALU.subtract).then_inc(bg_ready, 1)
                        if later:
                            merge(proj_pair((b + 3) % 4), (b + 3) % 4, n if b else n - 1, 2)
                        else:
                            at.next(f"merge{l}")
                        split_low()
                        split_low()
                        split_low()
                at.at[f"merge{l}"] = -1
                at.rounds(dve, NCH, gates)
                merge(proj_pair(3), 3, NCH - 1, 0)

                for i in range(2 * KB):
                    t, g = i // KB, i % KB
                    dve.wait_ge(merged_high, at.next("merged") + 1)
                    s = slice(g * KB, (g + 1) * KB)
                    dve.tensor_tensor(in_low[:, s, t, :], turn_banks[i % 2][:, :].rearrange("p (k n) -> p k n", n=P),
                                      in_high[:, s, t, :].bitcast(F32), ALU.subtract).then_inc(merged_low, 1)
                    mod_step(len(mod_stage(l, "merge")) * UPC // (2 * KB))

                def gate_rows(first, mod_units):
                    dve.memset(ones[:, :], 1.0)
                    dve.drain()
                    for i in range(2 * KB):
                        t, g = i // KB, i % KB
                        n = at.next("row")
                        need(dve, row_summed, n - 1)
                        for k in range(KB):
                            done = dve.tensor_scalar(full[:, i % 2, k * P:(k + 1) * P], ident,
                                                     mod[:, l, first + g * KB + k, t:t + 1], None, ALU.mult)
                        done.then_inc(diag_ready, 1)
                        mod_step(mod_units)
                    mod_step(0)
                gate_rows(32, len(mod_stage(l, "mixer rows")) * UPC // (2 * KB))

                def add_to_x(pair, n, after):
                    dve.drain()
                    dve.wait_ge(unit_used, at.done("unit") - after)
                    cols = bass.ds(n * COLS, COLS)
                    for t in range(TILES):
                        dve.tensor_tensor(prod[:, t, :], banks[2 * pair + t][:, :], gate_row[:, t, cols], ALU.mult)
                    dve.drain()
                    dve.tensor_tensor(x[:, :, cols], x[:, :, cols], prod[:, :, :], ALU.add).then_inc(chunk_read, 1)

                def w_out_pair(i):
                    for h in range(2):
                        split_low()
                        split_low()
                        if h or not at.first:
                            add_to_x((l * LAYER_CHUNKS + LAYER_CHUNKS - NE - 2 * NCH + h + 1) % 2, i * 2 + (h - 1), 2)
                        split_low()
                        split_low()
                dve.wait_ge(row_ready, at.done("row"))
                at.rounds(dve, NCH // 2, w_out_pair)
                add_to_x((l * LAYER_CHUNKS + LAYER_CHUNKS - NE - 2 * NCH + 1) % 2, NCH - 1, 0)

                norm(l, 1, len(mod_stage(l, "norm")) * UPC // (2 * KB))
                dve.wait_ge(router_high_s, l + 1)
                dve.tensor_tensor(router_low[:, :, :], router_raw[:, :, :], router_high[:, :, :].bitcast(F32), ALU.subtract).then_inc(router_ready, 1)
                gate_rows(80, len(mod_stage(l, "expert rows")) * UPC // (2 * KB))

                dve.memset(route[:, :, 0:8], -3e38)
                dve.drain()
                dve.wait_ge(routed, l + 1)
                logits = banks[4][:, 0:64].rearrange("p (t n) -> p t n", t=2)
                for a, n, c in ((0, 4, 0), (8, 16, 4)):
                    dve.tensor_tensor(route[:, :, a:a + n], logits[:, :, c:c + n],
                                      router_b[:, l, c:c + n].unsqueeze(1).broadcast_to([P, 2, n]), ALU.add)
                dve.drain()

                def best(cols):
                    for t in range(TILES):
                        dve.max(picked[:, t, :], route[:, t, cols])
                    dve.drain()
                    for t in range(TILES):
                        dve.max_index(picked_at[:, t, :], picked[:, t, :], route[:, t, cols])
                    dve.drain()
                best(slice(0, 8))
                dve.tensor_copy(route[:, :, 40:41], picked_at[:, :, 0:1])
                dve.tensor_scalar(route[:, :, 41:42], picked[:, :, 0:1], -1.0, None, ALU.mult).then_inc(route_top, 1)
                dve.drain()
                for t in range(TILES):
                    dve.tensor_scalar(route[:, t, 24:40], constant("group"), route[:, t, 40:41], None, ALU.is_equal)
                dve.drain()
                dve.tensor_scalar(route[:, :, 48:64], route[:, :, 24:40], 1e30, -1e30, ALU.mult, ALU.add)
                dve.tensor_tensor(route[:, :, 24:40], route[:, :, 24:40], route[:, :, 8:24], ALU.mult)
                dve.drain()
                dve.tensor_tensor(route[:, :, 24:40], route[:, :, 24:40], route[:, :, 48:64], ALU.add)
                dve.drain()
                best(slice(24, 40))
                dve.tensor_tensor(route[:, :, 43:44], picked[:, :, 1:2], picked[:, :, 0:1], ALU.subtract).then_inc(route_top, 1)
                dve.tensor_copy(route[:, :, 44:46], picked_at[:, :, 0:2])
                dve.wait_ge(route_exp, 2 * l + 2)
                dve.tensor_scalar(route[:, :, 46:47], route[:, :, 43:44], 1.0, None, ALU.add)
                dve.tensor_copy(route[:, :, 47:48], route[:, :, 42:43])
                dve.drain()
                dve.reciprocal(route[:, :, 46:48], route[:, :, 46:48])
                dve.drain()
                dve.tensor_tensor(route[:, :, 46:47], route[:, :, 46:47], route[:, :, 47:48], ALU.mult)
                dve.drain()
                dve.tensor_tensor(route[:, :, 47:48], route[:, :, 46:47], route[:, :, 43:44], ALU.mult)
                dve.drain()
                for t in range(TILES):
                    dve.tensor_scalar(comb[:, t, :], constant("which"), route[:, t, 44:45], route[:, t, 46:47], ALU.is_equal, ALU.mult)
                    dve.tensor_scalar(route[:, t, 48:64], constant("which"), route[:, t, 45:46], route[:, t, 47:48], ALU.is_equal, ALU.mult)
                dve.drain()
                dve.tensor_tensor(comb[:, :, :], comb[:, :, :], route[:, :, 48:64], ALU.add)
                dve.drain()

                def hidden(pair, e):
                    n = at.next("hidden")
                    dve.drain()
                    dve.wait_ge(gate_ready, n + 1)
                    need(dve, hid_turned, n)
                    for t in range(TILES):
                        dve.scalar_tensor_tensor(prod[:, t, 0:DE], banks[2 * pair + t][:, DE:2 * DE], comb[:, t, bass.ds(e, 1)],
                                                 sig[:, t, 0:DE], ALU.mult, ALU.mult)
                    dve.drain()
                    for t in range(TILES):
                        done = dve.tensor_tensor(prod[:, t, DE:2 * DE], banks[2 * pair + t][:, 0:DE], prod[:, t, 0:DE], ALU.mult)
                    done.then_inc(chunk_read, 1)

                def hid_rest(e, bank):
                    dve.wait_ge(hid_high_ready, at.next("hid") + 1)
                    cols = bass.ds(e * 512, 512)
                    dve.tensor_tensor(hid_low[:, :, :, :].rearrange("p k t n -> p (k t n)")[:, cols], turn_banks[bank][:, :],
                                      hid_high[:, :, :, :].rearrange("p k t n -> p (k t n)")[:, cols].bitcast(F32),
                                      ALU.subtract).then_inc(hid_stored, 1)

                first_pair = (l * LAYER_CHUNKS + LAYER_CHUNKS - NCH) % 2

                def experts(i):
                    for h in range(2):
                        later = h or not at.first
                        split_low()
                        split_low()
                        if later:
                            hidden((first_pair + h + 1) % 2, i * 2 + (h - 1))
                        else:
                            at.next("hidden")
                        split_low()
                        split_low()
                        if later:
                            hid_rest(i * 2 + (h - 1), (h + 1) % 2)
                        else:
                            at.next("hid")
                for name in ("hidden", "hid"):
                    at.at[name] = at.at.get(name, 0) - 1
                at.rounds(dve, NE // 2, experts)
                hidden((first_pair + 1) % 2, NE - 1)
                hid_rest(NE - 1, 1)

                def down_pair(i):
                    for h in range(2):
                        split_low()
                        split_low()
                        if h or not at.first:
                            add_to_x((first_pair + h + 1) % 2, i * 2 + (h - 1), 2)
                        for j in range(NE * DE // P // KB - 2):
                            split_low()
                dve.wait_ge(row_ready, at.done("row"))
                at.rounds(dve, NCH // 2, down_pair)
                add_to_x((first_pair + 1) % 2, NCH - 1, 0)

            mean_scale(D)
            dve.wait_ge(final_in, 16)
            for t in range(TILES):
                dve.scalar_tensor_tensor(x[:, t, :], x[:, t, :], rstd[:, t:t + 1], merged[:, 0, :], ALU.mult, ALU.mult).then_inc(final_scaled, 1)

        @block.tensor
        def _(pe):
            at = Cursor()

            def next_unit():
                part = at.parity("unit", SPLIT_SLOTS)
                pe.wait_ge(low_ready, at.next("unit") + 1)
                return part

            def chunk(highs, lows, first_block, blocks, width=COLS, bias=None):
                pair = at.parity("chunk", 2)
                need(pe, chunk_read, at.next("chunk") - 1)
                for j in range(blocks // KB):
                    part = next_unit()
                    for k in range(KB):
                        kk = first_block + j * KB + k
                        for t in range(TILES):
                            out = banks[2 * pair + t][:, 0:width]
                            start = j == 0 and k == 0
                            stop = j == blocks // KB - 1 and k == KB - 1
                            pe.matmul(out, highs[:, kk, t, :], high_w[:, part, k, 0:width], start=start, stop=False)
                            pe.matmul(out, highs[:, kk, t, :], low_w[:, part, k, 0:width], start=False, stop=False)
                            done = pe.matmul(out, lows[:, kk, t, :], high_w[:, part, k, 0:width], start=False, stop=stop)
                    done.then_inc(unit_used, 1)
                    if j == 2 and bias is not None:
                        bias(pair)

            def mod_units(units):
                for _ in range(units):
                    slot, j = at.parity("mod_unit", MOD_SLOTS), at.parity("mod_unit", UPC)
                    at.next("mod_unit")
                    if j == 0:
                        need(pe, mod_stored, at.next("mod_chunk"))
                    pe.wait_ge(mod_in[slot], at.next(f"mod_in{slot}") * 16 + 16)
                    for k in range(KB):
                        done = pe.matmul(mod_bank[32 * k:32 * k + 32, :], cond[:, j * KB + k, :], mod_w[:, slot, k, :],
                                         start=j == 0, stop=j == UPC - 1)
                    done.then_inc(mod_used, 1)

            def mod_turn():
                pe.wait_ge(mod_copied, at.next("mod_turn") + 1)
                for k in range(4):
                    done = pe.matmul(mod_bank[:, 2 * k:2 * k + 2], mod_sums[:, k * P:(k + 1) * P], fold, start=True, stop=True)
                done.then_inc(mod_turned, 1)

            def mod_step(units):
                if at.done("mod_unit") // UPC > at.done("mod_turn"):
                    mod_turn()
                mod_units(units)

            def turn(bank, col, src, width=P):
                return pe.transpose(bank[:, col:col + width], src, ident[0:src.shape[0], 0:src.shape[0]])

            def norm(mods=0):
                for i in range(2 * KB):
                    t, g = i // KB, i % KB
                    n = at.next("norm_group")
                    if g == 0:
                        pe.wait_ge(normed_ready, at.next("norm") + 1)
                    need(pe, norm_full, n - 1)
                    for k in range(KB):
                        done = turn(turn_banks[i % 2], k * P, normed[:, (g * KB + k) * P:(g * KB + k + 1) * P])
                    done.then_inc(norm_turned, 1)
                    mod_step(mods)
                pe.wait_ge(norm_low, at.done("norm_group"))

            def gate_rows(mods):
                for i in range(2 * KB):
                    n = at.next("row")
                    pe.wait_ge(diag_ready, n + 1)
                    need(pe, row_ready, n - 1)
                    pe.matmul(turn_banks[i % 2][:, :], ones[:, :], full[:, i % 2, :], start=True, stop=True).then_inc(row_summed, 1)
                    mod_step(mods)
                mod_step(0)

            pe.wait_ge(start_in, 16 * (3 + DEPTH + 2 * DEPTH))
            turn(mod_bank, 0, normed[0:2 * NK, 0:P], 2 * NK)
            for l in range(DEPTH):
                turn(mod_bank, 32 + l * MODS * 4, normed[0:MODS * 4, (1 + l) * P:(2 + l) * P], MODS * 4)
            turn(mod_bank, 224, normed[0:4 * NK, 3 * P:4 * P], 4 * NK).then_inc(start_turned, 1)
            pe.wait_ge(cond_ready, 1)

            def mod_start(c):
                mod_units(UPC)
                mod_turn()
            at.rounds(pe, FIRST, mod_start)
            pe.wait_ge(pick_ready, 1)

            for l in range(DEPTH):
                norm()

                def w_in_pair(i):
                    for h in range(2):
                        chunk(in_high, in_low, 0, NK)
                at.rounds(pe, IN_CHUNKS // 2, w_in_pair)
                chunk(in_high, in_low, 0, NK, IN_REST)
                pe.wait_ge(chunk_read, LAYER_CHUNKS * l + IN_CHUNKS + 1)

                for t in (SAMPLE, PROMPT):
                    n = at.next("fourier")
                    need(pe, f_copied, n)
                    for g in range(4):
                        done = pe.matmul(banks[g // 2][:, g % 2 * 256:g % 2 * 256 + 256],
                                         proj[:, t, FF + g * P:FF + (g + 1) * P], fourier, start=True, stop=True)
                    done.then_inc(f_first, 1)
                    mod_step(UPC)
                    pe.wait_ge(f_copied, n + 1)
                    need(pe, out_low, at.next("out"))
                    half = e_buf[:, t, :].rearrange("p (g c n) -> p g c n", g=4, c=2)
                    pe.matmul(banks[4][:, :], fourier[:, 0:P], half[:, :, 0, :], start=True, stop=False)
                    pe.matmul(banks[4][:, :], fourier[:, P:2 * P], half[:, :, 1, :], start=False, stop=True).then_inc(f_second, 1)

                def turn_qk(j):
                    b, t = jobs()[j]
                    row = proj[:, t, :]
                    if b == "A":
                        srcs = [row[:, AQ + i * P:AQ + (i + 1) * P] for i in range(5)]
                        cached = [cache_a[:, 0, :]]
                    else:
                        q, k = (BQ, BK) if b == "B" else (CQ, CK)
                        srcs = [row[:, a + i * P:a + (i + 1) * P] for a in (q, k) for i in range(4)]
                        cached = [cache_bc[:, 0, i * P:(i + 1) * P] for i in range(4)]
                    if t == SAMPLE:
                        srcs += cached
                        if b == "A":
                            pe.wait_ge(roped, 2 * l + 1)
                            pe.wait_ge(cache_a_in, 32 * (l + 1))
                        elif b == "B":
                            pe.wait_ge(roped, 2 * l + 2)
                            pe.wait_ge(cache_bc_in, 64 * l + 32)
                        else:
                            pe.wait_ge(cache_bc_in, 64 * l + 64)
                            pe.wait_ge(hankel_ready, l + 1)
                    for i in range(TURNS[j]):
                        need(pe, qk_ready, at.next("qk") - (i > 0))
                        for k, src in enumerate(srcs[4 * i:4 * i + 4]):
                            done = turn(turn_banks[i % 2], k * P, src)
                        done.then_inc(qk_turned, 1)

                def scores(G):
                    j, b, t, g = GROUPS[G]
                    pe.wait_ge(qk_ready, l * sum(TURNS) + sum(TURNS[:j + 1]))
                    if G >= 2:
                        pe.wait_ge(exp_ready, NG * l + G - 1)
                    for r, (q, k, half, head) in enumerate(heads(b, g)):
                        rows = slice(half * HD, (half + 1) * HD)
                        bank, c = score_row(G, r, t)
                        new, old = 4 + k, 4 + k_blocks(b) + k
                        for i, kb in enumerate((old, new) if t == SAMPLE else (new,)):
                            biased = b == "C" and t == SAMPLE and kb == new
                            out = bank[:, c + i * P:c + (i + 1) * P]
                            done = pe.matmul(out, qk_t[rows, j % 2, q, :], qk_t[rows, j % 2, kb, :], start=True, stop=not biased)
                            if biased:
                                done = pe.matmul(out, mirror, hankel[:, head, :], start=False, stop=True)
                    done.then_inc(scored, 1)

                def turn_weights(G):
                    j, b, t, g = GROUPS[G]
                    w = P * keys(t)
                    pe.wait_ge(weights_ready, NG * l + G + 1)
                    need(pe, p_ready, NG * l + G)
                    pe.wait_ge(qk_ready, at.done("qk"))
                    rows = (0, 2) if b == "B" else range(4)
                    n = 0
                    for r in rows:
                        for i in range(keys(t)):
                            c = r * w + i * P
                            done = turn(turn_banks[n // 4], n % 4 * P, e_buf[:, G % 2, c:c + P])
                            n += 1
                    done.then_inc(p_turned, 1)

                def values(G):
                    j, b, t, g = GROUPS[G]
                    pe.wait_ge(p_ready, NG * l + G + 1)
                    if not (b == "B" and g == 1):
                        need(pe, out_low, at.next("out"))
                    new = proj[:, t, V_AT[b]:V_AT[b] + (128 if b == "A" else 512)]
                    old = cache_a[:, 1, :] if b == "A" else cache_bc[:, 1, :]
                    rows = heads(b, g)
                    n = 0
                    for r in ((0, 2) if b == "B" else range(4)):
                        head = rows[r][3]
                        a, width = value_cols(b, head)
                        vals = [v[:, a:a + width] for v in ((old, new) if t == SAMPLE else (new,))]
                        for i, v in enumerate(vals):
                            ends = dict(start=i == 0, stop=i == len(vals) - 1)
                            if b == "B":
                                done = pe.matmul(banks[4][:, head * P:(head + 1) * P], p_t[:, n, :], v, **ends)
                            else:
                                half, slot = head % 2, (head // 4 if b == "A" else r // 2)
                                done = pe.matmul(banks[4][half * HD:(half + 1) * HD, slot * P:(slot + 1) * P], v, p_t[:, n, :], **ends)
                            n += 1
                    done.then_inc(pv_done, 1)
                    if b == "B" and g == 1:
                        pe.wait_ge(sub_ready, at.next("sub") + 1)
                        for h in range(B_H):
                            done = turn(banks[4], h * P, e_buf[:, G % 2, h * P:(h + 1) * P])
                        done.then_inc(sub_turned, 1)

                mod_step(0)
                turn_qk(0)
                scores(0)
                for G, (j, b, t, g) in enumerate(GROUPS):
                    if G + 1 < NG:
                        scores(G + 1)
                    mod_step(2)
                    turn_weights(G)
                    mod_units(UPC - 2)
                    values(G)
                    mod_step(0)
                    if g == 0 and j + 1 < len(jobs()):
                        turn_qk(j + 1)
                pe.wait_ge(out_low, at.done("out"))

                def gate_bias(pair, b):
                    if b == 0:
                        pe.wait_ge(bg_ready, at.next("bg") + 1)
                    for t in range(TILES):
                        pe.matmul(banks[2 * pair + t][:, :], pick[:, b, :], bg_split[:, :], start=False, stop=False)

                def gates(n):
                    for b in range(4):
                        chunk(in_high, in_low, 0, NK, bias=lambda pair: gate_bias(pair, b))
                        chunk(br_high, br_low, 4 * b, KB)
                at.rounds(pe, NCH, gates)

                pe.wait_ge(chunk_read, at.done("chunk"))
                for i in range(2 * KB):
                    t, g = i // KB, i % KB
                    n = at.next("merged")
                    need(pe, merged_low, n - 1)
                    for k in range(KB):
                        done = turn(turn_banks[i % 2], k * P, merged[:, t, (g * KB + k) * P:(g * KB + k + 1) * P])
                    done.then_inc(merged_turned, 1)
                    mod_step(len(mod_stage(l, "merge")) * UPC // (2 * KB))
                pe.wait_ge(merged_low, at.done("merged"))
                gate_rows(len(mod_stage(l, "mixer rows")) * UPC // (2 * KB))

                def w_out_pair(i):
                    for h in range(2):
                        chunk(in_high, in_low, 0, NK)
                at.rounds(pe, NCH // 2, w_out_pair)

                norm(len(mod_stage(l, "norm")) * UPC // (2 * KB))
                pe.wait_ge(router_ready, l + 1)
                for t in range(TILES):
                    for k in range(NK):
                        out = banks[4][:, t * 32:t * 32 + 20]
                        pe.matmul(out, in_high[:, k, t, :], router_high[:, k, :], start=k == 0, stop=False)
                        pe.matmul(out, in_high[:, k, t, :], router_low[:, k, :], start=False, stop=False)
                        done = pe.matmul(out, in_low[:, k, t, :], router_high[:, k, :], start=False, stop=k == NK - 1)
                done.then_inc(routed, 1)
                gate_rows(len(mod_stage(l, "expert rows")) * UPC // (2 * KB))
                pe.wait_ge(route_top, 2 * l + 1)

                def hid_turn(bank, half):
                    n = at.next("hid")
                    pe.wait_ge(chunk_read, at.done("chunk") - half)
                    need(pe, hid_stored, n - 1)
                    for k in range(2):
                        for t in range(TILES):
                            done = turn(turn_banks[bank], (k * 2 + t) * P, prod[:, t, DE + k * P:DE + (k + 1) * P])
                    done.then_inc(hid_turned, 1)

                def expert_chunk(turned_bank):
                    pair = at.parity("chunk", 2)
                    need(pe, chunk_read, at.next("chunk") - 1)
                    for j in range(UPC):
                        if j == 3 and turned_bank is not None:
                            hid_turn(turned_bank, 1)
                        part = next_unit()
                        for k in range(KB):
                            kk = j * KB + k
                            for t in range(TILES):
                                out = banks[2 * pair + t][:, :]
                                pe.matmul(out, in_high[:, kk, t, :], high_w[:, part, k, :], start=kk == 0, stop=False)
                                pe.matmul(out, in_high[:, kk, t, :], low_w[:, part, k, :], start=False, stop=False)
                                done = pe.matmul(out, in_low[:, kk, t, :], high_w[:, part, k, :], start=False, stop=kk == NK - 1)
                        done.then_inc(unit_used, 1)

                def experts(i):
                    for h in range(2):
                        if h or not at.first:
                            expert_chunk((h + 1) % 2)
                        else:
                            at.next("hid")
                            expert_chunk(None)
                at.at["hid"] = at.at.get("hid", 0) - 1
                at.rounds(pe, NE // 2, experts)
                hid_turn(1, 0)
                pe.wait_ge(hid_stored, at.done("hid"))

                def down_pair(i):
                    for h in range(2):
                        chunk(hid_high, hid_low, 0, NE * DE // P)
                at.rounds(pe, NCH // 2, down_pair)


def kernel(**inputs):
    import concourse.bacc as bacc
    from concourse.bass_utils import run_bass_kernel_spmd

    const, places, pick = shape_constants()
    nc = bacc.Bacc("TRN2", target_bir_lowering=False, num_devices=1, dynamic_dma_scratch_size=64)
    arrays = {n: np.ascontiguousarray(a) for n, a in inputs.items()}
    rpb = arrays["na_rpb"]
    arrays["na_rpb"] = np.pad(rpb, [(0, 0)] * 3 + [(GRID_W - NA_COLS, PAD_W - (GRID_W - NA_COLS) - rpb.shape[-1])])
    arrays["const"], arrays["pick"] = const, pick
    depth, d = inputs["w_in"].shape[:2]
    outs = {
        "y_prompt": inputs["x_prompt"].shape, "y_sample": inputs["x_sample"].shape,
        "new_attn_k": (1, depth, P) + inputs["cache_attn_k"].shape[3:],
        "new_attn_v": (1, depth, P) + inputs["cache_attn_v"].shape[3:],
        "new_diff_k": (1, depth, P) + inputs["cache_diff_k"].shape[3:],
        "new_diff_v": (1, depth, P) + inputs["cache_diff_v"].shape[3:],
        "new_na_k": (1, depth, P) + inputs["cache_na_k"].shape[3:],
        "new_na_v": (1, depth, P) + inputs["cache_na_v"].shape[3:],
    }
    io = {n: nc.dram_tensor("in_" + n, a.shape, F32, kind="ExternalInput").ap() for n, a in arrays.items()}
    io |= {n: nc.dram_tensor("out_" + n, s, F32, kind="ExternalOutput").ap() for n, s in outs.items()}
    trunk(nc, io, places)
    r = run_bass_kernel_spmd(nc, [{"in_" + n: a for n, a in arrays.items()}], core_ids=[0])
    return tuple(r.results[0]["out_" + n] for n in outs)
```

```python
import math
from contextlib import ExitStack

import numpy as np

import concourse.bass as bass
from concourse import mybir

F32 = mybir.dt.float32
F32R = mybir.dt.float32r
U32 = mybir.dt.uint32
I32 = mybir.dt.int32
ALU = mybir.AluOpType
ACT = mybir.ActivationFunctionType
AX = mybir.AxisListType

P = 128
TILES = 2
PROMPT, SAMPLE = 0, 1
COLS = 512
KB = 4
RAW_SLOTS = 4
SPLIT_SLOTS = 2
MOD_SLOTS = 4
HALF = 2
HALVES = KB // HALF
HD = 64
EPS = 1e-6
GRID_W = 64
NA_ROWS, NA_COLS = 8, 16
PAD_W = 128


def need(engine, semaphore, count):
    if not (isinstance(count, int) and count <= 0):
        engine.wait_ge(semaphore, count)


class Cursor:

    def __init__(self):
        self.at = {}
        self.loop = None
        self.first = False

    def next(self, name):
        k = self.at.get(name, 0)
        self.at[name] = k + 1
        if self.loop is None:
            return k
        register, first, start, rates = self.loop
        return (register - first) * rates.get(name, 0) + k

    def done(self, name):
        k = self.next(name)
        self.at[name] -= 1
        return k

    def parity(self, name, slots):
        return self.at.get(name, 0) % slots

    def rounds(self, engine, count, body):
        start = dict(self.at)
        self.first = True
        body(0)
        self.first = False
        rates = {n: k - start.get(n, 0) for n, k in self.at.items()}
        start = dict(self.at)
        if count == 1:
            return
        with engine.Fori(1, count) as i:
            self.loop = (i, 1, start, rates)
            body(i)
            self.loop = None
        for n, k in start.items():
            if self.at[n] != k:
                assert self.at[n] - k == rates[n]
                self.at[n] = k + rates[n] * (count - 1)


def shape_constants():
    t = np.arange(P)
    nf = HD // 4
    inv = (np.float32(10000.0) ** (-np.arange(nf, dtype=np.float32) / np.float32(nf))).astype(np.float32)
    pos = np.stack([t // GRID_W, t % GRID_W], -1).astype(np.float32)
    ang = (pos[:, :, None] * inv).astype(np.float32)
    rope = np.concatenate([np.cos(ang).reshape(P, 2 * nf), np.sin(ang).reshape(P, 2 * nf)], 1).astype(np.float32)
    w = 2 * np.pi * ((t[:, None] * t[None, :]) % P) / P
    fourier = np.concatenate([np.cos(w), np.sin(w)], 1).astype(np.float32)
    ident = np.eye(P, dtype=np.float32)
    back = t // GRID_W * GRID_W + GRID_W - 1 - t % GRID_W
    mirror = ident[back]
    qc = t % GRID_W
    cs = np.clip(qc - NA_COLS // 2, 0, GRID_W - NA_COLS)
    ok = (qc[None, :] >= cs[:, None]) & (qc[None, :] < cs[:, None] + NA_COLS)
    mask = np.where(ok, 0.0, -1e30).astype(np.float32)[back]
    pick = np.zeros((P, 4, P), np.float32)
    for b in range(4):
        pick[b, b] = pick[32 + b, b] = 1.0
    fold = np.zeros((P, 2), np.float32)
    for w in range(2):
        fold[w::32, w] = 1.0
    which = np.tile(np.arange(16, dtype=np.float32), (P, 1))
    group = np.tile(np.arange(16, dtype=np.float32) // 4, (P, 1))
    order = np.stack([t, t + P], 1).astype(np.float32)
    places_in_order = np.tile(np.arange(2 * P, dtype=np.float32), (P, 1))
    parts = {"ident": ident, "rope": rope, "fourier": fourier, "mirror": mirror, "mask": mask,
             "which": which, "group": group, "fold": fold, "order": order}
    places, at = {}, 0
    for n, a in parts.items():
        places[n] = (at, a.shape[1])
        at += a.shape[1]
    return np.ascontiguousarray(np.concatenate(list(parts.values()), 1)), places, pick.reshape(P, 4 * P), places_in_order


def trunk(nc, io, places):
    D = io["x_prompt"].shape[2]
    DEPTH = io["w_in"].shape[0]
    IN_W = io["w_in"].shape[2]
    NK = D // P
    NE = io["w_exp_gate"].shape[1]
    DE = io["w_exp_gate"].shape[3]
    NCH = D // COLS
    MODS = 6 * D // COLS
    UPC = NK // KB
    FIRST = 2 * D // COLS

    def mod_stage(l, stage):
        spans = {"fourier": [(l, FIRST, FIRST + 2)], "attention": [(l, FIRST + 2, MODS - 2)]}
        if l + 1 < DEPTH:
            spans |= {"merge": [(l, MODS - 2, MODS)], "mixer rows": [(l + 1, 0, 2)], "norm": [(l + 1, 2, FIRST - 4)],
                      "expert rows": [(l + 1, FIRST - 4, FIRST - 2)], "sort": [(l + 1, FIRST - 2, FIRST)]}
        else:
            spans |= {"norm": [(l, MODS - 2, MODS)]}
        return [(m, c) for m, a, b in spans.get(stage, []) for c in range(a, b)]

    STAGES = ("fourier", "attention", "merge", "mixer rows", "norm", "expert rows", "sort")
    MOD_ORDER = [(0, c) for c in range(FIRST)] + [m for l in range(DEPTH) for s in STAGES for m in mod_stage(l, s)]
    A_H, B_H, C_H = 8, 4, 8
    AQ, AK, AV, BQ, BK, BV, CQ, CK, CV, FF = 0, 512, 640, 768, 1280, 1792, 2304, 2816, 3328, 3840
    IN_CHUNKS = IN_W // COLS
    IN_REST = IN_W - IN_CHUNKS * COLS
    LAYER_CHUNKS = IN_CHUNKS + 1 + 2 * 4 * NCH + NCH + NE + NCH
    LAM = [0.8 - 0.6 * math.exp(-0.3 * l) for l in range(DEPTH)]

    with ExitStack() as ctx:
        spot = [(nc.sbuf_base + 31) // 32 * 32]

        def place(name, shape, dtype=F32, at=None):
            size = 4 * int(np.prod(shape[1:]))
            where = spot[0] if at is None else at
            t = nc.alloc_sbuf_tensor_at(name, shape, dtype, offset=where)
            if at is None:
                spot[0] += (size + 31) // 32 * 32
            return t

        raw_w = place("raw_w", [P, RAW_SLOTS, KB, COLS])
        high_w = place("high_w", [P, SPLIT_SLOTS, KB, COLS], F32R)
        low_w = place("low_w", [P, SPLIT_SLOTS, KB, COLS], F32R)
        mod_w = place("mod_w", [P, MOD_SLOTS, KB, COLS], at=spot[0] - 4 * MOD_SLOTS * KB * COLS)
        x = place("x", [P, TILES, D])
        in_high = place("in_high", [P, NK, TILES, P], F32R)
        in_low = place("in_low", [P, NK, TILES, P], F32R)
        region = spot[0]
        br_high = place("br_high", [P, NK, TILES, P], F32R)
        br_low = place("br_low", [P, NK, TILES, P], F32R)
        proj = place("proj", [P, TILES, IN_W])
        mix = spot[0]
        merged = place("merged", [P, TILES, D])
        hid_high = place("hid_high", [P, NE * 2, TILES, P], F32R, at=region)
        hid_low = place("hid_low", [P, NE * 2, TILES, P], F32R, at=region + 4 * NE * 2 * TILES * P)
        gate_row = place("gate_row", [P, TILES, D], at=mix)
        normed = place("normed", [P, D], at=region + 4 * NE * 4 * TILES * P - 8192)
        router_raw = place("router_raw", [P, NK, 20], at=region + 32768)
        router_high = place("router_high", [P, NK, 20], F32R, at=region + 32768 + 80 * NK)
        router_low = place("router_low", [P, NK, 20], F32R, at=region + 32768 + 160 * NK)
        qk_t = place("qk_t", [P, 2, 12, P], at=mix)
        hankel = place("hankel", [P, C_H, P], at=mix + 8 * 12 * P)
        e_buf = place("e_buf", [P, 2, 1024])
        ones_at = spot[0] - 8192
        sig = place("sig", [P, TILES, COLS], at=spot[0] - 8192)
        prod = place("prod", [P, TILES, COLS], at=spot[0] - 4096)
        p_t = place("p_t", [P, 8, P])
        full_at = spot[0] - 4096
        full = place("full", [P, 2, COLS], at=full_at)
        cache_bc = place("cache_bc", [P, 2, 512])
        bg_split = place("bg_split", [36, COLS], F32R, at=spot[0] - 4096)
        bg_raw = place("bg_raw", [36, COLS])
        lam_in = place("lam_in", [P, 4, HD], at=spot[0] - 2048)
        cache_a = place("cache_a", [P, 2, 128], at=spot[0] - 1024)
        mod_sums = place("mod_sums", [P, COLS])
        zeros = place("zeros", [P, P], F32R, at=spot[0] - 4 * COLS)
        const = place("const", [P, places["order"][0] + 2])
        pick = place("pick", [36, 4, P], F32R)
        mod = place("mod", [P, 2, MODS * 4, 2])
        gains = place("gains", [P, 2 * DEPTH, NK])
        scale_t = place("scale_t", [P, NK, TILES])
        cond = place("cond", [P, NK, 32])
        sub_g = place("sub_g", [P, DEPTH])
        sinks = place("sinks", [P, DEPTH, A_H])
        small = place("small", [P, 128])
        spans = place("spans", [P, 2, NE], I32, at=spot[0] - 256)
        numbers = place("numbers", [P, 2 * P], at=region)
        less = place("less", [P, 2 * P], at=region + 1024)
        sort = place("sort", [P, TILES, 2 * P], F32R, at=region + 2048)
        ranks = place("ranks", [P, 16], at=region + 4096)
        turned_high = place("turned_high", [P, 2, TILES, 2, P], F32R, at=ones_at)
        turned_low = place("turned_low", [P, 2, TILES, 2, P], F32R, at=ones_at + 4096)
        unsort = place("unsort", [P, TILES, TILES, P], F32R, at=region + 4 * NE * 4 * TILES * P)
        sorted_high = place("sorted_high", [P, TILES, COLS], F32R, at=ones_at)
        sorted_low = place("sorted_low", [P, TILES, COLS], F32R, at=full_at)
        comb = place("comb", [P, TILES, 16])
        router_b = place("router_b", [P, DEPTH, 20])
        route = place("route", [P, TILES, 96], at=region + 32768 + 240 * NK)
        ones = place("ones", [P, P], at=ones_at)
        picked = place("picked", [P, TILES, 8])
        picked_at = place("picked_at", [P, TILES, 8], U32)
        assert spot[0] <= nc.sbuf_usable_end, spot[0] - nc.sbuf_usable_end

        sum_sq, rstd = small[:, 0:2], small[:, 2:4]
        lam_sum, lam_exp, lam = small[:, 4:6], small[:, 6:8], small[:, 8:9]
        top = small[:, 16:24]
        neg_top = small[:, 24:32]
        esum = small[:, 32:40]
        rsum = small[:, 40:48]
        esink = small[:, 48:56]
        sub_sq, sub_rstd = small[:, 56:60], small[:, 60:64]

        def constant(name):
            a, n = places[name]
            return const[:, a:a + n]

        ident, mirror, mask = constant("ident"), constant("mirror"), constant("mask")
        fourier = constant("fourier")
        fold = const[:, places["fold"][0]:places["fold"][0] + 2]

        banks = [ctx.enter_context(nc.psum_tensor(f"bank{i}", [P, 512], F32)) for i in range(8)]
        turn_banks, mod_bank = banks[5:7], banks[7]

        def sem(name):
            return ctx.enter_context(nc.semaphore(name))

        raw_in = [sem(f"raw_in{i}") for i in range(RAW_SLOTS)]
        high_ready, low_ready, unit_used = sem("high_ready"), sem("low_ready"), sem("unit_used")
        chunk_read, gate_ready = sem("chunk_read"), sem("gate_ready")
        mod_in = [sem(f"mod_in{i}") for i in range(MOD_SLOTS)]
        mod_used, mod_copied, mod_turned, mod_stored = sem("mod_used"), sem("mod_copied"), sem("mod_turned"), sem("mod_stored")
        hid_turned, hid_high_ready, hid_stored = sem("hid_turned"), sem("hid_high_ready"), sem("hid_stored")
        start_in, start_turned, cond_sig, cond_ready = sem("start_in"), sem("start_turned"), sem("cond_sig"), sem("cond_ready")
        pick_in, pick_ready, vectors_in = sem("pick_in"), sem("pick_ready"), sem("vectors_in")
        bg_in, bg_clear, bg_high, bg_ready = sem("bg_in"), sem("bg_clear"), sem("bg_high"), sem("bg_ready")
        squares, mean_ready, root_ready, normed_ready = sem("squares"), sem("mean_ready"), sem("root_ready"), sem("normed_ready")
        norm_turned, norm_full, norm_high, norm_low = sem("norm_turned"), sem("norm_full"), sem("norm_high"), sem("norm_low")
        roped = sem("roped")
        cache_a_in, cache_bc_in, hankel_in, lam_in_s, router_in = sem("cache_a_in"), sem("cache_bc_in"), sem("hankel_in"), sem("lam_in_s"), sem("router_in")
        lam_sum_ready, lam_exp_ready = sem("lam_sum_ready"), sem("lam_exp_ready")
        hankel_ready = sem("hankel_ready")
        f_first, f_copied, f_second = sem("f_first"), sem("f_copied"), sem("f_second")
        qk_turned, qk_ready = sem("qk_turned"), sem("qk_ready")
        scored, top_ready, exp_ready, weights_ready = sem("scored"), sem("top_ready"), sem("exp_ready"), sem("weights_ready")
        p_turned, p_ready, pv_done, out_high, out_low = sem("p_turned"), sem("p_ready"), sem("pv_done"), sem("out_high"), sem("out_low")
        sub_squares, sub_mean, sub_root, sub_ready, sub_turned = sem("sub_squares"), sem("sub_mean"), sem("sub_root"), sem("sub_ready"), sem("sub_turned")
        diag_ready, row_summed, row_ready = sem("diag_ready"), sem("row_summed"), sem("row_ready")
        merged_turned, merged_high, merged_low = sem("merged_turned"), sem("merged_high"), sem("merged_low")
        router_high_s, router_ready, routed, route_top, route_exp, comb_ready = (
            sem("router_high_s"), sem("router_ready"), sem("routed"), sem("route_top"), sem("route_exp"), sem("comb_ready"))
        final_in, final_scaled, out_stored, cache_stored = sem("final_in"), sem("final_scaled"), sem("out_stored"), sem("cache_stored")
        x_ready = sem("x_ready")
        zeros_ready = sem("zeros_ready")
        numbers_in, keys_ready, keys_spread, sort_ready = sem("numbers_in"), sem("keys_ready"), sem("keys_spread"), sem("sort_ready")
        unsort_turned, unsort_ready, comb_sorted = sem("unsort_turned"), sem("unsort_ready"), sem("comb_sorted")
        back_turned = [sem("back_turned_high"), sem("back_turned_low")]
        back_copied = [sem("back_copied_high"), sem("back_copied_low")]
        sort_summed = [sem("sort_summed_high"), sem("sort_summed_low")]
        sort_stored = [sem("sort_stored_high"), sem("sort_stored_low")]
        out_sorted_high, out_back, added = sem("out_sorted_high"), sem("out_back"), sem("added")

        def jobs():
            return [(b, t) for b in "ABC" for t in (SAMPLE, PROMPT)]

        def q_blocks(b):
            return 4

        def k_blocks(b):
            return 1 if b == "A" else 4

        def n_blocks(b, t):
            return q_blocks(b) + k_blocks(b) * (2 if t == SAMPLE else 1)

        def heads(b, g):
            if b == "A":
                return [(2 * g + r // 2, 0, r % 2, 2 * g + r // 2 + 4 * (r % 2)) for r in range(4)]
            if b == "B":
                return [(2 * g + r // 2, 2 * g + r // 2, r % 2, 2 * g + r // 2) for r in range(4)]
            return [(2 * g + r // 2, 2 * g + r // 2, r % 2, 4 * g + r) for r in range(4)]

        GROUPS = [(j, b, t, g) for j, (b, t) in enumerate(jobs()) for g in range(2)]
        NG = len(GROUPS)
        TURNS = [(n_blocks(b, t) + 3) // 4 for b, t in jobs()]

        def keys(t):
            return 2 if t == SAMPLE else 1

        def score_row(g, r, t):
            return banks[2 * (g % 2) + r % 2], r // 2 * P * keys(t)

        def value_cols(b, head):
            return (head // 4 * HD, HD) if b == "A" else ((head * P, P) if b == "B" else (head * HD, HD))

        V_AT = {"A": AV, "B": BV, "C": CV}
        BRANCH = {"A": 0, "B": 1, "C": 2, "F": 3}

        def weight_tile(w, l, col, width, block):
            return w[l, block * KB * P:(block + 1) * KB * P, col].rearrange("(k p) n -> p k n", p=P)

        block = ctx.enter_context(nc.Block())

        @block.sync
        def _(sp):
            at = Cursor()

            def load(src, width=COLS):
                slot = at.parity("unit", RAW_SLOTS)
                u = at.next("unit")
                need(sp, low_ready, (u - RAW_SLOTS + 1) * HALVES)
                at.next(f"in{slot}")
                sp.dma_start(raw_w[:, slot, :, 0:width], src).then_inc(raw_in[slot], 16)

            def load_mod(l, c):
                for j in range(UPC):
                    slot = at.parity("mod_unit", MOD_SLOTS)
                    need(sp, mod_used, at.next("mod_unit") - MOD_SLOTS + 1)
                    sp.dma_start(mod_w[:, slot, :, :], weight_tile(io["w_mod"], l, bass.ds(c * COLS, COLS), COLS, j)
                                 ).then_inc(mod_in[slot], 16)

            def load_mods(chunks):
                need(sp, unit_used, (at.done("unit") - UPC) * HALVES if chunks else 0)
                for l, c in chunks:
                    load_mod(l, c)

            sp.dma_start(const[:, :], io["const"]).then_inc(start_in, 16)
            sp.dma_start(normed[0:NK, 0:P], io["c_ctx"].rearrange("(k p) -> k p", p=P)).then_inc(start_in, 16)
            sp.dma_start(normed[NK:2 * NK, 0:P], io["c"].rearrange("a (k p) -> (a k) p", p=P)).then_inc(start_in, 16)
            for l in range(DEPTH):
                sp.dma_start(normed[0:MODS * 4, (1 + l) * P:(2 + l) * P],
                             io["b_mod"][l].rearrange("(k p) -> k p", p=P)).then_inc(start_in, 16)
            for l in range(DEPTH):
                for i, n in enumerate(("norm1_g", "norm2_g")):
                    r = (2 * l + i) * NK
                    sp.dma_start(normed[r:r + NK, 3 * P:4 * P],
                                 io[n][l].rearrange("(k p) -> k p", p=P)).then_inc(start_in, 16)
            sp.dma_start(x[:, PROMPT, :], io["x_prompt"][0]).then_inc(x_ready, 16)
            sp.dma_start(x[:, SAMPLE, :], io["x_sample"][0]).then_inc(x_ready, 16)

            def mod_start(c):
                load_mod(0, c)
            at.rounds(sp, FIRST, mod_start)
            sp.dma_start(proj[0:36, 0, 0:4 * P], io["pick"][0:36, :]).then_inc(pick_in, 16)
            for l in range(DEPTH):
                sp.dma_start(sub_g[:, l:l + 1], io["diff_sub_g"][l].rearrange("(p a) -> p a", a=1)).then_inc(vectors_in, 16)
                sp.dma_start(sinks[:, l, :], io["attn_sink"][l:l + 1, :].broadcast_to([P, A_H])).then_inc(vectors_in, 16)
                sp.dma_start(router_b[:, l, 0:4], io["b_router_group"][l:l + 1, :].broadcast_to([P, 4])).then_inc(vectors_in, 16)
                sp.dma_start(router_b[:, l, 4:20], io["b_router_expert"][l:l + 1, :].broadcast_to([P, 16])).then_inc(vectors_in, 16)

            for l in range(DEPTH):
                def operands():
                    if l:
                        sp.wait_ge(added, NCH * l)
                    sp.dma_start(cache_a[:, 0, :], io["cache_attn_k"][0, l].rearrange("s h d -> s (h d)")).then_inc(cache_a_in, 16)
                    sp.dma_start(cache_a[:, 1, :], io["cache_attn_v"][0, l].rearrange("s h d -> s (h d)")).then_inc(cache_a_in, 16)
                    sp.dma_start(cache_bc[:, 0, :], io["cache_diff_k"][0, l].rearrange("s h m d -> s (h m d)")).then_inc(cache_bc_in, 16)
                    sp.dma_start(cache_bc[:, 1, :], io["cache_diff_v"][0, l].rearrange("s h d -> s (h d)")).then_inc(cache_bc_in, 16)
                    sp.dma_start(lam_in[:, :, :], io["diff_lambda"][l:l + 1].broadcast_to([P, 4, HD])).then_inc(lam_in_s, 16)
                    rpb = io["na_rpb"]
                    for qr in range(2):
                        for kr in range(2):
                            first = (l * C_H * (2 * NA_ROWS - 1) + NA_ROWS - 1 - qr + kr) * PAD_W
                            src = bass.AP(tensor=rpb.tensor, offset=first,
                                          ap=[[1, GRID_W], [(2 * NA_ROWS - 1) * PAD_W, C_H], [1, GRID_W]])
                            sp.dma_start(hankel[qr * GRID_W:(qr + 1) * GRID_W, :, kr * GRID_W:(kr + 1) * GRID_W],
                                         src).then_inc(hankel_in, 16)

                def w_in_pair(i):
                    for h in range(2):
                        for j in range(UPC):
                            load(weight_tile(io["w_in"], l, bass.ds((i * 2 + h) * COLS, COLS), COLS, j))
                        if h == 0 and at.first:
                            operands()
                at.rounds(sp, IN_CHUNKS // 2, w_in_pair)
                for j in range(UPC):
                    load(weight_tile(io["w_in"], l, slice(IN_CHUNKS * COLS, IN_W), IN_REST, j), IN_REST)

                def mixers():
                    sp.wait_ge(chunk_read, LAYER_CHUNKS * l + IN_CHUNKS + 1)
                    for name, a, n in (("new_attn_k", AK, 128), ("new_attn_v", AV, 128), ("new_diff_k", BK, 512),
                                       ("new_diff_v", BV, 512), ("new_na_k", CK, 512), ("new_na_v", CV, 512)):
                        dst = io[name][0, l]
                        dst = dst.rearrange("s h m d -> s (h m d)") if name == "new_diff_k" else dst.rearrange("s h d -> s (h d)")
                        sp.dma_start(dst, proj[:, PROMPT, a:a + n]).then_inc(cache_stored, 16)
                    beside = mod_stage(l, "fourier") + mod_stage(l, "attention")
                    early = 2 + 6
                    load_mods(beside[:early])
                    sp.wait_ge(pv_done, NG * l + 6)
                    sp.dma_start(cache_bc[:, 0, :], io["cache_na_k"][0, l].rearrange("s h d -> s (h d)")).then_inc(cache_bc_in, 16)
                    sp.dma_start(cache_bc[:, 1, :], io["cache_na_v"][0, l].rearrange("s h d -> s (h d)")).then_inc(cache_bc_in, 16)
                    load_mods(beside[early:])

                def gates(n):
                    for b in range(4):
                        for j in range(UPC):
                            load(weight_tile(io["w_gate"], l, bass.ds(n * COLS + b * D, COLS), COLS, j))
                        if b == 0:
                            r = at.next("bg")
                            if at.first:
                                mixers()
                                sp.wait_ge(bg_clear, l + 1)
                            need(sp, bg_ready, r)
                            for row in (0, 32):
                                sp.dma_start(bg_raw[row:row + 4, :],
                                             io["b_gate"][l].rearrange("(b n) -> b n", b=4)[:, bass.ds(n * COLS, COLS)]
                                             ).then_inc(bg_in, 16)
                        load(io["w_branch"][l, b, :, bass.ds(n * COLS, COLS)].rearrange("(k p) n -> p k n", p=P))
                at.rounds(sp, NCH, gates)

                def merge():
                    sp.wait_ge(cache_stored, 16 * 6 * (l + 1))
                    sp.dma_start(router_raw[:, :, 0:4], io["w_router_group"][l].rearrange("(k p) n -> p k n", p=P)).then_inc(router_in, 16)
                    sp.dma_start(router_raw[:, :, 4:20], io["w_router_expert"][l].rearrange("(k p) n -> p k n", p=P)).then_inc(router_in, 16)
                    load_mods(mod_stage(l, "merge") + mod_stage(l, "mixer rows"))

                def w_out(n):
                    for j in range(UPC):
                        load(weight_tile(io["w_out"], l, bass.ds(n * COLS, COLS), COLS, j))
                    if at.first:
                        merge()
                at.rounds(sp, NCH, w_out)

                def routing():
                    sp.dma_start(numbers[:, :], io["numbers"]).then_inc(numbers_in, 16)
                    load_mods(mod_stage(l, "norm") + mod_stage(l, "expert rows") + mod_stage(l, "sort"))

                def experts(i):
                    for h in range(2):
                        for j in range(UPC):
                            slot = at.parity("unit", RAW_SLOTS)
                            u = at.next("unit")
                            need(sp, low_ready, (u - RAW_SLOTS + 1) * HALVES)
                            for half, name in enumerate(("w_exp_gate", "w_exp_up")):
                                at.next(f"in{slot}")
                                src = io[name][l][bass.ds(i * 2 + h, 1), j * KB * P:(j + 1) * KB * P, :]
                                sp.dma_start(raw_w[:, slot, :, half * DE:(half + 1) * DE],
                                             src.rearrange("e (k p) f -> p (e k) f", p=P)).then_inc(raw_in[slot], 16)
                        if h == 0 and at.first:
                            routing()
                at.rounds(sp, NE // 2, experts)

                def down(n):
                    rows = io["w_exp_down"][l].rearrange("e (k p) n -> p (e k) n", p=P)
                    for j in range(NE * DE // P // KB):
                        load(rows[:, j * KB:(j + 1) * KB, bass.ds(n * COLS, COLS)])
                at.rounds(sp, NCH, down)

            sp.wait_ge(added, NCH * DEPTH)
            sp.dma_start(merged[:, 0, :], io["final_g"].rearrange("(a n) -> a n", a=1).broadcast_to([P, D])).then_inc(final_in, 16)
            for t, name in enumerate(("y_prompt", "y_sample")):
                sp.wait_ge(final_scaled, t + 1)
                sp.dma_start(io[name][0], x[:, t, :]).then_inc(out_stored, 16)
            sp.wait_ge(out_stored, 32)
            sp.wait_ge(cache_stored, 16 * 6 * DEPTH)

        @block.scalar
        def _(act):
            at = Cursor()

            def split_high(width=COLS, loads=1):
                slot, part = at.parity("unit", RAW_SLOTS), at.parity("unit", SPLIT_SLOTS)
                u = at.next("unit")
                for _ in range(loads):
                    k = at.next(f"in{slot}")
                act.wait_ge(raw_in[slot], k * 16 + 16)
                for h in range(HALVES):
                    need(act, unit_used, (u - SPLIT_SLOTS) * HALVES + h + 1)
                    ks = slice(h * HALF, (h + 1) * HALF)
                    act.activation(high_w[:, part, ks, 0:width], raw_w[:, slot, ks, 0:width], ACT.Copy).then_inc(high_ready, 1)

            def mods_done():
                act.wait_ge(mod_used, mods_done.units)
            mods_done.units = UPC * FIRST

            def root_mean_square():
                for t in range(TILES):
                    act.activation(normed[:, :], x[:, t, :], ACT.Square, accum_out=sum_sq[:, t:t + 1]).then_inc(squares, 1)
                    act.drain()
                act.wait_ge(mean_ready, at.next("norm") + 1)
                act.activation(rstd, rstd, ACT.Sqrt).then_inc(root_ready, 1)

            def norm():
                for i in range(2 * KB):
                    t, g = i // KB, i % KB
                    act.wait_ge(norm_full, at.next("norm_group") + 1)
                    act.activation(in_high[:, g * KB:(g + 1) * KB, t, :],
                                   full[:, i % 2, :].rearrange("p (k n) -> p k n", n=P), ACT.Copy).then_inc(norm_high, 1)

            act.wait_ge(start_turned, 1)
            act.activation(sig[:, 0, 0:2 * NK], mod_bank[:, 0:2 * NK], ACT.Sigmoid).then_inc(cond_sig, 1)
            act.wait_ge(x_ready, 32)
            root_mean_square()
            act.wait_ge(pick_in, 16)
            act.activation(pick[:, :, :], proj[0:36, 0, 0:4 * P].rearrange("p (b n) -> p b n", b=4), ACT.Copy).then_inc(pick_ready, 1)

            for l in range(DEPTH):
                if l:
                    act.wait_ge(added, NCH * l)
                    root_mean_square()
                norm()

                def copy_proj(col, width, after):
                    at.next("chunk")
                    act.wait_ge(unit_used, (at.done("unit") - after) * HALVES)
                    for t in range(TILES):
                        dst, src = proj[:, t, bass.ds(col, width)], banks[copy_proj.pair * 2 + t][:, 0:width]
                        if isinstance(col, int) and col == AQ:
                            dst = dst.rearrange("p (h a d) -> p a h d", a=2, d=HD)
                            src = src.rearrange("p (a h d) -> p a h d", a=2, d=HD)
                        copied = act.activation(dst, src, ACT.Copy)
                        if t == 0:
                            continue
                        copied.then_inc(chunk_read, 1)

                at.at["chunk"] = at.at.get("chunk", 0) - 1
                mods_done()

                def w_in_pair(i):
                    for h in range(2):
                        split_high()
                        split_high()
                        if h or not at.first:
                            copy_proj.pair = (l * LAYER_CHUNKS + h + 1) % 2
                            copy_proj((i * 2 + h - 1) * COLS, COLS, 2)
                        else:
                            at.next("chunk")
                        split_high()
                        split_high()
                at.rounds(act, IN_CHUNKS // 2, w_in_pair)
                split_high(IN_REST)
                split_high(IN_REST)
                copy_proj.pair = (l * LAYER_CHUNKS + 1) % 2
                copy_proj((IN_CHUNKS - 1) * COLS, COLS, 2)
                split_high(IN_REST)
                split_high(IN_REST)
                copy_proj.pair = l * LAYER_CHUNKS % 2
                copy_proj(IN_CHUNKS * COLS, IN_REST, 0)

                def out_copy(first, step, t, source, scale=1.0):
                    n = at.next("out")
                    dst = br_high[:, first:first + step * (source.shape[1] - 1) + 1:step, t, :]
                    act.activation(dst, source, ACT.Copy, scale=scale).then_inc(out_high, 1)

                for t in (SAMPLE, PROMPT):
                    n = at.next("fourier")
                    act.wait_ge(f_first, n + 1)
                    for g in range(2):
                        for part, scale in ((0, 1.0 / P), (1, -1.0 / P)):
                            src = banks[g][:, :].rearrange("p (g c n) -> p g c n", g=2, c=2)[:, :, part, :]
                            dst = e_buf[:, t, g * 512:(g + 1) * 512].rearrange("p (g c n) -> p g c n", g=2, c=2)[:, :, part, :]
                            copied = act.activation(dst, src, ACT.Copy, scale=scale)
                    copied.then_inc(f_copied, 1)
                    act.wait_ge(f_second, n + 1)
                    out_copy(4 * BRANCH["F"], 1, t, banks[4][:, :].rearrange("p (g n) -> p g n", n=P))

                act.wait_ge(lam_sum_ready, l + 1)
                act.activation(lam_exp, lam_sum, ACT.Exp).then_inc(lam_exp_ready, 1)

                def copy_qk(j):
                    b, t = jobs()[j]
                    if j >= 2:
                        act.wait_ge(scored, NG * l + 2 * (j - 1))
                    for i in range(TURNS[j]):
                        n = min(4, n_blocks(b, t) - 4 * i)
                        act.wait_ge(qk_turned, at.next("qk") + 1)
                        act.activation(qk_t[:, j % 2, 4 * i:4 * i + n, :],
                                       turn_banks[i % 2][:, 0:n * P].rearrange("p (k n) -> p k n", n=P), ACT.Copy,
                                       scale=HD ** -0.5 if i == 0 else 1.0).then_inc(qk_ready, 1)

                def exps(G):
                    j, b, t, g = GROUPS[G]
                    act.wait_ge(top_ready, NG * l + G + 1)
                    if G >= 2:
                        act.wait_ge(p_turned, NG * l + G - 1)
                    w = P * keys(t)
                    if b == "A":
                        act.activation(esink[:, 4 * (G % 2):4 * (G % 2) + 4], esink[:, 4 * (G % 2):4 * (G % 2) + 4], ACT.Exp)
                    for r in range(4):
                        bank, c = score_row(G, r, t)
                        k = 4 * (G % 2) + r
                        done = act.activation(e_buf[:, G % 2, r * w:(r + 1) * w], bank[:, c:c + w], ACT.Exp,
                                              bias=neg_top[:, k:k + 1], accum_out=esum[:, k:k + 1])
                    done.then_inc(exp_ready, 1)

                def copy_p(G):
                    j, b, t, g = GROUPS[G]
                    n = (2 if b == "B" else 4) * keys(t)
                    act.wait_ge(p_turned, NG * l + G + 1)
                    need(act, pv_done, NG * l + G)
                    for h in range((n + 3) // 4):
                        m = min(4, n - 4 * h)
                        copied = act.activation(p_t[:, 4 * h:4 * h + m, :],
                                                turn_banks[h][:, 0:m * P].rearrange("p (k n) -> p k n", n=P), ACT.Copy)
                    copied.then_inc(p_ready, 1)

                copy_qk(0)
                exps(0)
                for G, (j, b, t, g) in enumerate(GROUPS):
                    if G + 1 < NG:
                        exps(G + 1)
                    copy_p(G)
                    if b != "B":
                        act.wait_ge(pv_done, NG * l + G + 1)
                        first, step = (g, 2) if b == "A" else (8 + 2 * g, 1)
                        out_copy(first, step, t, banks[4][:, 0:2 * P].rearrange("p (k n) -> p k n", n=P))
                    elif g == 1:
                        n = at.next("sub")
                        act.wait_ge(pv_done, NG * l + G + 1)
                        out_b = e_buf[:, G % 2, 0:512]
                        for h in range(B_H):
                            done = act.activation(out_b[:, h * P:(h + 1) * P], banks[4][:, h * P:(h + 1) * P], ACT.Square,
                                                  accum_out=sub_sq[:, h:h + 1])
                        done.then_inc(sub_squares, 1)
                        act.wait_ge(sub_mean, n + 1)
                        act.activation(sub_rstd, sub_rstd, ACT.Sqrt).then_inc(sub_root, 1)
                        act.wait_ge(sub_turned, n + 1)
                        out_copy(4, 1, t, banks[4][:, :].rearrange("p (k n) -> p k n", n=P), scale=sub_g[:, l:l + 1])
                    if g == 0 and j + 1 < len(jobs()):
                        copy_qk(j + 1)

                def gate_pair(b):
                    return (l * LAYER_CHUNKS + IN_CHUNKS + 1 + 2 * b) % 2

                def sigmoids(b, after, done_s, width=COLS):
                    act.wait_ge(unit_used, (at.done("unit") - after) * HALVES)
                    need(act, chunk_read, at.done("chunk") - 1)
                    for t in range(TILES):
                        done = act.activation(sig[:, t, 0:width], banks[2 * b + t][:, 0:width], ACT.Sigmoid)
                    done.then_inc(done_s, 1)

                mods_done.units += UPC * len(mod_stage(l, "fourier") + mod_stage(l, "attention"))
                mods_done()

                def gates(n):
                    for b in range(4):
                        for j in range(UPC):
                            if b == 0 and j == 2:
                                r = at.next("bg")
                                act.wait_ge(bg_in, r * 32 + 32)
                                need(act, unit_used, (at.done("unit") - 3) * HALVES)
                                act.activation(bg_split[:, :], bg_raw[:, :], ACT.Copy).then_inc(bg_high, 1)
                            split_high()
                        at.next("chunk")
                        split_high()
                        sigmoids(gate_pair(b), 1, chunk_read)
                        at.next("chunk")
                at.rounds(act, NCH, gates)

                for i in range(2 * KB):
                    t, g = i // KB, i % KB
                    act.wait_ge(merged_turned, at.next("merged") + 1)
                    act.activation(in_high[:, g * KB:(g + 1) * KB, t, :],
                                   turn_banks[i % 2][:, :].rearrange("p (k n) -> p k n", n=P), ACT.Copy).then_inc(merged_high, 1)

                def gate_rows():
                    for i in range(2 * KB):
                        t, g = i // KB, i % KB
                        act.wait_ge(row_summed, at.next("row") + 1)
                        act.activation(gate_row[:, t, g * COLS:(g + 1) * COLS], turn_banks[i % 2][:, :], ACT.Copy).then_inc(row_ready, 1)
                gate_rows()
                mods_done.units += UPC * len(mod_stage(l, "merge") + mod_stage(l, "mixer rows"))
                mods_done()

                def w_out(n):
                    for j in range(UPC):
                        split_high()
                    at.next("chunk")
                at.rounds(act, NCH, w_out)

                act.wait_ge(router_in, 32 * (l + 1))
                act.activation(router_high[:, :, :], router_raw[:, :, :], ACT.Copy).then_inc(router_high_s, 1)
                act.wait_ge(chunk_read, at.done("chunk"))
                root_mean_square()
                norm()
                gate_rows()
                act.wait_ge(route_top, 2 * l + 1)
                for t in range(TILES):
                    done = act.activation(route[:, t, 64:68], route[:, t, 0:4], ACT.Exp, bias=route[:, t, 41:42],
                                          accum_out=route[:, t, 42:43])
                done.then_inc(route_exp, 1)
                act.wait_ge(route_top, 2 * l + 2)
                act.activation(route[:, :, 43:44], route[:, :, 43:44], ACT.Exp).then_inc(route_exp, 1)


                act.wait_ge(unsort_turned, l + 1)
                act.activation(unsort[:, :, :, :].rearrange("p s t n -> p (s t n)"), turn_banks[0][:, :], ACT.Copy).then_inc(unsort_ready, 1)

                def copy_back(q):
                    n = NK // 2 * l + q
                    act.wait_ge(back_turned[0], n + 1)
                    need(act, sort_summed[0], n - 1)
                    act.activation(turned_high[:, q % 2, :, :, :].rearrange("p t k n -> p (t k n)"), banks[0][:, :], ACT.Copy).then_inc(back_copied[0], 1)

                copy_back(0)
                for q in range(NK // 2):
                    if q + 1 < NK // 2:
                        copy_back(q + 1)
                    act.wait_ge(sort_summed[0], NK // 2 * l + q + 1)
                    act.activation(in_high[:, 2 * q:2 * q + 2, :, :].rearrange("p k t n -> p (k t n)"), banks[2][:, :], ACT.Copy).then_inc(sort_stored[0], 1)

                mods_done.units += UPC * len(mod_stage(l, "norm") + mod_stage(l, "expert rows") + mod_stage(l, "sort"))
                mods_done()

                def hid_copy(e):
                    act.wait_ge(hid_turned, at.next("hid") + 1)
                    act.activation(hid_high[:, :, :, :].rearrange("p k t n -> p (k t n)")[:, bass.ds(e * 512, 512)],
                                   turn_banks[hid_copy.bank][:, :], ACT.Copy).then_inc(hid_high_ready, 1)

                def experts(i):
                    for h in range(2):
                        split_high(loads=2)
                        split_high(loads=2)
                        later = h or not at.first
                        if later:
                            sigmoids((l * LAYER_CHUNKS + LAYER_CHUNKS - NCH + h + 1) % 2, 2, gate_ready, DE)
                        split_high(loads=2)
                        split_high(loads=2)
                        hid_copy.bank = (h + 1) % 2
                        if later:
                            hid_copy(i * 2 + (h - 1))
                        else:
                            at.next("hid")
                        at.next("chunk")
                at.at["hid"] = at.at.get("hid", 0) - 1
                at.rounds(act, NE // 2, experts)
                sigmoids((l * LAYER_CHUNKS + LAYER_CHUNKS - NCH + 1) % 2, 0, gate_ready, DE)
                hid_copy.bank = 1
                hid_copy(NE - 1)

                first_pair = (l * LAYER_CHUNKS + LAYER_CHUNKS - NCH) % 2

                def sorted_out(pair, after):
                    n = at.next("sorted_out")
                    act.wait_ge(unit_used, (at.done("unit") - after) * HALVES)
                    need(act, out_back, n)
                    for t in range(TILES):
                        done = act.activation(sorted_high[:, t, :], banks[2 * pair + t][:, :], ACT.Copy)
                    done.then_inc(out_sorted_high, 1)

                def down_pair(i):
                    for h in range(2):
                        split_high()
                        split_high()
                        if h or not at.first:
                            sorted_out((first_pair + h + 1) % 2, 2)
                        else:
                            at.next("sorted_out")
                        for j in range(NE * DE // P // KB - 2):
                            split_high()
                        at.next("chunk")
                at.at["sorted_out"] = at.at.get("sorted_out", 0) - 1
                at.rounds(act, NCH // 2, down_pair)
                sorted_out((first_pair + 1) % 2, 0)

            act.wait_ge(added, NCH * DEPTH)
            root_mean_square()

        @block.vector
        def _(dve):
            at = Cursor()

            def split_low(width=COLS):
                slot, part = at.parity("unit", RAW_SLOTS), at.parity("unit", SPLIT_SLOTS)
                u = at.next("unit")
                for h in range(HALVES):
                    dve.wait_ge(high_ready, u * HALVES + h + 1)
                    ks = slice(h * HALF, (h + 1) * HALF)
                    dve.tensor_tensor(low_w[:, part, ks, 0:width], raw_w[:, slot, ks, 0:width],
                                      high_w[:, part, ks, 0:width].bitcast(F32), ALU.subtract).then_inc(low_ready, 1)

            def mod_copy():
                m = at.next("mod_copy")
                dve.wait_ge(mod_used, m * UPC + UPC)
                need(dve, mod_turned, m)
                dve.tensor_copy(mod_sums[:, :], mod_bank[:, :]).then_inc(mod_copied, 1)

            def mod_store(layer, c):
                m = at.next("mod_store")
                dve.wait_ge(mod_turned, m + 1)
                own = mod[:, layer, bass.ds(c * 4, 4), :]
                dve.tensor_tensor(own, own, mod_bank[:, 0:8].rearrange("p (k w) -> p k w", w=2), ALU.add).then_inc(mod_stored, 1)

            def mod_step(units):
                if at.done("mod_store") < at.done("mod_copy"):
                    mod_store(*MOD_ORDER[at.done("mod_store")])
                at.at["mod_unit"] = at.done("mod_unit") + units
                if at.done("mod_unit") // UPC > at.done("mod_copy"):
                    mod_copy()

            def root_mean_square():
                n = at.next("norm")
                dve.wait_ge(squares, 2 * n + 2)
                dve.tensor_scalar(sum_sq, sum_sq, 1.0 / D, EPS, ALU.mult, ALU.add)
                dve.drain()
                dve.reciprocal(rstd, sum_sq).then_inc(mean_ready, 1)
                dve.wait_ge(root_ready, n + 1)

            def norm(l, which, mod_units=0):
                shift, scale, gain = 48 * which, 48 * which + 16, 2 * l + which
                if l or which:
                    root_mean_square()
                dve.drain()
                dve.scalar_tensor_tensor(scale_t[:, :, :], mod[:, l, scale:scale + NK, :], 1.0,
                                         gains[:, gain, :].unsqueeze(2).broadcast_to([P, NK, 2]), ALU.add, ALU.mult)
                def low(i):
                    t, g = i // KB, i % KB
                    dve.wait_ge(norm_high, at.next("norm_low") + 1)
                    dst = slice(g * KB, (g + 1) * KB)
                    dve.tensor_tensor(in_low[:, dst, t, :], full[:, i % 2, :].rearrange("p (k n) -> p k n", n=P),
                                      in_high[:, dst, t, :].bitcast(F32), ALU.subtract).then_inc(norm_low, 1)

                for i in range(2 * KB):
                    t, g = i // KB, i % KB
                    n = at.next("norm_group")
                    if g == 0:
                        need(dve, norm_turned, n)
                        dve.tensor_scalar(normed[:, :], x[:, t, :], rstd[:, t:t + 1], None, ALU.mult).then_inc(normed_ready, 1)
                    dve.wait_ge(norm_turned, n + 1)
                    dve.drain()
                    for k in range(KB):
                        kk = g * KB + k
                        done = dve.tensor_scalar(full[:, i % 2, k * P:(k + 1) * P], turn_banks[i % 2][:, k * P:(k + 1) * P],
                                                 scale_t[:, kk, t:t + 1], mod[:, l, shift + kk, t:t + 1], ALU.mult, ALU.add)
                    done.then_inc(norm_full, 1)
                    if i:
                        low(i - 1)
                    mod_step(mod_units)
                dve.wait_ge(norm_high, n + 1)
                low(2 * KB - 1)

            dve.wait_ge(cond_sig, 1)
            dve.memset(cond[:, :, :], 0.0)
            dve.drain()
            dve.tensor_copy(mod[:, :, :, :].rearrange("p l k w -> p (l k) w"),
                            mod_bank[:, 32:32 + DEPTH * MODS * 4].unsqueeze(2).broadcast_to([P, DEPTH * MODS * 4, 2]))
            dve.tensor_copy(gains[:, :, :].rearrange("p l k -> p (l k)"), mod_bank[:, 224:224 + 4 * NK])
            dve.tensor_tensor(cond[:, :, 0:2].rearrange("p k w -> p w k"),
                              mod_bank[:, 0:2 * NK].rearrange("p (w k) -> p w k", w=2),
                              sig[:, 0, 0:2 * NK].rearrange("p (w k) -> p w k", w=2), ALU.mult).then_inc(cond_ready, 1)

            root_mean_square()

            def mod_start(c):
                mod_copy()
                mod_store(0, c)
            at.rounds(dve, FIRST, mod_start)
            at.at["mod_unit"] = UPC * FIRST
            dve.wait_ge(vectors_in, 16 * 4 * DEPTH)
            for l in range(DEPTH):
                dve.tensor_scalar(sub_g[:, l:l + 1], sub_g[:, l:l + 1], 1.0 - LAM[l], None, ALU.mult)

            for l in range(DEPTH):
                norm(l, 0)

                def w_in_pair(i):
                    for j in range(2 * UPC):
                        split_low()
                    at.next("chunk")
                    at.next("chunk")
                at.rounds(dve, IN_CHUNKS // 2, w_in_pair)
                for j in range(UPC):
                    split_low(IN_REST)
                at.next("chunk")

                dve.wait_ge(chunk_read, LAYER_CHUNKS * l + IN_CHUNKS + 1)
                cos, sin = (constant("rope")[:, i * 32:(i + 1) * 32].rearrange("p (x f) -> p x f", x=2) for i in range(2))
                for a, n in ((AQ, 10), (BQ, 16)):
                    pair = proj[:, SAMPLE, a:a + n * HD].rearrange("p (h x y f) -> p h x y f", x=2, y=2, f=HD // 4)
                    one, two = pair[:, :, :, 0, :], pair[:, :, :, 1, :]
                    c, s = (v.unsqueeze(1).broadcast_to([P, n, 2, HD // 4]) for v in (cos, sin))
                    flat = p_t[:, :, :].rearrange("p k n -> p (k n)")
                    u, v = (flat[:, i * 512:i * 512 + n * 32].rearrange("p (h x f) -> p h x f", x=2, f=HD // 4) for i in range(2))
                    dve.tensor_tensor(u, one, s, ALU.mult)
                    dve.tensor_tensor(v, two, s, ALU.mult)
                    dve.drain()
                    dve.tensor_tensor(one, one, c, ALU.mult)
                    dve.tensor_tensor(two, two, c, ALU.mult)
                    dve.drain()
                    dve.tensor_tensor(one, one, v, ALU.subtract)
                    dve.tensor_tensor(two, two, u, ALU.add).then_inc(roped, 1)
                    dve.drain()

                dve.wait_ge(lam_in_s, 16 * (l + 1))
                quad = lam_in[:, :, :].rearrange("p (a b) n -> p a b n", b=2)
                dve.tensor_tensor(quad[:, :, 0, :], quad[:, :, 0, :], quad[:, :, 1, :], ALU.mult)
                dve.drain()
                dve.tensor_reduce(lam_sum, quad[:, :, 0, :], AX.X, ALU.add).then_inc(lam_sum_ready, 1)
                dve.wait_ge(hankel_in, 64 * (l + 1))
                dve.tensor_tensor(hankel[:, :, :], hankel[:, :, :], mask.unsqueeze(1).broadcast_to([P, C_H, P]), ALU.add).then_inc(hankel_ready, 1)

                def out_rest(first, step, t, source, scale=None):
                    n = at.next("out")
                    dve.wait_ge(out_high, n + 1)
                    s = slice(first, first + step * (source.shape[1] - 1) + 1, step)
                    if scale is None:
                        done = dve.tensor_tensor(br_low[:, s, t, :], source, br_high[:, s, t, :].bitcast(F32), ALU.subtract)
                    else:
                        done = dve.scalar_tensor_tensor(br_low[:, s, t, :], source, scale, br_high[:, s, t, :].bitcast(F32),
                                                        ALU.mult, ALU.subtract)
                    done.then_inc(out_low, 1)

                for t in (SAMPLE, PROMPT):
                    mod_step(UPC)
                    out_rest(4 * BRANCH["F"], 1, t, banks[4][:, :].rearrange("p (g n) -> p g n", n=P))
                mod_step(0)
                dve.wait_ge(lam_exp_ready, l + 1)
                dve.tensor_tensor(lam, lam_exp[:, 0:1], lam_exp[:, 1:2], ALU.subtract)
                dve.drain()
                dve.tensor_scalar(lam, lam, LAM[l], None, ALU.add)

                def tops(G):
                    j, b, t, g = GROUPS[G]
                    w, k = P * keys(t), 4 * (G % 2)
                    dve.wait_ge(scored, NG * l + G + 1)
                    for h in range(2):
                        bank, _ = score_row(G, h, t)
                        dve.tensor_reduce(top[:, k + h:k + 4:2], bank[:, 0:2 * w].rearrange("p (r n) -> p r n", n=w), AX.X, ALU.max)
                    dve.drain()
                    if b == "A":
                        sink = sinks[:, l, :].rearrange("p (a h) -> p h a", a=2)[:, 2 * g:2 * g + 2, :]
                        v = top[:, k:k + 4].rearrange("p (h a) -> p h a", a=2)
                        dve.tensor_tensor(v, v, sink, ALU.max)
                        dve.drain()
                        dve.tensor_tensor(esink[:, k:k + 4].rearrange("p (h a) -> p h a", a=2), sink, v, ALU.subtract)
                    dve.tensor_scalar(neg_top[:, k:k + 4], top[:, k:k + 4], -1.0, None, ALU.mult).then_inc(top_ready, 1)

                def weights(G):
                    j, b, t, g = GROUPS[G]
                    w, k = P * keys(t), 4 * (G % 2)
                    dve.wait_ge(exp_ready, NG * l + G + 1)
                    if b == "A":
                        dve.tensor_tensor(esum[:, k:k + 4], esum[:, k:k + 4], esink[:, k:k + 4], ALU.add)
                        dve.drain()
                    dve.reciprocal(rsum[:, k:k + 4], esum[:, k:k + 4])
                    dve.drain()
                    e = e_buf[:, G % 2, 0:4 * w].rearrange("p (r n) -> p r n", n=w)
                    if b == "B":
                        odd = rsum[:, k + 1:k + 4:2]
                        dve.tensor_scalar(odd, odd, lam, None, ALU.mult)
                        dve.drain()
                        for h in range(2):
                            dve.tensor_scalar(e[:, 2 * h + 1, :], e[:, 2 * h + 1, :], rsum[:, k + 2 * h + 1:k + 2 * h + 2], None, ALU.mult)
                        dve.drain()
                        for h in range(2):
                            done = dve.scalar_tensor_tensor(e[:, 2 * h, :], e[:, 2 * h, :], rsum[:, k + 2 * h:k + 2 * h + 1],
                                                            e[:, 2 * h + 1, :], ALU.mult, ALU.subtract)
                    else:
                        done = dve.tensor_tensor(e, e, rsum[:, k:k + 4].unsqueeze(2).broadcast_to([P, 4, w]), ALU.mult)
                    done.then_inc(weights_ready, 1)

                tops(0)
                for G, (j, b, t, g) in enumerate(GROUPS):
                    weights(G)
                    if G + 1 < NG:
                        tops(G + 1)
                    mod_step(UPC)
                    if b != "B":
                        first, step = (g, 2) if b == "A" else (8 + 2 * g, 1)
                        out_rest(first, step, t, banks[4][:, 0:2 * P].rearrange("p (k n) -> p k n", n=P))
                    elif g == 1:
                        n = at.next("sub")
                        dve.wait_ge(sub_squares, n + 1)
                        dve.tensor_scalar(sub_sq, sub_sq, 1.0 / P, EPS, ALU.mult, ALU.add)
                        dve.drain()
                        dve.reciprocal(sub_rstd, sub_sq).then_inc(sub_mean, 1)
                        dve.wait_ge(sub_root, n + 1)
                        dve.tensor_tensor(e_buf[:, G % 2, 0:512].rearrange("p (h n) -> p h n", n=P),
                                          banks[4][:, :].rearrange("p (h n) -> p h n", n=P),
                                          sub_rstd.unsqueeze(2).broadcast_to([P, B_H, P]), ALU.mult).then_inc(sub_ready, 1)
                        out_rest(4, 1, t, banks[4][:, :].rearrange("p (k n) -> p k n", n=P), scale=sub_g[:, l:l + 1])
                    mod_step(0)

                def merge(pair, b, n, after):
                    m = at.next(f"merge{l}")
                    dve.drain()
                    dve.wait_ge(chunk_read, m * 2 + (LAYER_CHUNKS * l + IN_CHUNKS + 2))
                    dve.wait_ge(unit_used, (at.done("unit") - after) * HALVES)
                    cols = bass.ds(n * COLS, COLS)
                    for t in range(TILES):
                        dst = merged[:, t, cols] if b == 0 else prod[:, t, :]
                        done = dve.tensor_tensor(dst, banks[2 * pair + t][:, :], sig[:, t, :], ALU.mult)
                    if b:
                        dve.drain()
                        done = dve.tensor_tensor(merged[:, :, cols], merged[:, :, cols], prod[:, :, :], ALU.add)
                    done.then_inc(chunk_read, 1)

                def proj_pair(b):
                    return (l * LAYER_CHUNKS + IN_CHUNKS + 2 + 2 * b) % 2

                dve.memset(bg_raw[:, :], 0.0).then_inc(bg_clear, 1)

                def gates(n):
                    r = at.next("bg")
                    for b in range(4):
                        later = b or not at.first
                        split_low()
                        split_low()
                        if b == 0:
                            dve.wait_ge(bg_high, r + 1)
                            dve.tensor_tensor(bg_split[32:36, :], bg_raw[32:36, :], bg_split[32:36, :].bitcast(F32), ALU.subtract).then_inc(bg_ready, 1)
                        if later:
                            merge(proj_pair((b + 3) % 4), (b + 3) % 4, n if b else n - 1, 2)
                        else:
                            at.next(f"merge{l}")
                        split_low()
                        split_low()
                        split_low()
                at.at[f"merge{l}"] = -1
                at.rounds(dve, NCH, gates)
                merge(proj_pair(3), 3, NCH - 1, 0)

                for i in range(2 * KB):
                    t, g = i // KB, i % KB
                    dve.wait_ge(merged_high, at.next("merged") + 1)
                    s = slice(g * KB, (g + 1) * KB)
                    dve.tensor_tensor(in_low[:, s, t, :], turn_banks[i % 2][:, :].rearrange("p (k n) -> p k n", n=P),
                                      in_high[:, s, t, :].bitcast(F32), ALU.subtract).then_inc(merged_low, 1)
                    mod_step(len(mod_stage(l, "merge")) * UPC // (2 * KB))

                def gate_rows(first, mod_units):
                    dve.memset(ones[:, :], 1.0)
                    dve.drain()
                    for i in range(2 * KB):
                        t, g = i // KB, i % KB
                        n = at.next("row")
                        need(dve, row_summed, n - 1)
                        for k in range(KB):
                            done = dve.tensor_scalar(full[:, i % 2, k * P:(k + 1) * P], ident,
                                                     mod[:, l, first + g * KB + k, t:t + 1], None, ALU.mult)
                        done.then_inc(diag_ready, 1)
                        mod_step(mod_units)
                    mod_step(0)
                gate_rows(32, len(mod_stage(l, "mixer rows")) * UPC // (2 * KB))

                def add_to_x(pair, n, after):
                    dve.drain()
                    dve.wait_ge(unit_used, (at.done("unit") - after) * HALVES)
                    cols = bass.ds(n * COLS, COLS)
                    for t in range(TILES):
                        dve.tensor_tensor(prod[:, t, :], banks[2 * pair + t][:, :], gate_row[:, t, cols], ALU.mult)
                    dve.drain()
                    dve.tensor_tensor(x[:, :, cols], x[:, :, cols], prod[:, :, :], ALU.add).then_inc(chunk_read, 1)

                def w_out_pair(i):
                    for h in range(2):
                        split_low()
                        split_low()
                        if h or not at.first:
                            add_to_x((l * LAYER_CHUNKS + LAYER_CHUNKS - NE - 2 * NCH + h + 1) % 2, i * 2 + (h - 1), 2)
                        split_low()
                        split_low()
                dve.wait_ge(row_ready, at.done("row"))
                at.rounds(dve, NCH // 2, w_out_pair)
                add_to_x((l * LAYER_CHUNKS + LAYER_CHUNKS - NE - 2 * NCH + 1) % 2, NCH - 1, 0)

                dve.wait_ge(router_high_s, l + 1)
                dve.tensor_tensor(router_low[:, :, :], router_raw[:, :, :], router_high[:, :, :].bitcast(F32), ALU.subtract).then_inc(router_ready, 1)
                norm(l, 1, len(mod_stage(l, "norm")) * UPC // (2 * KB))
                gate_rows(80, len(mod_stage(l, "expert rows")) * UPC // (2 * KB))

                dve.memset(route[:, :, 0:8], -3e38)
                dve.drain()
                dve.wait_ge(routed, l + 1)
                logits = banks[4][:, 0:64].rearrange("p (t n) -> p t n", t=2)
                for a, n, c in ((0, 4, 0), (8, 16, 4)):
                    dve.tensor_tensor(route[:, :, a:a + n], logits[:, :, c:c + n],
                                      router_b[:, l, c:c + n].unsqueeze(1).broadcast_to([P, 2, n]), ALU.add)
                dve.drain()

                def best(cols):
                    for t in range(TILES):
                        dve.max(picked[:, t, :], route[:, t, cols])
                    dve.drain()
                    for t in range(TILES):
                        dve.max_index(picked_at[:, t, :], picked[:, t, :], route[:, t, cols])
                    dve.drain()
                best(slice(0, 8))
                dve.tensor_copy(route[:, :, 40:41], picked_at[:, :, 0:1])
                dve.tensor_scalar(route[:, :, 41:42], picked[:, :, 0:1], -1.0, None, ALU.mult).then_inc(route_top, 1)
                dve.drain()
                for t in range(TILES):
                    dve.tensor_scalar(route[:, t, 24:40], constant("group"), route[:, t, 40:41], None, ALU.is_equal)
                dve.drain()
                dve.tensor_scalar(route[:, :, 48:64], route[:, :, 24:40], 1e30, -1e30, ALU.mult, ALU.add)
                dve.tensor_tensor(route[:, :, 24:40], route[:, :, 24:40], route[:, :, 8:24], ALU.mult)
                dve.drain()
                dve.tensor_tensor(route[:, :, 24:40], route[:, :, 24:40], route[:, :, 48:64], ALU.add)
                dve.drain()
                best(slice(24, 40))
                dve.tensor_tensor(route[:, :, 43:44], picked[:, :, 1:2], picked[:, :, 0:1], ALU.subtract).then_inc(route_top, 1)
                dve.tensor_copy(route[:, :, 44:46], picked_at[:, :, 0:2])
                dve.wait_ge(route_exp, 2 * l + 2)
                dve.tensor_scalar(route[:, :, 46:47], route[:, :, 43:44], 1.0, None, ALU.add)
                dve.tensor_copy(route[:, :, 47:48], route[:, :, 42:43])
                dve.drain()
                dve.reciprocal(route[:, :, 46:48], route[:, :, 46:48])
                dve.drain()
                dve.tensor_tensor(route[:, :, 46:47], route[:, :, 46:47], route[:, :, 47:48], ALU.mult)
                dve.drain()
                dve.tensor_tensor(route[:, :, 47:48], route[:, :, 46:47], route[:, :, 43:44], ALU.mult)
                dve.drain()
                for t in range(TILES):
                    dve.tensor_scalar(comb[:, t, :], constant("which"), route[:, t, 44:45], route[:, t, 46:47], ALU.is_equal, ALU.mult)
                    dve.tensor_scalar(route[:, t, 48:64], constant("which"), route[:, t, 45:46], route[:, t, 47:48], ALU.is_equal, ALU.mult)
                dve.drain()
                dve.tensor_tensor(comb[:, :, :], comb[:, :, :], route[:, :, 48:64], ALU.add).then_inc(comb_ready, 1)
                dve.drain()

                key, rank, ends = ranks[:, 0:2], ranks[:, 2:4], ranks[:, 4:9]
                dve.scalar_tensor_tensor(key, route[:, :, 40], float(2 * P), constant("order"), ALU.mult, ALU.add)
                dve.memset(ends[:, 0:1], 0.0)
                dve.memset(ends[:, 4:5], float(2 * P))
                dve.drain()
                dve.wait_ge(row_summed, at.done("row"))
                for t in range(TILES):
                    done = dve.tensor_scalar(full[:, 0, t * P:(t + 1) * P], ident, key[:, t:t + 1], None, ALU.mult)
                done.then_inc(keys_ready, 1)
                dve.wait_ge(keys_spread, l + 1)
                all_keys = banks[4][:, 0:2 * P]
                for t in range(TILES):
                    dve.tensor_scalar(less[:, :], all_keys, key[:, t:t + 1], None, ALU.is_lt)
                    dve.drain()
                    dve.tensor_reduce(rank[:, t:t + 1], less[:, :], AX.X, ALU.add)
                    dve.drain()
                dve.wait_ge(numbers_in, 16 * (l + 1))
                for t in range(TILES):
                    dve.tensor_scalar(sort[:, t, :], numbers[:, :], rank[:, t:t + 1], None, ALU.is_equal)
                dve.drain()
                for g in range(1, 4):
                    dve.tensor_scalar(less[:, :], all_keys, float(2 * P * g), None, ALU.is_lt)
                    dve.drain()
                    dve.tensor_reduce(ends[:, g:g + 1], less[:, :], AX.X, ALU.add)
                    dve.drain()
                for i in range(2):
                    done = dve.tensor_copy(spans[:, i, :].rearrange("p (g e) -> p g e", g=4),
                                           ends[:, i:i + 4].unsqueeze(2).broadcast_to([P, 4, NE // 4]))
                done.then_inc(sort_ready, 1)

                def copy_back(q):
                    n = NK // 2 * l + q
                    dve.wait_ge(back_turned[1], n + 1)
                    need(dve, sort_summed[1], n - 1)
                    dve.tensor_copy(turned_low[:, q % 2, :, :, :].rearrange("p t k n -> p (t k n)"), banks[1][:, :]).then_inc(back_copied[1], 1)

                dve.wait_ge(comb_sorted, l + 1)
                dve.tensor_copy(comb[:, :, :].rearrange("p t e -> p (t e)"), banks[4][:, 0:TILES * NE])
                copy_back(0)
                for q in range(NK // 2):
                    if q + 1 < NK // 2:
                        copy_back(q + 1)
                    dve.wait_ge(sort_summed[1], NK // 2 * l + q + 1)
                    dve.tensor_copy(in_low[:, 2 * q:2 * q + 2, :, :].rearrange("p k t n -> p (k t n)"), banks[3][:, :]).then_inc(sort_stored[1], 1)
                    mod_step(len(mod_stage(l, "sort")) * UPC // (NK // 2))
                mod_step(0)
                dve.tensor_scalar(zeros[:, :], ident, 0.0, None, ALU.mult).then_inc(zeros_ready, 1)

                def hidden(pair, e):
                    n = at.next("hidden")
                    dve.drain()
                    dve.wait_ge(gate_ready, n + 1)
                    need(dve, hid_turned, n)
                    for t in range(TILES):
                        dve.scalar_tensor_tensor(prod[:, t, 0:DE], banks[2 * pair + t][:, DE:2 * DE], comb[:, t, bass.ds(e, 1)],
                                                 sig[:, t, 0:DE], ALU.mult, ALU.mult)
                    dve.drain()
                    for t in range(TILES):
                        done = dve.tensor_tensor(prod[:, t, DE:2 * DE], banks[2 * pair + t][:, 0:DE], prod[:, t, 0:DE], ALU.mult)
                    done.then_inc(chunk_read, 1)

                def hid_rest(e, bank):
                    dve.wait_ge(hid_high_ready, at.next("hid") + 1)
                    cols = bass.ds(e * 512, 512)
                    dve.tensor_tensor(hid_low[:, :, :, :].rearrange("p k t n -> p (k t n)")[:, cols], turn_banks[bank][:, :],
                                      hid_high[:, :, :, :].rearrange("p k t n -> p (k t n)")[:, cols].bitcast(F32),
                                      ALU.subtract).then_inc(hid_stored, 1)

                first_pair = (l * LAYER_CHUNKS + LAYER_CHUNKS - NCH) % 2

                def experts(i):
                    for h in range(2):
                        later = h or not at.first
                        split_low()
                        split_low()
                        if later:
                            hidden((first_pair + h + 1) % 2, i * 2 + (h - 1))
                        else:
                            at.next("hidden")
                        split_low()
                        split_low()
                        if later:
                            hid_rest(i * 2 + (h - 1), (h + 1) % 2)
                        else:
                            at.next("hid")
                for name in ("hidden", "hid"):
                    at.at[name] = at.at.get(name, 0) - 1
                at.rounds(dve, NE // 2, experts)
                hidden((first_pair + 1) % 2, NE - 1)
                hid_rest(NE - 1, 1)

                def sorted_rest(pair):
                    n = at.next("sorted_rest")
                    dve.wait_ge(out_sorted_high, n + 1)
                    need(dve, out_back, n)
                    for t in range(TILES):
                        done = dve.tensor_tensor(sorted_low[:, t, :], banks[2 * pair + t][:, :], sorted_high[:, t, :].bitcast(F32), ALU.subtract)
                    done.then_inc(chunk_read, 1)

                def add_back(n):
                    dve.drain()
                    dve.wait_ge(out_back, at.next("add_back") + 1)
                    cols = bass.ds(n * COLS, COLS)
                    for t in range(TILES):
                        dve.tensor_tensor(prod[:, t, :], turn_banks[t][:, :], gate_row[:, t, cols], ALU.mult)
                    dve.drain()
                    dve.tensor_tensor(x[:, :, cols], x[:, :, cols], prod[:, :, :], ALU.add).then_inc(added, 1)

                def down_pair(i):
                    for h in range(2):
                        later = h or not at.first
                        split_low()
                        split_low()
                        if later:
                            sorted_rest((first_pair + h + 1) % 2)
                        else:
                            at.next("sorted_rest")
                            at.next("add_back")
                        for j in range(3):
                            split_low()
                        if later:
                            add_back(i * 2 + (h - 1))
                        for j in range(NE * DE // P // KB - 5):
                            split_low()
                dve.wait_ge(row_ready, at.done("row"))
                for name in ("sorted_rest", "add_back"):
                    at.at[name] = at.at.get(name, 0) - 1
                at.rounds(dve, NCH // 2, down_pair)
                sorted_rest((first_pair + 1) % 2)
                add_back(NCH - 1)

            root_mean_square()
            dve.wait_ge(final_in, 16)
            for t in range(TILES):
                dve.scalar_tensor_tensor(x[:, t, :], x[:, t, :], rstd[:, t:t + 1], merged[:, 0, :], ALU.mult, ALU.mult).then_inc(final_scaled, 1)

        @block.tensor
        def _(pe):
            at = Cursor()

            def chunk(highs, lows, first_block, blocks, width=COLS, bias=None):
                pair = at.parity("chunk", 2)
                need(pe, chunk_read, at.next("chunk") - 1)
                for j in range(blocks // KB):
                    part, u = at.parity("unit", SPLIT_SLOTS), at.next("unit")
                    for k in range(KB):
                        if k % HALF == 0:
                            pe.wait_ge(low_ready, u * HALVES + k // HALF + 1)
                        kk = first_block + j * KB + k
                        for t in range(TILES):
                            out = banks[2 * pair + t][:, 0:width]
                            start = j == 0 and k == 0
                            stop = j == blocks // KB - 1 and k == KB - 1
                            pe.matmul(out, highs[:, kk, t, :], high_w[:, part, k, 0:width], start=start, stop=False)
                            pe.matmul(out, highs[:, kk, t, :], low_w[:, part, k, 0:width], start=False, stop=False)
                            done = pe.matmul(out, lows[:, kk, t, :], high_w[:, part, k, 0:width], start=False, stop=stop)
                        if k % HALF == HALF - 1:
                            done.then_inc(unit_used, 1)
                    if j == 2 and bias is not None:
                        bias(pair)

            def mod_units(units):
                for _ in range(units):
                    slot, j = at.parity("mod_unit", MOD_SLOTS), at.parity("mod_unit", UPC)
                    at.next("mod_unit")
                    if j == 0:
                        need(pe, mod_stored, at.next("mod_chunk"))
                    pe.wait_ge(mod_in[slot], at.next(f"mod_in{slot}") * 16 + 16)
                    for k in range(KB):
                        done = pe.matmul(mod_bank[32 * k:32 * k + 32, :], cond[:, j * KB + k, :], mod_w[:, slot, k, :],
                                         start=j == 0, stop=j == UPC - 1)
                    done.then_inc(mod_used, 1)

            def mod_turn():
                pe.wait_ge(mod_copied, at.next("mod_turn") + 1)
                for k in range(4):
                    done = pe.matmul(mod_bank[:, 2 * k:2 * k + 2], mod_sums[:, k * P:(k + 1) * P], fold, start=True, stop=True)
                done.then_inc(mod_turned, 1)

            def mod_step(units):
                if at.done("mod_unit") // UPC > at.done("mod_turn"):
                    mod_turn()
                mod_units(units)

            def turn(bank, col, src, width=P):
                return pe.transpose(bank[:, col:col + width], src, ident[0:src.shape[0], 0:src.shape[0]])

            def route_logits(i):
                t, g = i // KB, i % KB
                for k in range(g * KB, (g + 1) * KB):
                    out = banks[4][:, t * 32:t * 32 + 20]
                    pe.matmul(out, in_high[:, k, t, :], router_high[:, k, :], start=k == 0, stop=False)
                    pe.matmul(out, in_high[:, k, t, :], router_low[:, k, :], start=False, stop=False)
                    done = pe.matmul(out, in_low[:, k, t, :], router_high[:, k, :], start=False, stop=k == NK - 1)
                return done

            def norm(mods=0, routes=False):
                for i in range(2 * KB):
                    t, g = i // KB, i % KB
                    n = at.next("norm_group")
                    if g == 0:
                        pe.wait_ge(normed_ready, at.next("norm") + 1)
                    need(pe, norm_full, n - 1)
                    for k in range(KB):
                        done = turn(turn_banks[i % 2], k * P, normed[:, (g * KB + k) * P:(g * KB + k + 1) * P])
                    done.then_inc(norm_turned, 1)
                    mod_step(mods)
                    if routes and i >= 2:
                        pe.wait_ge(norm_low, n - 1)
                        route_logits(i - 2)
                if routes:
                    pe.wait_ge(norm_low, at.done("norm_group") - 1)
                    route_logits(2 * KB - 2)
                pe.wait_ge(norm_low, at.done("norm_group"))
                if routes:
                    route_logits(2 * KB - 1).then_inc(routed, 1)

            def gate_rows(mods):
                for i in range(2 * KB):
                    n = at.next("row")
                    pe.wait_ge(diag_ready, n + 1)
                    need(pe, row_ready, n - 1)
                    pe.matmul(turn_banks[i % 2][:, :], ones[:, :], full[:, i % 2, :], start=True, stop=True).then_inc(row_summed, 1)
                    mod_step(mods)
                mod_step(0)

            pe.wait_ge(start_in, 16 * (3 + DEPTH + 2 * DEPTH))
            turn(mod_bank, 0, normed[0:2 * NK, 0:P], 2 * NK)
            for l in range(DEPTH):
                turn(mod_bank, 32 + l * MODS * 4, normed[0:MODS * 4, (1 + l) * P:(2 + l) * P], MODS * 4)
            turn(mod_bank, 224, normed[0:4 * NK, 3 * P:4 * P], 4 * NK).then_inc(start_turned, 1)
            pe.wait_ge(cond_ready, 1)

            def mod_start(c):
                mod_units(UPC)
                mod_turn()
            at.rounds(pe, FIRST, mod_start)
            pe.wait_ge(pick_ready, 1)

            for l in range(DEPTH):
                norm()

                def w_in_pair(i):
                    for h in range(2):
                        chunk(in_high, in_low, 0, NK)
                at.rounds(pe, IN_CHUNKS // 2, w_in_pair)
                chunk(in_high, in_low, 0, NK, IN_REST)
                pe.wait_ge(chunk_read, LAYER_CHUNKS * l + IN_CHUNKS + 1)

                for t in (SAMPLE, PROMPT):
                    n = at.next("fourier")
                    need(pe, f_copied, n)
                    for g in range(4):
                        done = pe.matmul(banks[g // 2][:, g % 2 * 256:g % 2 * 256 + 256],
                                         proj[:, t, FF + g * P:FF + (g + 1) * P], fourier, start=True, stop=True)
                    done.then_inc(f_first, 1)
                    mod_step(UPC)
                    pe.wait_ge(f_copied, n + 1)
                    need(pe, out_low, at.next("out"))
                    half = e_buf[:, t, :].rearrange("p (g c n) -> p g c n", g=4, c=2)
                    pe.matmul(banks[4][:, :], fourier[:, 0:P], half[:, :, 0, :], start=True, stop=False)
                    pe.matmul(banks[4][:, :], fourier[:, P:2 * P], half[:, :, 1, :], start=False, stop=True).then_inc(f_second, 1)

                def turn_qk(j):
                    b, t = jobs()[j]
                    row = proj[:, t, :]
                    if b == "A":
                        srcs = [row[:, AQ + i * P:AQ + (i + 1) * P] for i in range(5)]
                        cached = [cache_a[:, 0, :]]
                    else:
                        q, k = (BQ, BK) if b == "B" else (CQ, CK)
                        srcs = [row[:, a + i * P:a + (i + 1) * P] for a in (q, k) for i in range(4)]
                        cached = [cache_bc[:, 0, i * P:(i + 1) * P] for i in range(4)]
                    if t == SAMPLE:
                        srcs += cached
                        if b == "A":
                            pe.wait_ge(roped, 2 * l + 1)
                            pe.wait_ge(cache_a_in, 32 * (l + 1))
                        elif b == "B":
                            pe.wait_ge(roped, 2 * l + 2)
                            pe.wait_ge(cache_bc_in, 64 * l + 32)
                        else:
                            pe.wait_ge(cache_bc_in, 64 * l + 64)
                            pe.wait_ge(hankel_ready, l + 1)
                    for i in range(TURNS[j]):
                        need(pe, qk_ready, at.next("qk") - (i > 0))
                        for k, src in enumerate(srcs[4 * i:4 * i + 4]):
                            done = turn(turn_banks[i % 2], k * P, src)
                        done.then_inc(qk_turned, 1)

                def scores(G):
                    j, b, t, g = GROUPS[G]
                    pe.wait_ge(qk_ready, l * sum(TURNS) + sum(TURNS[:j + 1]))
                    if G >= 2:
                        pe.wait_ge(exp_ready, NG * l + G - 1)
                    for r, (q, k, half, head) in enumerate(heads(b, g)):
                        rows = slice(half * HD, (half + 1) * HD)
                        bank, c = score_row(G, r, t)
                        new, old = 4 + k, 4 + k_blocks(b) + k
                        for i, kb in enumerate((old, new) if t == SAMPLE else (new,)):
                            biased = b == "C" and t == SAMPLE and kb == new
                            out = bank[:, c + i * P:c + (i + 1) * P]
                            done = pe.matmul(out, qk_t[rows, j % 2, q, :], qk_t[rows, j % 2, kb, :], start=True, stop=not biased)
                            if biased:
                                done = pe.matmul(out, mirror, hankel[:, head, :], start=False, stop=True)
                    done.then_inc(scored, 1)

                def turn_weights(G):
                    j, b, t, g = GROUPS[G]
                    w = P * keys(t)
                    pe.wait_ge(weights_ready, NG * l + G + 1)
                    need(pe, p_ready, NG * l + G)
                    pe.wait_ge(qk_ready, at.done("qk"))
                    rows = (0, 2) if b == "B" else range(4)
                    n = 0
                    for r in rows:
                        for i in range(keys(t)):
                            c = r * w + i * P
                            done = turn(turn_banks[n // 4], n % 4 * P, e_buf[:, G % 2, c:c + P])
                            n += 1
                    done.then_inc(p_turned, 1)

                def values(G):
                    j, b, t, g = GROUPS[G]
                    pe.wait_ge(p_ready, NG * l + G + 1)
                    if not (b == "B" and g == 1):
                        need(pe, out_low, at.next("out"))
                    new = proj[:, t, V_AT[b]:V_AT[b] + (128 if b == "A" else 512)]
                    old = cache_a[:, 1, :] if b == "A" else cache_bc[:, 1, :]
                    rows = heads(b, g)
                    n = 0
                    for r in ((0, 2) if b == "B" else range(4)):
                        head = rows[r][3]
                        a, width = value_cols(b, head)
                        vals = [v[:, a:a + width] for v in ((old, new) if t == SAMPLE else (new,))]
                        for i, v in enumerate(vals):
                            ends = dict(start=i == 0, stop=i == len(vals) - 1)
                            if b == "B":
                                done = pe.matmul(banks[4][:, head * P:(head + 1) * P], p_t[:, n, :], v, **ends)
                            else:
                                half, slot = head % 2, (head // 4 if b == "A" else r // 2)
                                done = pe.matmul(banks[4][half * HD:(half + 1) * HD, slot * P:(slot + 1) * P], v, p_t[:, n, :], **ends)
                            n += 1
                    done.then_inc(pv_done, 1)
                    if b == "B" and g == 1:
                        pe.wait_ge(sub_ready, at.next("sub") + 1)
                        for h in range(B_H):
                            done = turn(banks[4], h * P, e_buf[:, G % 2, h * P:(h + 1) * P])
                        done.then_inc(sub_turned, 1)

                mod_step(0)
                turn_qk(0)
                scores(0)
                for G, (j, b, t, g) in enumerate(GROUPS):
                    if G + 1 < NG:
                        scores(G + 1)
                    mod_step(2)
                    turn_weights(G)
                    mod_units(UPC - 2)
                    values(G)
                    mod_step(0)
                    if g == 0 and j + 1 < len(jobs()):
                        turn_qk(j + 1)
                pe.wait_ge(out_low, at.done("out"))

                def gate_bias(pair, b):
                    if b == 0:
                        pe.wait_ge(bg_ready, at.next("bg") + 1)
                    for t in range(TILES):
                        pe.matmul(banks[2 * pair + t][:, :], pick[:, b, :], bg_split[:, :], start=False, stop=False)

                def gates(n):
                    for b in range(4):
                        chunk(in_high, in_low, 0, NK, bias=lambda pair: gate_bias(pair, b))
                        chunk(br_high, br_low, 4 * b, KB)
                at.rounds(pe, NCH, gates)

                pe.wait_ge(chunk_read, at.done("chunk"))
                for i in range(2 * KB):
                    t, g = i // KB, i % KB
                    n = at.next("merged")
                    need(pe, merged_low, n - 1)
                    for k in range(KB):
                        done = turn(turn_banks[i % 2], k * P, merged[:, t, (g * KB + k) * P:(g * KB + k + 1) * P])
                    done.then_inc(merged_turned, 1)
                    mod_step(len(mod_stage(l, "merge")) * UPC // (2 * KB))
                pe.wait_ge(merged_low, at.done("merged"))
                gate_rows(len(mod_stage(l, "mixer rows")) * UPC // (2 * KB))

                def w_out_pair(i):
                    for h in range(2):
                        chunk(in_high, in_low, 0, NK)
                at.rounds(pe, NCH // 2, w_out_pair)

                pe.wait_ge(router_ready, l + 1)
                norm(len(mod_stage(l, "norm")) * UPC // (2 * KB), routes=True)
                gate_rows(len(mod_stage(l, "expert rows")) * UPC // (2 * KB))

                pe.wait_ge(keys_ready, l + 1)
                pe.matmul(banks[4][:, 0:2 * P], ones[:, :], full[:, 0, 0:2 * P], start=True, stop=True).then_inc(keys_spread, 1)
                pe.wait_ge(sort_ready, l + 1)
                pe.wait_ge(row_ready, at.done("row"))
                for z in range(TILES):
                    for t in range(TILES):
                        done = turn(turn_banks[0], (z * 2 + t) * P, sort[:, t, z * P:(z + 1) * P].bitcast(F32))
                done.then_inc(unsort_turned, 1)
                pe.wait_ge(comb_ready, l + 1)
                for z in range(TILES):
                    for t in range(TILES):
                        done = pe.matmul(banks[4][:, z * NE:(z + 1) * NE], sort[:, t, z * P:(z + 1) * P].bitcast(F32), comb[:, t, :],
                                         start=t == 0, stop=t == 1)
                done.then_inc(comb_sorted, 1)

                def turn_back(q):
                    n = NK // 2 * l + q
                    for part, src in enumerate((in_high, in_low)):
                        need(pe, back_copied[part], n)
                        for t in range(TILES):
                            for k in range(2):
                                done = turn(banks[part], (t * 2 + k) * P, src[:, 2 * q + k, t, :].bitcast(F32))
                        done.then_inc(back_turned[part], 1)

                turn_back(0)
                for q in range(NK // 2):
                    n = NK // 2 * l + q
                    if q + 1 < NK // 2:
                        turn_back(q + 1)
                    for part, turned in enumerate((turned_high, turned_low)):
                        pe.wait_ge(back_copied[part], n + 1)
                        need(pe, sort_stored[part], n)
                        for k in range(2):
                            for t in range(TILES):
                                done = pe.matmul(banks[2 + part][:, k * 2 * P:(k + 1) * 2 * P], turned[:, q % 2, t, k, :], sort[:, t, :],
                                                 start=t == 0, stop=t == 1)
                        done.then_inc(sort_summed[part], 1)
                    mod_step(len(mod_stage(l, "sort")) * UPC // (NK // 2))
                mod_step(0)
                for part in range(2):
                    pe.wait_ge(sort_stored[part], NK // 2 * (l + 1))

                def of_tiles(first, last, body):
                    start = dict(at.at)

                    def own(*tiles):
                        at.at = dict(start)
                        body(tiles)

                    def not_second():
                        if isinstance(last, int):
                            return own(0, 1)
                        with pe.If(last <= P):
                            own(0)
                        with pe.Else():
                            own(0, 1)
                    if isinstance(first, int):
                        return not_second()
                    with pe.If(first >= P):
                        own(1)
                    with pe.Else():
                        not_second()
                def hid_turn(bank, half):
                    n = at.next("hid")
                    pe.wait_ge(chunk_read, at.done("chunk") - half)
                    need(pe, hid_stored, n - 1)
                    for k in range(2):
                        for t in range(TILES):
                            done = turn(turn_banks[bank], (k * 2 + t) * P, prod[:, t, DE + k * P:DE + (k + 1) * P])
                    done.then_inc(hid_turned, 1)

                def expert_chunk(turned_bank, tiles):
                    pair = at.parity("chunk", 2)
                    need(pe, chunk_read, at.next("chunk") - 1)
                    for j in range(UPC):
                        if j == 3 and turned_bank is not None:
                            hid_turn(turned_bank, 1)
                        part, u = at.parity("unit", SPLIT_SLOTS), at.next("unit")
                        for k in range(KB):
                            if k % HALF == 0:
                                pe.wait_ge(low_ready, u * HALVES + k // HALF + 1)
                            kk = j * KB + k
                            for t in tiles:
                                out = banks[2 * pair + t][:, :]
                                pe.matmul(out, in_high[:, kk, t, :], high_w[:, part, k, :], start=kk == 0, stop=False)
                                pe.matmul(out, in_high[:, kk, t, :], low_w[:, part, k, :], start=False, stop=False)
                                done = pe.matmul(out, in_low[:, kk, t, :], high_w[:, part, k, :], start=False, stop=kk == NK - 1)
                            if k % HALF == HALF - 1:
                                done.then_inc(unit_used, 1)

                def experts(i):
                    for h in range(2):
                        first, last = (pe.value_load(spans[0:1, z, bass.ds(i * 2 + h, 1)], min_val=0, max_val=2 * P) for z in range(2))
                        turned = (h + 1) % 2 if h or not at.first else None
                        if turned is None:
                            at.next("hid")
                        of_tiles(first, last, lambda tiles: expert_chunk(turned, tiles))
                at.at["hid"] = at.at.get("hid", 0) - 1
                at.rounds(pe, NE // 2, experts)
                hid_turn(1, 0)
                pe.wait_ge(hid_stored, at.done("hid"))

                ends = [pe.value_load(spans[0:1, 0, g * NE // 4:g * NE // 4 + 1], min_val=0, max_val=2 * P) for g in range(1, 4)]
                ends = [0] + ends + [2 * P]

                def back(after_low):
                    n = at.next("back")
                    pe.wait_ge(chunk_read, after_low)
                    need(pe, added, n)
                    for t in range(TILES):
                        for z in range(TILES):
                            pe.matmul(turn_banks[t][:, :], unsort[:, z, t, :], sorted_high[:, z, :], start=z == 0, stop=False)
                            done = pe.matmul(turn_banks[t][:, :], unsort[:, z, t, :], sorted_low[:, z, :], start=False, stop=z == 1)
                    done.then_inc(out_back, 1)

                def down_units(pair, j, tiles, last):
                    for unit in (j, j + 1):
                        part, u = at.parity("unit", SPLIT_SLOTS), at.next("unit")
                        for k in range(KB):
                            if k % HALF == 0:
                                pe.wait_ge(low_ready, u * HALVES + k // HALF + 1)
                            kk = unit * KB + k
                            for t in tiles:
                                out = banks[2 * pair + t][:, :]
                                pe.matmul(out, hid_high[:, kk, t, :], high_w[:, part, k, :], start=False, stop=False)
                                pe.matmul(out, hid_high[:, kk, t, :], low_w[:, part, k, :], start=False, stop=False)
                                done = pe.matmul(out, hid_low[:, kk, t, :], high_w[:, part, k, :], start=False, stop=False)
                            if k % HALF == HALF - 1 and not (last and kk == NE * DE // P - 1):
                                done.then_inc(unit_used, 1)

                pe.wait_ge(zeros_ready, l + 1)

                def zero_product(pair, **ends):
                    for t in range(TILES):
                        done = pe.matmul(banks[2 * pair + t][:, :], zeros[:, :], hid_high[:, 0:2, :, :].rearrange("p k t n -> p (k t n)"), **ends)
                    return done

                def down_pair(i):
                    for h in range(2):
                        pair = at.parity("chunk", 2)
                        need(pe, chunk_read, at.next("chunk") - 1)
                        zero_product(pair, start=True, stop=False)
                        for g in range(4):
                            if g == 2 and (h or not at.first):
                                back(at.done("chunk") - 1)
                            elif g == 2:
                                at.next("back")
                            of_tiles(ends[g], ends[g + 1], lambda tiles: down_units(pair, 2 * g, tiles, g == 3))
                        zero_product(pair, start=False, stop=True).then_inc(unit_used, 1)
                at.at["back"] = at.at.get("back", 0) - 1
                at.rounds(pe, NCH // 2, down_pair)
                pe.wait_ge(chunk_read, at.done("chunk"))
                back(at.done("chunk"))


def kernel(**inputs):
    import concourse.bacc as bacc
    from concourse.bass_utils import run_bass_kernel_spmd

    const, places, pick, numbers = shape_constants()
    nc = bacc.Bacc("TRN2", target_bir_lowering=False, num_devices=1, dynamic_dma_scratch_size=64)
    arrays = {n: np.ascontiguousarray(a) for n, a in inputs.items()}
    rpb = arrays["na_rpb"]
    arrays["na_rpb"] = np.pad(rpb, [(0, 0)] * 3 + [(GRID_W - NA_COLS, PAD_W - (GRID_W - NA_COLS) - rpb.shape[-1])])
    arrays["const"], arrays["pick"], arrays["numbers"] = const, pick, numbers
    depth, d = inputs["w_in"].shape[:2]
    outs = {
        "y_prompt": inputs["x_prompt"].shape, "y_sample": inputs["x_sample"].shape,
        "new_attn_k": (1, depth, P) + inputs["cache_attn_k"].shape[3:],
        "new_attn_v": (1, depth, P) + inputs["cache_attn_v"].shape[3:],
        "new_diff_k": (1, depth, P) + inputs["cache_diff_k"].shape[3:],
        "new_diff_v": (1, depth, P) + inputs["cache_diff_v"].shape[3:],
        "new_na_k": (1, depth, P) + inputs["cache_na_k"].shape[3:],
        "new_na_v": (1, depth, P) + inputs["cache_na_v"].shape[3:],
    }
    io = {n: nc.dram_tensor("in_" + n, a.shape, F32, kind="ExternalInput").ap() for n, a in arrays.items()}
    io |= {n: nc.dram_tensor("out_" + n, s, F32, kind="ExternalOutput").ap() for n, s in outs.items()}
    trunk(nc, io, places)
    r = run_bass_kernel_spmd(nc, [{"in_" + n: a for n, a in arrays.items()}], core_ids=[0])
    return tuple(r.results[0]["out_" + n] for n in outs)
```
